# Optimizing a Trainium2 kernel written in Bass

```python
import jax, jax.numpy as jnp
from jax import lax
import numpy as np

D_MODEL = 1024
BATCH = 1
SEQ = 2048
DEPTH = 1
DEC_BATCH = 1
DEC_SEQ = 64
PAST_LEN = 128

CHUNK = 64
HEAD_DIM = 64
MIX_WIDTH = D_MODEL
EPS = 1e-6
SCALE = HEAD_DIM ** -0.5
NEG = -1e30
A_HEADS = 8
A_LEFT_CHUNKS = 8
A_BAND = A_LEFT_CHUNKS + 1
A_CTX = A_LEFT_CHUNKS * CHUNK
MAX_REL = 128
A_WIDTH = A_HEADS * HEAD_DIM
B_HEADS = 8
B_KV_HEADS = 2
B_GROUP = B_HEADS // B_KV_HEADS
WINDOW = 128
B_LEFT_CHUNKS = WINDOW // CHUNK
B_BAND = B_LEFT_CHUNKS + 1
B_CTX = WINDOW
B_WIDTH = B_HEADS * HEAD_DIM
B_KV_WIDTH = B_KV_HEADS * HEAD_DIM
ROPE_THETA = 10000.0
IN_COLS = 3 * A_WIDTH + B_WIDTH + 2 * B_KV_WIDTH
IN_SPLITS = [A_WIDTH, 2 * A_WIDTH, 3 * A_WIDTH, 3 * A_WIDTH + B_WIDTH, 3 * A_WIDTH + B_WIDTH + B_KV_WIDTH]
D_FF = 2816
CONV_W = 3

kernel_name = "hybrid_chunkband_swa_sink_convffn_step"

def rms_norm(x, g):
    xf = x.astype(jnp.float32)
    y = xf * lax.rsqrt(jnp.mean(xf * xf, axis=-1, keepdims=True) + EPS)
    return (y * g.astype(jnp.float32)).astype(x.dtype)

def rope(x, pos):
    half = HEAD_DIM // 2
    inv = jnp.power(ROPE_THETA, -jnp.arange(half, dtype=jnp.float32) / half)
    ang = pos.astype(jnp.float32)[:, None] * inv[None, :]
    cos = jnp.cos(ang)[:, None, :]
    sin = jnp.sin(ang)[:, None, :]
    x1 = x[..., :half].astype(jnp.float32)
    x2 = x[..., half:].astype(jnp.float32)
    return jnp.concatenate([x1 * cos - x2 * sin, x2 * cos + x1 * sin], axis=-1).astype(x.dtype)

def project_heads(h, pos, w_in, q_norm_a, k_norm_a, q_norm_b, k_norm_b):
    bsz, s, _ = h.shape
    p = jnp.einsum("bsd,dc->bsc", h, w_in)
    qa, ka, va, qb, kb, vb = jnp.split(p, IN_SPLITS, axis=-1)
    qa = rms_norm(qa.reshape(bsz, s, A_HEADS, HEAD_DIM), q_norm_a)
    ka = rms_norm(ka.reshape(bsz, s, A_HEADS, HEAD_DIM), k_norm_a)
    va = va.reshape(bsz, s, A_HEADS, HEAD_DIM)
    qb = rope(rms_norm(qb.reshape(bsz, s, B_HEADS, HEAD_DIM), q_norm_b), pos)
    kb = rope(rms_norm(kb.reshape(bsz, s, B_KV_HEADS, HEAD_DIM), k_norm_b), pos)
    vb = vb.reshape(bsz, s, B_KV_HEADS, HEAD_DIM)
    return qa, ka, va, qb, kb, vb

def rel_bias(table, qpos, kpos):
    d = jnp.clip(qpos[:, None] - kpos[None, :], -MAX_REL, MAX_REL) + MAX_REL
    return table[:, d].astype(jnp.float32)

def band_gather(x, n_left):
    bsz, s, nh, d = x.shape
    nc = s // CHUNK
    xc = x.reshape(bsz, nc, CHUNK, nh, d)
    xp = jnp.pad(xc, ((0, 0), (n_left, 0), (0, 0), (0, 0), (0, 0)))
    idx = jnp.arange(nc)[:, None] + jnp.arange(n_left + 1)[None, :]
    return xp[:, idx].reshape(bsz, nc, (n_left + 1) * CHUNK, nh, d)

def band_valid(nc, n_left):
    kchunk = jnp.arange((n_left + 1) * CHUNK) // CHUNK
    return (jnp.arange(nc)[:, None] - n_left + kchunk[None, :]) >= 0

def sink_softmax(scores, sinks):
    s = sinks.astype(jnp.float32).reshape(B_KV_HEADS, B_GROUP, 1, 1)
    m = jnp.maximum(jnp.max(scores, axis=-1, keepdims=True), s)
    e = jnp.exp(scores - m)
    return e / (jnp.sum(e, axis=-1, keepdims=True) + jnp.exp(s - m))

def band_attn_a_prompt(q, k, v, rel_table):
    bsz, s, nh, d = q.shape
    nc = s // CHUNK
    qc = q.reshape(bsz, nc, CHUNK, nh, d)
    kb = band_gather(k, A_LEFT_CHUNKS)
    vb = band_gather(v, A_LEFT_CHUNKS)
    scores = jnp.einsum("bnqhd,bnkhd->bnhqk", qc, kb, preferred_element_type=jnp.float32) * SCALE
    bias = rel_bias(rel_table, A_LEFT_CHUNKS * CHUNK + jnp.arange(CHUNK), jnp.arange(A_BAND * CHUNK))
    valid = band_valid(nc, A_LEFT_CHUNKS)
    scores = jnp.where(valid[None, :, None, None, :], scores + bias[None, None], NEG)
    p = jax.nn.softmax(scores, axis=-1)
    out = jnp.einsum("bnhqk,bnkhd->bnqhd", p.astype(v.dtype), vb)
    return out.reshape(bsz, s, A_WIDTH)

def band_attn_a_sample(q, k_new, v_new, k_cache, v_cache, rel_table):
    bsz, t = q.shape[:2]
    past = k_cache.shape[1]
    k = jnp.concatenate([k_cache.astype(k_new.dtype), k_new], axis=1)
    v = jnp.concatenate([v_cache.astype(v_new.dtype), v_new], axis=1)
    scores = jnp.einsum("bqhd,bkhd->bhqk", q, k, preferred_element_type=jnp.float32) * SCALE
    scores = scores + rel_bias(rel_table, past + jnp.arange(t), jnp.arange(past + t))[None]
    p = jax.nn.softmax(scores, axis=-1)
    out = jnp.einsum("bhqk,bkhd->bqhd", p.astype(v.dtype), v)
    return out.reshape(bsz, t, A_WIDTH)

def window_attn_b_prompt(q, k, v, sinks):
    bsz, s = q.shape[:2]
    nc = s // CHUNK
    qc = q.reshape(bsz, nc, CHUNK, B_KV_HEADS, B_GROUP, HEAD_DIM)
    kb = band_gather(k, B_LEFT_CHUNKS)
    vb = band_gather(v, B_LEFT_CHUNKS)
    scores = jnp.einsum("bnqgrd,bnkgd->bngrqk", qc, kb, preferred_element_type=jnp.float32) * SCALE
    valid = band_valid(nc, B_LEFT_CHUNKS)
    scores = jnp.where(valid[None, :, None, None, None, :], scores, NEG)
    p = sink_softmax(scores, sinks)
    out = jnp.einsum("bngrqk,bnkgd->bnqgrd", p.astype(v.dtype), vb)
    return out.reshape(bsz, s, B_WIDTH)

def window_attn_b_sample(q, k_new, v_new, k_cache, v_cache, sinks):
    bsz, t = q.shape[:2]
    k = jnp.concatenate([k_cache.astype(k_new.dtype), k_new], axis=1)
    v = jnp.concatenate([v_cache.astype(v_new.dtype), v_new], axis=1)
    qg = q.reshape(bsz, t, B_KV_HEADS, B_GROUP, HEAD_DIM)
    scores = jnp.einsum("bqgrd,bkgd->bgrqk", qg, k, preferred_element_type=jnp.float32) * SCALE
    p = sink_softmax(scores, sinks)
    out = jnp.einsum("bgrqk,bkgd->bqgrd", p.astype(v.dtype), v)
    return out.reshape(bsz, t, B_WIDTH)

def conv_ffn(h, conv_state, w_gate_up, conv_w, conv_b, w_down):
    t = h.shape[1]
    gate, up = jnp.split(jnp.einsum("bsd,df->bsf", h, w_gate_up), 2, axis=-1)
    ext = jnp.concatenate([conv_state.astype(gate.dtype), gate], axis=1)
    conv = conv_b
    for i in range(CONV_W):
        conv = conv + conv_w[i] * ext[:, i:i + t]
    y = jax.nn.silu(conv) * up
    return jnp.einsum("bsf,fd->bsd", y, w_down), ext[:, -(CONV_W - 1):]

def setup_inputs(seed: int = 0) -> dict:
    key = jax.random.key(seed)
    ks = jax.random.split(key, 21)

    def nrm(k, shape, scale=1.0):
        return scale * jax.random.normal(k, shape, jnp.float32)

    a_len = min(A_CTX, PAST_LEN)
    b_len = min(B_CTX, PAST_LEN)
    return {
        "x_prompt": nrm(ks[0], (BATCH, SEQ, D_MODEL)),
        "x_sample": nrm(ks[1], (DEC_BATCH, DEC_SEQ, D_MODEL)),
        "cache_a_k": nrm(ks[2], (DEPTH, DEC_BATCH, a_len, A_HEADS, HEAD_DIM)),
        "cache_a_v": nrm(ks[3], (DEPTH, DEC_BATCH, a_len, A_HEADS, HEAD_DIM)),
        "cache_b_k": nrm(ks[4], (DEPTH, DEC_BATCH, b_len, B_KV_HEADS, HEAD_DIM)),
        "cache_b_v": nrm(ks[5], (DEPTH, DEC_BATCH, b_len, B_KV_HEADS, HEAD_DIM)),
        "state_conv": nrm(ks[6], (DEPTH, DEC_BATCH, CONV_W - 1, D_FF)),
        "norm_attn": 1.0 + nrm(ks[7], (DEPTH, D_MODEL), 0.05),
        "w_in": nrm(ks[8], (DEPTH, D_MODEL, IN_COLS), D_MODEL ** -0.5),
        "q_norm_a": 1.0 + nrm(ks[9], (DEPTH, HEAD_DIM), 0.05),
        "k_norm_a": 1.0 + nrm(ks[10], (DEPTH, HEAD_DIM), 0.05),
        "rel_bias_a": nrm(ks[11], (DEPTH, A_HEADS, 2 * MAX_REL + 1), 0.1),
        "q_norm_b": 1.0 + nrm(ks[12], (DEPTH, HEAD_DIM), 0.05),
        "k_norm_b": 1.0 + nrm(ks[13], (DEPTH, HEAD_DIM), 0.05),
        "sinks_b": nrm(ks[14], (DEPTH, B_HEADS), 0.5),
        "w_out": nrm(ks[15], (DEPTH, MIX_WIDTH, D_MODEL), MIX_WIDTH ** -0.5),
        "norm_ffn": 1.0 + nrm(ks[16], (DEPTH, D_MODEL), 0.05),
        "w_gate_up": nrm(ks[17], (DEPTH, D_MODEL, 2 * D_FF), D_MODEL ** -0.5),
        "conv_w": nrm(ks[18], (DEPTH, CONV_W, D_FF), CONV_W ** -0.5),
        "conv_b": nrm(ks[19], (DEPTH, D_FF), 0.01),
        "w_down": nrm(ks[20], (DEPTH, D_FF, D_MODEL), D_FF ** -0.5),
    }

def reference(x_prompt, x_sample, cache_a_k, cache_a_v, cache_b_k, cache_b_v, state_conv,
              norm_attn, w_in, q_norm_a, k_norm_a, rel_bias_a, q_norm_b, k_norm_b, sinks_b,
              w_out, norm_ffn, w_gate_up, conv_w, conv_b, w_down):
    y_prompt = x_prompt
    y_sample = x_sample
    pos_p = jnp.arange(x_prompt.shape[1])
    pos_s = PAST_LEN + jnp.arange(x_sample.shape[1])
    zero_conv = jnp.zeros((x_prompt.shape[0], CONV_W - 1, D_FF), x_prompt.dtype)
    akp, avp, bkp, bvp, cvp = [], [], [], [], []
    aks, avs, bks, bvs, cvs = [], [], [], [], []
    for l in range(DEPTH):
        h = rms_norm(y_prompt, norm_attn[l])
        qa, ka, va, qb, kb, vb = project_heads(h, pos_p, w_in[l], q_norm_a[l], k_norm_a[l], q_norm_b[l], k_norm_b[l])
        oa = band_attn_a_prompt(qa, ka, va, rel_bias_a[l])
        ob = window_attn_b_prompt(qb, kb, vb, sinks_b[l])
        y_prompt = y_prompt + jnp.einsum("bsc,cd->bsd", jnp.concatenate([oa, ob], axis=-1), w_out[l])
        f, conv_new = conv_ffn(rms_norm(y_prompt, norm_ffn[l]), zero_conv, w_gate_up[l], conv_w[l], conv_b[l], w_down[l])
        y_prompt = y_prompt + f
        akp.append(ka[:, -A_CTX:])
        avp.append(va[:, -A_CTX:])
        bkp.append(kb[:, -B_CTX:])
        bvp.append(vb[:, -B_CTX:])
        cvp.append(conv_new)
        h = rms_norm(y_sample, norm_attn[l])
        qa, ka, va, qb, kb, vb = project_heads(h, pos_s, w_in[l], q_norm_a[l], k_norm_a[l], q_norm_b[l], k_norm_b[l])
        oa = band_attn_a_sample(qa, ka, va, cache_a_k[l], cache_a_v[l], rel_bias_a[l])
        ob = window_attn_b_sample(qb, kb, vb, cache_b_k[l], cache_b_v[l], sinks_b[l])
        y_sample = y_sample + jnp.einsum("bsc,cd->bsd", jnp.concatenate([oa, ob], axis=-1), w_out[l])
        f, conv_new = conv_ffn(rms_norm(y_sample, norm_ffn[l]), state_conv[l], w_gate_up[l], conv_w[l], conv_b[l], w_down[l])
        y_sample = y_sample + f
        aks.append(ka)
        avs.append(va)
        bks.append(kb)
        bvs.append(vb)
        cvs.append(conv_new)
    return (y_prompt, y_sample,
            jnp.stack(akp), jnp.stack(avp), jnp.stack(bkp), jnp.stack(bvp), jnp.stack(cvp),
            jnp.stack(aks), jnp.stack(avs), jnp.stack(bks), jnp.stack(bvs), jnp.stack(cvs))


_drawn_inputs = setup_inputs


def setup_inputs(seed=0):
    import zlib

    import numpy as np

    out = dict(_drawn_inputs(seed))
    spreads = {}
    factors = {'q_norm_a': 8.0, 'rel_bias_a': 6.605, 'q_norm_b': 8.0, 'sinks_b': 64.0, 'conv_b': 8.0}
    for name, (base, spread) in spreads.items():
        noise = np.random.default_rng([zlib.crc32(name.encode()), seed]).standard_normal(out[name].shape)
        drawn = base * np.exp(spread * noise) if base else spread * noise
        out[name] = __import__('jax').numpy.asarray(drawn.astype(out[name].dtype))
    for name, factor in factors.items():
        out[name] = (out[name] * factor).astype(out[name].dtype)
    return out
```

```python
from contextlib import ExitStack

import concourse.bass as bass
from concourse import mybir
from concourse.alu_op_type import AluOpType as ALU

F32 = mybir.dt.float32
F32R = mybir.dt.float32r
BF16 = mybir.dt.bfloat16
ACT = mybir.ActivationFunctionType
AX = mybir.AxisListType

P = 128
D_MODEL = 1024
SEQ = 2048
DEC = 64
PAST = 128
TOKENS = SEQ + DEC
CHUNK = 64
HEAD = 64
HEADS = 8
D_FF = 2816
EPS = 1e-6
NEG = -1e30
SCALE = HEAD ** -0.5
MAX_REL = 128
KD = D_MODEL // P
N_BLOCKS = 3
BLOCK = TOKENS // N_BLOCKS
KF = D_FF // P
SUBS = 2
SUB = BLOCK // SUBS
PASSES = ((0, 0), (0, 1), (1, 0))
ds = bass.ds


class Memory:

    def __init__(self, nc, ctx, stage):
        self.nc, self.ctx, self.stage, self.sems = nc, ctx, stage, []
        ctx.callback(self.clear)

    def clear(self):
        self.nc.clear_and_free_semaphores(self.sems)
        self.nc.all_engine_barrier()

    def sbuf(self, name, shape, dtype=F32):
        return self.ctx.enter_context(self.nc.sbuf_tensor(f"{self.stage}_{name}", shape, dtype))

    def psum(self, name, shape, dtype=F32):
        return self.ctx.enter_context(self.nc.psum_tensor(f"{self.stage}_{name}", shape, dtype))

    def sem(self, name):
        self.sems.append(self.nc.alloc_semaphore(f"{self.stage}_{name}"))
        return self.sems[-1]


def dense(nc, out, w_parts, act_parts, n_k, last_wait=None):
    for k in range(n_k):
        if k == n_k - 1 and last_wait:
            last_wait()
        for w, a in PASSES:
            last = nc.tensor.matmul(out, w_parts[w](k), act_parts[a](k),
                                    start=(k == 0 and (w, a) == PASSES[0]),
                                    stop=(k == n_k - 1 and (w, a) == PASSES[-1]))
    return last


def project(nc, xT, w_qk, w_rv, gains, rope_cos, rope_sin, swap, head_ones, all_ones, ident,
            rel, q_a, k_a, qk_b, v_all, rel_rows):
    QK_PAIRS, RV_PAIRS = 4, 5
    PAIRS = QK_PAIRS + RV_PAIRS
    VT = 88
    NV = SUB // VT
    with ExitStack() as ctx:
        m = Memory(nc, ctx, "project")
        x_raw = m.sbuf("x_raw", [P, KD, BLOCK])
        x_sq = m.sbuf("x_sq", [P, KD, SUB])
        x_ssq = m.sbuf("x_ssq", [P, BLOCK])
        h = m.sbuf("h", [P, 2, BLOCK])
        h_hi = [m.sbuf(f"h_hi{i}", [P, KD, BLOCK], F32R) for i in range(2)]
        h_lo = [m.sbuf(f"h_lo{i}", [P, KD, BLOCK], F32R) for i in range(2)]
        n_r = m.sbuf("n_r", [P, SUBS, SUB])
        n_r2 = m.sbuf("n_r2", [P, SUBS, SUB])
        n_t = m.sbuf("n_t", [P, SUBS, SUB])
        n_c = m.sbuf("n_c", [P, SUBS, SUB])
        w_raw = [m.sbuf(f"w_raw{s}", [P, KD, P]) for s in range(2)]
        w_hi = [m.sbuf(f"w_hi{s}", [P, KD, P], F32R) for s in range(2)]
        w_lo = [m.sbuf(f"w_lo{s}", [P, KD, P], F32R) for s in range(2)]
        g_x = m.sbuf("g_x", [P, KD])
        g_q = m.sbuf("g_q", [P, 2])
        g_r = m.sbuf("g_r", [P, 2])
        g_in = m.sbuf("g_in", [P, KD + 4])
        eps = m.sbuf("eps", [P, 1])
        cos_sb = m.sbuf("cos", [P, BLOCK])
        sin_sb = m.sbuf("sin", [P, BLOCK])
        swap_sb = m.sbuf("swap", [P, P])
        head_ones_sb = m.sbuf("head_ones", [P, P])
        all_ones_sb = m.sbuf("all_ones", [P, P])
        ident_sb = m.sbuf("ident", [P, P])
        sq = [m.sbuf(f"sq{i}", [P, SUB]) for i in range(2)]
        ln = [m.sbuf(f"ln{i}", [P, SUB]) for i in range(2)]
        r0 = [m.sbuf(f"r0{i}", [P, SUB]) for i in range(2)]
        r2 = [m.sbuf(f"r2{i}", [P, SUB]) for i in range(2)]
        tmp = [m.sbuf(f"tmp{i}", [P, SUB]) for i in range(2)]
        corr = [m.sbuf(f"corr{i}", [P, SUB]) for i in range(2)]
        zg = [m.sbuf(f"zg{i}", [P, SUB]) for i in range(2)]
        zc = m.sbuf("zc", [P, SUB])
        zs = m.sbuf("zs", [P, SUB])
        zr = m.sbuf("zr", [P, SUB])
        out_t = [[m.sbuf(f"out{s}{i}", [P, SUB]) for i in range(2)] for s in range(2)]
        v_f = [m.sbuf(f"v_f{i}", [P, SUB]) for i in range(2)]
        v_t = [m.sbuf(f"v_t{i}", [VT, NV, P]) for i in range(2)]

        z = [[m.psum(f"z{s}{i}", [P, 512]) for i in range(2)] for s in range(2)]
        st = m.psum("stat", [P, SUBS, 512])
        rv_banks = m.psum("rv_banks", [P, 2, 512])
        rot = rv_banks[:, 0, 0:SUB]
        vtr = rv_banks[0:VT, 1, :].rearrange("p (c f) -> p c f", c=NV)

        const_ld, x_ld, cs_ld, rel_st = (m.sem(n) for n in ("const_ld", "x_ld", "cs_ld", "rel_st"))
        w_ld = [m.sem(f"w_ld{s}") for s in range(2)]
        w_hi_ok = [m.sem(f"w_hi_ok{s}") for s in range(2)]
        w_lo_ok = [m.sem(f"w_lo_ok{s}") for s in range(2)]
        z_ok = [[m.sem(f"z_ok{s}{i}") for i in range(2)] for s in range(2)]
        out_ok = [[m.sem(f"out_ok{s}{i}") for i in range(2)] for s in range(2)]
        stored = [[m.sem(f"stored{s}{i}") for i in range(2)] for s in range(2)]
        gains_ok, eps_ok = m.sem("gains_ok"), m.sem("eps_ok")
        x_sq_ok, x_ssq_ok, x_ms_ok = m.sem("x_sq_ok"), m.sem("x_ssq_ok"), m.sem("x_ms_ok")
        x_ln_ok, x_r_ok, x_r2_ok, x_t_ok, x_c_ok = (m.sem(n) for n in ("x_ln_ok", "x_r_ok", "x_r2_ok", "x_t_ok", "x_c_ok"))
        h_ok, h_hi_ok, h_lo_ok = m.sem("h_ok"), m.sem("h_hi_ok"), m.sem("h_lo_ok")
        sq_ok, st_ok, ln_ok, r0_ok, r2_ok, corr_ok, zg_ok, rot_ok, rotated, vf_ok, vtr_ok = (
            [m.sem(f"{n}{i}") for i in range(2)] for n in
            ("sq_ok", "st_ok", "ln_ok", "r0_ok", "r2_ok", "corr_ok", "zg_ok", "rot_ok", "rotated", "vf_ok", "vtr_ok"))
        tmp_ok, zc_ok, zr_ok = m.sem("tmp_ok"), m.sem("zc_ok"), m.sem("zr_ok")

        NORMS = QK_PAIRS * 2 + RV_PAIRS
        LAST = N_BLOCKS - 1

        def rv_loop(eng, body, last_of_stage):
            with eng.Fori(0, RV_PAIRS - 1) as i:
                body(i, 0, True)
            body(RV_PAIRS - 1, 1, not last_of_stage)

        def at(ap, i):
            return ap[i] if isinstance(i, int) else ap[ds(i, 1)].rearrange("a p n -> p (a n)")

        block = ctx.enter_context(nc.Block())

        @block.sync
        def _(sp):
            def load_x(b):
                t0 = b * BLOCK
                if b:
                    sp.wait_ge(h_ok, KD * b)
                sp.dma_start(x_raw[:], xT[:, :, t0:t0 + BLOCK].rearrange("k p n -> p k n")).then_inc(x_ld, 16)

            def load_pair(g, src):
                for s in range(2):
                    sp.wait_ge(w_lo_ok[s], g)
                    sp.dma_start(w_raw[s][:], src(s)).then_inc(w_ld[s], 16)

            def store(s, j, g, dst, src):
                sp.wait_ge(out_ok[s][j], g + 1)
                sp.dma_start(dst, src).then_inc(stored[s][j], 16)

            load_x(0)
            sp.dma_start(g_in[:], gains).then_inc(const_ld, 16)
            sp.dma_start(all_ones_sb[:], all_ones).then_inc(const_ld, 16)
            sp.dma_start(head_ones_sb[:], head_ones).then_inc(const_ld, 16)
            sp.dma_start(swap_sb[:], swap).then_inc(const_ld, 16)
            sp.dma_start(ident_sb[:], ident).then_inc(const_ld, 16)
            load_pair(0, lambda s: w_qk[0, s])
            load_x(1)
            sp.dma_start(rel_rows, bass.AP(rel.tensor, 0, [[0, P], [rel.shape[1], rel.shape[0]], [1, rel.shape[1]]]))\
                .then_inc(rel_st, 16)
            for b in range(N_BLOCKS):
                t0 = b * BLOCK
                halves = [slice(t0 + j * SUB, t0 + (j + 1) * SUB) for j in range(SUBS)]
                for j in range(SUBS):
                    if b:
                        sp.wait_ge(zr_ok, 2 * b * RV_PAIRS)
                sp.dma_start(cos_sb[:], rope_cos[:, t0:t0 + BLOCK]).then_inc(cs_ld, 16)
                sp.dma_start(sin_sb[:], rope_sin[:, t0:t0 + BLOCK]).then_inc(cs_ld, 16)

                def qk(i, g, nxt):
                    load_pair(g + 1, nxt)
                    for s, dst in ((0, q_a), (1, k_a)):
                        for j in range(SUBS):
                            store(s, j, g, at(dst[:, :, halves[j]], i), out_t[s][j][:])

                with sp.Fori(0, QK_PAIRS - 1) as i:
                    qk(i, b * PAIRS + i, lambda s: w_qk[ds(i + 1, 1), s].rearrange("a p k n -> p (a k) n"))
                qk(QK_PAIRS - 1, b * PAIRS + QK_PAIRS - 1, lambda s: w_rv[0, s])
                if b + 2 < N_BLOCKS:
                    load_x(b + 2)

                def rv(i, g, nxt):
                    if nxt:
                        load_pair(g + 1, nxt)
                    for j in range(SUBS):
                        store(0, j, g, at(qk_b[:, :, halves[j]], i), out_t[0][j][:])
                    for j in range(SUBS):
                        store(1, j, g, v_all[halves[j], ds(i * P, P)].rearrange("(c p) f -> p c f", p=VT), v_t[j][:])

                with sp.Fori(0, RV_PAIRS - 1) as i:
                    rv(i, b * PAIRS + QK_PAIRS + i,
                       lambda s: w_rv[ds(i + 1, 1), s].rearrange("a p k n -> p (a k) n"))
                rv(RV_PAIRS - 1, b * PAIRS + PAIRS - 1, (lambda s: w_qk[0, s]) if b < LAST else None)
            sp.wait_ge(rel_st, 16)
            for s in range(2):
                for j in range(SUBS):
                    sp.wait_ge(stored[s][j], 16 * N_BLOCKS * PAIRS)

        @block.tensor
        def _(pe):
            def tile(s, j, b, g):
                if j == 0:
                    pe.wait_ge(w_lo_ok[s], g + 1)
                pe.wait_ge(out_ok[s][j], g)
                cols = slice(j * SUB, (j + 1) * SUB)
                hh, hl = h_hi[b % 2], h_lo[b % 2]
                dense(nc, z[s][j][:, 0:SUB], (lambda k: w_hi[s][:, k, :], lambda k: w_lo[s][:, k, :]),
                      (lambda k: hh[:, k, cols], lambda k: hl[:, k, cols]), KD).then_inc(z_ok[s][j], 1)

            def stat(j, n):
                pe.wait_ge(sq_ok[j], n + 1)
                pe.wait_ge(corr_ok[j], n)
                nc.tensor.matmul(st[:, j, 0:SUB], head_ones_sb[:], sq[j][:], start=True, stop=True)\
                    .then_inc(st_ok[j], 1)

            def swapped(j, r):
                pe.wait_ge(zg_ok[j], r + 1)
                pe.wait_ge(rotated[1 - j], r + j)
                nc.tensor.matmul(rot, swap_sb[:], zg[j][:], start=True, stop=True).then_inc(rot_ok[j], 1)

            def values(j, r, g):
                pe.wait_ge(vf_ok[j], r + 1)
                pe.wait_ge(out_ok[1][1 - j], g + j)
                for c in range(NV):
                    last = nc.tensor.transpose(vtr[:, c, :], v_f[j][:, c * VT:(c + 1) * VT], ident_sb[:])
                last.then_inc(vtr_ok[j], 1)

            def x_stat(b):
                pe.wait_ge(x_ssq_ok, SUBS * (b + 1))
                for j in range(SUBS):
                    last = nc.tensor.matmul(rv_banks[:, j, 0:SUB], all_ones_sb[:], x_ssq[:, j * SUB:(j + 1) * SUB],
                                            start=True, stop=True)
                last.then_inc(x_ms_ok, 1)

            pe.wait_ge(const_ld, 5 * 16)
            x_stat(0)
            for b in range(N_BLOCKS):
                pe.wait_ge(h_lo_ok, KD * (b + 1))

                with pe.Fori(0, QK_PAIRS) as i:
                    g, n = b * PAIRS + i, b * NORMS + 2 * i
                    tile(0, 0, b, g)
                    tile(0, 1, b, g)
                    stat(0, n)
                    tile(1, 0, b, g)
                    stat(1, n)
                    tile(1, 1, b, g)
                    stat(0, n + 1)
                    stat(1, n + 1)
                if b < LAST:
                    for j in range(SUBS):
                        pe.wait_ge(rotated[j], b * RV_PAIRS)
                        pe.wait_ge(out_ok[1][j], b * PAIRS)
                    x_stat(b + 1)

                with pe.Fori(0, RV_PAIRS) as i:
                    g, n, r = b * PAIRS + QK_PAIRS + i, b * NORMS + 2 * QK_PAIRS + i, b * RV_PAIRS + i
                    tile(0, 0, b, g)
                    tile(0, 1, b, g)
                    stat(0, n)
                    if b < LAST:
                        pe.wait_ge(x_c_ok, b + 2)
                    swapped(0, r)
                    tile(1, 0, b, g)
                    stat(1, n)
                    swapped(1, r)
                    tile(1, 1, b, g)
                    values(0, r, g)
                    values(1, r, g)

        @block.scalar
        def _(act):
            nc.scalar.preload_act_table_set("natural_log_exp_and_others")

            def split_hi(s, g):
                act.wait_ge(w_ld[s], 16 * (g + 1))
                act.wait_ge(z_ok[s][1], g)
                nc.scalar.activation(w_hi[s][:], w_raw[s][:], ACT.Copy).then_inc(w_hi_ok[s], 1)

            def square(s, j, g, n):
                act.wait_ge(z_ok[s][j], g + 1)
                act.wait_ge(st_ok[j], n)
                nc.scalar.activation(sq[j][:], z[s][j][:, 0:SUB], ACT.Square).then_inc(sq_ok[j], 1)

            def root(j, n):
                act.wait_ge(st_ok[j], n + 1)
                act.wait_ge(corr_ok[j], n)
                nc.scalar.activation(ln[j][:], st[:, j, 0:SUB], ACT.Ln, bias=eps[:, 0:1]).then_inc(ln_ok[j], 1)
                act.wait_ge(ln_ok[j], n + 1)
                nc.scalar.activation(r0[j][:], ln[j][:], ACT.Exp, scale=-0.5).then_inc(r0_ok[j], 1)
                act.wait_ge(r0_ok[j], n + 1)
                nc.scalar.activation(r2[j][:], r0[j][:], ACT.Square).then_inc(r2_ok[j], 1)

            def x_square(b):
                act.wait_ge(x_ld, 16 * (b + 1))
                for j in range(SUBS):
                    if b or j:
                        act.wait_ge(x_ssq_ok, SUBS * b + j)
                    nc.scalar.activation(x_sq[:], x_raw[:, :, j * SUB:(j + 1) * SUB], ACT.Square).then_inc(x_sq_ok, 1)

            def x_root(b):
                act.wait_ge(x_ms_ok, b + 1)
                if b:
                    act.wait_ge(x_c_ok, b)
                nc.scalar.activation(n_t[:], rv_banks[:, :, 0:SUB], ACT.Ln, bias=eps[:, 0:1]).then_inc(x_ln_ok, 1)
                act.wait_ge(x_ln_ok, b + 1)
                nc.scalar.activation(n_r[:], n_t[:], ACT.Exp, scale=-0.5).then_inc(x_r_ok, 1)
                act.wait_ge(x_r_ok, b + 1)
                nc.scalar.activation(n_r2[:], n_r[:], ACT.Square).then_inc(x_r2_ok, 1)

            def h_split(b):
                for k in range(KD):
                    act.wait_ge(h_ok, b * KD + k + 1)
                    nc.scalar.activation(h_hi[b % 2][:, k, :], h[:, k % 2, :], ACT.Copy).then_inc(h_hi_ok, 1)

            act.wait_ge(eps_ok, 1)
            x_square(0)
            for s in range(2):
                act.wait_ge(w_ld[s], 16)
                nc.scalar.activation(w_hi[s][:], w_raw[s][:], ACT.Copy).then_inc(w_hi_ok[s], 1)
            x_root(0)
            h_split(0)
            for b in range(N_BLOCKS):
                if b < LAST:
                    x_square(b + 1)

                with nc.scalar.Fori(0, QK_PAIRS) as i:
                    g, n = b * PAIRS + i, b * NORMS + 2 * i
                    square(0, 0, g, n)
                    square(0, 1, g, n)
                    root(0, n)
                    split_hi(0, g + 1)
                    square(1, 0, g, n + 1)
                    root(1, n)
                    square(1, 1, g, n + 1)
                    root(0, n + 1)
                    split_hi(1, g + 1)
                    root(1, n + 1)
                if b < LAST:
                    x_root(b + 1)
                    h_split(b + 1)

                def rv(i, gain, prefetch):
                    g, n, r = b * PAIRS + QK_PAIRS + i, b * NORMS + 2 * QK_PAIRS + i, b * RV_PAIRS + i
                    for j in range(SUBS):
                        square(0, j, g, n)
                        act.wait_ge(rotated[j], r)
                        nc.scalar.activation(zg[j][:], z[0][j][:, 0:SUB], ACT.Copy, scale=g_r[:, gain:gain + 1])\
                            .then_inc(zg_ok[j], 1)
                    root(0, n)
                    if prefetch:
                        split_hi(0, g + 1)
                    for j in range(SUBS):
                        act.wait_ge(z_ok[1][j], g + 1)
                        act.wait_ge(vtr_ok[j], r)
                        nc.scalar.activation(v_f[j][:], z[1][j][:, 0:SUB], ACT.Copy).then_inc(vf_ok[j], 1)
                        if j == 0:
                            root(1, n)
                    if prefetch:
                        split_hi(1, g + 1)

                rv_loop(nc.scalar, rv, b == LAST)

        @block.vector
        def _(dve):
            def split_lo(s, g):
                dve.wait_ge(w_hi_ok[s], g + 1)
                nc.vector.tensor_tensor(w_lo[s][:], w_raw[s][:], w_hi[s][:].bitcast(F32), ALU.subtract)\
                    .then_inc(w_lo_ok[s], 1)

            def correction(j, n, m_, before, count):
                dve.wait_ge(r2_ok[j], n + 1)
                nc.vector.scalar_tensor_tensor(tmp[j][:], st[:, j, 0:SUB], eps[:, 0:1], r2[j][:], ALU.add, ALU.mult)\
                    .then_inc(tmp_ok, 1)
                dve.wait_ge(before[j], count)
                dve.wait_ge(tmp_ok, m_ + 1)
                nc.vector.scalar_tensor_tensor(corr[j][:], tmp[j][:], 3.0, r0[j][:], ALU.subtract, ALU.mult)\
                    .then_inc(corr_ok[j], 1)

            def norm(s, j, g, n, m_):
                correction(j, n, m_, out_ok[1 - s], g + s)
                dve.wait_ge(stored[s][j], 16 * g)
                dve.wait_ge(corr_ok[j], n + 1)
                nc.vector.scalar_tensor_tensor(out_t[s][j][:], z[s][j][:, 0:SUB], g_q[:, s:s + 1], corr[j][:],
                                               ALU.mult, ALU.mult).then_inc(out_ok[s][j], 1)

            def norm_rotary(j, g, n, m_, r):
                cols = slice(j * SUB, (j + 1) * SUB)
                correction(j, n, m_, out_ok[1], g)
                dve.wait_ge(zr_ok, 2 * r + j)
                dve.wait_ge(zg_ok[j], r + 1)
                nc.vector.tensor_tensor(zc[:], zg[j][:], cos_sb[:, cols], ALU.mult).then_inc(zc_ok, 1)
                dve.wait_ge(rot_ok[j], r + 1)
                nc.vector.tensor_tensor(zs[:], rot, sin_sb[:, cols], ALU.mult).then_inc(rotated[j], 1)
                dve.wait_ge(zc_ok, 2 * r + j + 1)
                dve.wait_ge(rotated[j], r + 1)
                dve.wait_ge(out_ok[0][1 - j], g + j)
                nc.vector.tensor_tensor(zr[:], zc[:], zs[:], ALU.add).then_inc(zr_ok, 1)
                dve.wait_ge(stored[0][j], 16 * g)
                dve.wait_ge(corr_ok[j], n + 1)
                dve.wait_ge(zr_ok, 2 * r + j + 1)
                nc.vector.scalar_tensor_tensor(out_t[0][j][:], zr[:], -0.5, corr[j][:], ALU.mult, ALU.mult)\
                    .then_inc(out_ok[0][j], 1)

            def value(j, g, r):
                dve.wait_ge(vtr_ok[j], r + 1)
                dve.wait_ge(stored[1][j], 16 * g)
                nc.vector.tensor_copy(v_t[j][:], vtr).then_inc(out_ok[1][j], 1)

            def x_sum(b):
                if b:
                    dve.wait_ge(x_ms_ok, b)
                for j in range(SUBS):
                    dve.wait_ge(x_sq_ok, SUBS * b + j + 1)
                    nc.vector.tensor_reduce(x_ssq[:, j * SUB:(j + 1) * SUB], x_sq[:].rearrange("p k n -> p n k"),
                                            AX.X, ALU.add).then_inc(x_ssq_ok, 1)

            def h_make(b):
                dve.wait_ge(x_r2_ok, b + 1)
                nc.vector.scalar_tensor_tensor(n_t[:], rv_banks[:, :, 0:SUB], eps[:, 0:1], n_r2[:], ALU.add, ALU.mult)\
                    .then_inc(x_t_ok, 1)
                dve.wait_ge(x_t_ok, b + 1)
                nc.vector.scalar_tensor_tensor(n_c[:], n_t[:], 3.0, n_r[:], ALU.subtract, ALU.mult)\
                    .then_inc(x_c_ok, 1)
                dve.wait_ge(x_c_ok, b + 1)
                c = n_c[:].rearrange("p a n -> p (a n)")

                def low(k):
                    dve.wait_ge(h_hi_ok, b * KD + k + 1)
                    nc.vector.tensor_tensor(h_lo[b % 2][:, k, :], h[:, k % 2, :],
                                            h_hi[b % 2][:, k, :].bitcast(F32), ALU.subtract).then_inc(h_lo_ok, 1)

                for k in range(KD):
                    if b or k > 1:
                        dve.wait_ge(h_lo_ok, b * KD + k - 1)
                    nc.vector.scalar_tensor_tensor(h[:, k % 2, :], x_raw[:, k, :], g_x[:, k:k + 1], c,
                                                   ALU.mult, ALU.mult).then_inc(h_ok, 1)
                    if k:
                        low(k - 1)
                low(KD - 1)

            nc.vector.memset(eps[:], EPS).then_inc(eps_ok, 1)
            dve.wait_ge(const_ld, 5 * 16)
            for out, src, by in ((g_x[:], g_in[:, 0:KD], -0.5), (g_q[:, 0:1], g_in[:, KD:KD + 1], -0.5 * SCALE),
                                 (g_q[:, 1:2], g_in[:, KD + 1:KD + 2], -0.5),
                                 (g_r[:, 0:1], g_in[:, KD + 2:KD + 3], SCALE),
                                 (g_r[:, 1:2], g_in[:, KD + 3:KD + 4], 1.0)):
                nc.vector.tensor_scalar(out, src, by, None, ALU.mult).then_inc(gains_ok, 1)
            dve.wait_ge(gains_ok, 5)
            dve.wait_ge(eps_ok, 1)
            x_sum(0)
            for s in range(2):
                split_lo(s, 0)
            h_make(0)
            for b in range(N_BLOCKS):
                if b < LAST:
                    x_sum(b + 1)
                m0 = 2 * b * NORMS

                with nc.vector.Fori(0, QK_PAIRS) as i:
                    g, n, m_ = b * PAIRS + i, b * NORMS + 2 * i, m0 + 4 * i
                    norm(0, 0, g, n, m_)
                    split_lo(0, g + 1)
                    norm(0, 1, g, n, m_ + 1)
                    norm(1, 0, g, n + 1, m_ + 2)
                    split_lo(1, g + 1)
                    norm(1, 1, g, n + 1, m_ + 3)
                if b < LAST:
                    h_make(b + 1)
                dve.wait_ge(cs_ld, 32 * (b + 1))

                def rv(i, gain, prefetch):
                    g, n, r = b * PAIRS + QK_PAIRS + i, b * NORMS + 2 * QK_PAIRS + i, b * RV_PAIRS + i
                    m_ = m0 + 4 * QK_PAIRS + 2 * i
                    norm_rotary(0, g, n, m_, r)
                    if prefetch:
                        split_lo(0, g + 1)
                    norm_rotary(1, g, n, m_ + 1, r)
                    value(0, g, r)
                    if prefetch:
                        split_lo(1, g + 1)
                    value(1, g, r)

                rv_loop(nc.vector, rv, b == LAST)


def attend(nc, q_a, k_a, qk_b, v_all, ka_cache, kb_cache, va_cache, vb_cache, rel_rows, sinks, ident, oT):
    TILES = SEQ // P
    UNITS, A_UNITS = 12, HEADS
    FULL = 5
    NEAR = 2 * P
    HALF = FULL * P // 2
    LOOP = FULL + 1
    KEYS = SEQ + 2 * P
    PAIRS_A, PAIRS_B = 4, 4
    CLEARED = 11
    NQ, NKEY = PAIRS_A + PAIRS_B, PAIRS_A + 1
    with ExitStack() as ctx:
        m = Memory(nc, ctx, "attend")
        k_hi = m.sbuf("k_hi", [P, NKEY, KEYS], F32R)
        k_lo = m.sbuf("k_lo", [P, NKEY, KEYS], F32R)
        v = m.sbuf("v", [P, TILES + 2, NKEY * P])
        raw = m.sbuf("raw", [P, PAIRS_A + NKEY, P])
        raw_b = m.sbuf("raw_b", [P, PAIRS_B, P])
        q_hi = m.sbuf("q_hi", [P, 2 * NQ, P], F32R)
        q_lo = m.sbuf("q_lo", [P, 2 * NQ, P], F32R)
        bias = m.sbuf("bias", [P, HEADS, NEAR])
        far = m.sbuf("far", [P, HEADS, 2])
        sink = m.sbuf("sink", [P, HEADS])
        neg_sink = m.sbuf("neg_sink", [P, HEADS])
        mask_q = m.sbuf("mask_q", [P, P], BF16)
        mask_k = m.sbuf("mask_k", [P, NEAR], BF16)
        ident_sb = m.sbuf("ident", [P, P])
        prob = [m.sbuf(f"prob{i}", [P, FULL * P]) for i in range(2)]
        prob_t = [m.sbuf(f"prob_t{i}", [P, FULL * P]) for i in range(2)]
        nmax_raw = m.sbuf("nmax_raw", [P, 2])
        nmax = [m.sbuf(f"nmax{i}", [P, 2]) for i in range(2)]
        s_arg = [m.sbuf(f"s_arg{i}", [P, 2]) for i in range(2)]
        den = [m.sbuf(f"den{i}", [P, 2]) for i in range(4)]
        s_exp = [m.sbuf(f"s_exp{i}", [P, 2]) for i in range(4)]
        dsum = m.sbuf("dsum", [P, 2])
        rden = m.sbuf("rden", [P, 2])
        o = m.sbuf("o", [P, D_MODEL])
        o_t = m.sbuf("o_t", [P, KD, P])
        s_ps = [m.psum(f"s{i}", [P, 2, 512]) for i in range(2)]
        t_ps = m.psum("t", [P, 1024])
        o_ps = [m.psum(f"o{i}", [P, 512]) for i in range(2)]

        ld, ld_b, const_ld, cache_ld = m.sem("ld"), m.sem("ld_b"), m.sem("const_ld"), m.sem("cache_ld")
        zero_ok, bias_sub, bias_set, k0_hi, k0_ok = (
            m.sem(n) for n in ("zero_ok", "bias_sub", "bias_set", "k0_hi", "k0_ok"))
        hi_ok, qk_ok, hi_b_ok, qb_ok = m.sem("hi_ok"), m.sem("qk_ok"), m.sem("hi_b_ok"), m.sem("qb_ok")
        s_ok, biased, red_ok, min_ok, max_ok, exp_ok = (
            m.sem(n) for n in ("s_ok", "biased", "red_ok", "min_ok", "max_ok", "exp_ok"))
        t_ok, t_act, t_dve, pv_ok, dsum_ok, rden_ok, o_ok, o_st = (
            m.sem(n) for n in ("t_ok", "t_act", "t_dve", "pv_ok", "dsum_ok", "rden_ok", "o_ok", "o_st"))

        def window(n, mixer):
            if isinstance(n, int) and n == 0:
                return SEQ, 2 * P
            w = FULL if mixer == "a" else 2
            if isinstance(n, int):
                w = min(n, w)
            return (n - w) * P, w * P

        def first_tile(n, mixer):
            return TILES if isinstance(n, int) and n == 0 else n - window(n, mixer)[1] // P

        def before(n, u):
            return (n, u - 1) if u else (n - 1, UNITS - 1)

        def outs(n, u):
            return n if u > 1 or (isinstance(n, int) and n == 0) else n - 1

        def turns(n, u):
            return UNITS * n + u + outs(n, u)

        def dve_turns(n, u):
            whole = 0 if isinstance(n, int) and n < FULL else A_UNITS * (n - FULL) + min(u, A_UNITS)
            return whole + outs(n, u)

        def output_turn(n):
            return turns(n + 1, 2) - (3 if isinstance(n, int) and n == TILES else 1)

        def dve_output_turn(n):
            return dve_turns(n + 1, 2) - (3 if isinstance(n, int) and n == TILES else 1)

        def is_whole(n, u):
            return u < A_UNITS and window(n, "a")[1] == FULL * P

        def scores_of(n, u):
            ps, sb = s_ps[u % 2], prob[u % 2]
            if is_whole(n, u):
                return ps[:, :, 0:HALF], sb[:].rearrange("p (a n) -> p a n", a=2)
            w = window(n, "a" if u < A_UNITS else "b")[1]
            if u < A_UNITS:
                return ps[:, 0, 0:w], sb[:, 0:w]
            return (ps[:, 0, 0:2 * w].rearrange("p (a n) -> p a n", a=2),
                    sb[:, 0:2 * w].rearrange("p (a n) -> p a n", a=2))

        def run(eng, step, last):
            for n in range(LOOP):
                for u in range(UNITS):
                    step(n, u)
            with eng.Fori(LOOP, TILES + 1) as n:
                for u in range(UNITS):
                    step(n, u)
            last()

        block = ctx.enter_context(nc.Block())

        @block.sync
        def _(sp):
            def load(n):
                c, w = (SEQ, DEC) if isinstance(n, int) and n == 0 else ((n - 1) * P, P)
                tile = TILES + 1 if isinstance(n, int) and n == 0 else n - 1
                sp.dma_start(raw[:, 0:PAIRS_A, 0:w], q_a[:, :, ds(c, w)].rearrange("f p n -> p f n")).then_inc(ld, 16)
                sp.dma_start(raw[:, PAIRS_A:2 * PAIRS_A, 0:w], k_a[:, :, ds(c, w)].rearrange("f p n -> p f n"))\
                    .then_inc(ld, 16)
                sp.dma_start(raw[:, 2 * PAIRS_A, 0:w], qk_b[PAIRS_B, :, ds(c, w)]).then_inc(ld, 16)
                sp.dma_start(v[0:w, ds(tile, 1), :].rearrange("p a f -> p (a f)"), v_all[ds(c, w), :]).then_inc(ld, 16)

            def load_b(n):
                c, w = (SEQ, DEC) if isinstance(n, int) and n == 0 else ((n - 1) * P, P)
                sp.dma_start(raw_b[:, :, 0:w], qk_b[0:PAIRS_B, :, ds(c, w)].rearrange("f p n -> p f n"))\
                    .then_inc(ld_b, 16)

            def store(n):
                c, w = (SEQ, DEC) if isinstance(n, int) and n == 0 else ((n - 1) * P, P)
                sp.wait_ge(t_act, output_turn(n) + 1)
                sp.wait_ge(t_dve, dve_output_turn(n) + 1)
                sp.dma_start(oT[:, :, ds(c, w)].rearrange("k p n -> p k n"), o_t[:, :, 0:w]).then_inc(o_st, 16)

            sp.dma_start(raw[:, PAIRS_A:2 * PAIRS_A, :], ka_cache.rearrange("f p n -> p f n")).then_inc(cache_ld, 16)
            sp.dma_start(raw[:, 2 * PAIRS_A, :], kb_cache).then_inc(cache_ld, 16)
            sp.dma_start(v[:, TILES, 0:PAIRS_A * P], va_cache).then_inc(cache_ld, 16)
            sp.dma_start(v[:, TILES, PAIRS_A * P:], vb_cache).then_inc(cache_ld, 16)
            sp.dma_start(ident_sb[:], ident).then_inc(const_ld, 16)
            row = rel_rows.shape[1] * rel_rows.shape[2]
            sp.dma_start(bias[:], bass.AP(rel_rows.tensor, P - 1, [[row - 1, P], [rel_rows.shape[2], HEADS], [1, NEAR]]))\
                .then_inc(const_ld, 16)
            sp.dma_start(far[:], rel_rows[:, :, 0:2]).then_inc(const_ld, 16)
            sp.dma_start(sink[:], bass.AP(sinks.tensor, 0, [[0, P], [1, HEADS]])).then_inc(const_ld, 16)
            sp.wait_ge(zero_ok, CLEARED)
            sp.wait_ge(k0_ok, 1)
            load(0)
            load_b(0)
            for n in range(LOOP - 1):
                sp.wait_ge(qk_ok, n + 1)
                load(n + 1)
                sp.wait_ge(qb_ok, n + 1)
                load_b(n + 1)
                if n:
                    store(n - 1)
            with sp.Fori(LOOP - 1, TILES) as n:
                sp.wait_ge(qk_ok, n + 1)
                load(n + 1)
                sp.wait_ge(qb_ok, n + 1)
                load_b(n + 1)
                store(n - 1)
            store(TILES - 1)
            store(TILES)
            sp.wait_ge(o_st, 16 * (TILES + 1))

        @block.gpsimd
        def _(pool):
            for done, (out, value) in enumerate((
                    (q_hi[:].bitcast(F32), 0.0), (q_lo[:].bitcast(F32), 0.0), (v[DEC:, TILES + 1, :], 0.0),
                    (raw_b[:, :, DEC:], 0.0), (mask_q[:], 0.0), (mask_k[:], 0.0),
                    (mask_q[0:1, CHUNK:], 1.0), (mask_q[32:33, 0:CHUNK], 1.0),
                    (mask_k[0:1, 0:CHUNK], NEG), (mask_k[32:33, NEAR - CHUNK:], NEG))):
                if done:
                    pool.wait_ge(zero_ok, done)
                nc.gpsimd.memset(out, value).then_inc(zero_ok, 1)
            pool.wait_ge(zero_ok, 10)
            pool.wait_ge(k0_ok, 1)
            nc.gpsimd.memset(raw[:, :, DEC:], 0.0).then_inc(zero_ok, 1)

        @block.tensor
        def _(pe):
            def scores(n, u):
                if u == 0:
                    pe.wait_ge(qk_ok, n + 1)
                if u == A_UNITS:
                    pe.wait_ge(qb_ok, n + 1)
                k = UNITS * n + u
                if not isinstance(n, int) or k > 1:
                    pe.wait_ge(exp_ok, k - 1)
                ps = s_ps[u % 2]
                slots = [(u, u // 2)] if u < A_UNITS else [(2 * u - 8 + i, PAIRS_A) for i in range(2)]
                c, w = window(n, "a" if u < A_UNITS else "b")
                spans = [(0, 0, HALF), (1, HALF, HALF)] if is_whole(n, u) else [(0, 0, w)]
                for at, (slot, pair) in enumerate(slots):
                    for bank, first, width in spans:
                        out = ps[:, bank, at * w:at * w + width]
                        masked = (bank == 0 and is_whole(n, u)) or u >= A_UNITS
                        if masked:
                            cols = w if u >= A_UNITS else CHUNK
                            first_key = NEAR - w if u >= A_UNITS else 0
                            nc.tensor.matmul(out[:, 0:cols], mask_q[:], mask_k[:, first_key:first_key + cols],
                                             start=True, stop=False, skip_group_check=True)
                        for q, key in PASSES:
                            last = nc.tensor.matmul(
                                out, (q_hi, q_lo)[q][:, slot, :],
                                (k_hi, k_lo)[key][:, pair, ds(c + first, width)],
                                start=(q, key) == PASSES[0] and not masked, stop=(q, key) == PASSES[-1],
                                skip_group_check=masked)
                last.then_inc(s_ok, 1)

            def transposes(n, u):
                k = UNITS * n + u
                pe.wait_ge(exp_ok, k + 1)
                pe.wait_ge(t_act, turns(n, u))
                pe.wait_ge(t_dve, dve_turns(n, u))
                w = window(n, "a")[1] if u < A_UNITS else 2 * window(n, "b")[1]
                for j in range(w // P):
                    cols = slice(j * P, (j + 1) * P)
                    last = nc.tensor.transpose(t_ps[:, cols], prob[u % 2][:, cols], ident_sb[:])
                last.then_inc(t_ok, 1)

            def values(n, u):
                k = UNITS * n + u
                pe.wait_ge(t_act, turns(n, u) + 1)
                pe.wait_ge(t_dve, dve_turns(*((n, u + 1) if u + 1 < A_UNITS else (n, u))) if not is_whole(n, u)
                           else dve_turns(n, u) + 1)
                if not isinstance(n, int) or k > 1:
                    pe.wait_ge(o_ok, k - 1)
                mixer = "a" if u < A_UNITS else "b"
                tile, w = first_tile(n, mixer), window(n, mixer)[1] // P
                pair = u // 2 if u < A_UNITS else PAIRS_A
                for head in range(1 if u < A_UNITS else 2):
                    for j in range(w):
                        src = (head * w + j) * P
                        last = nc.tensor.matmul(
                            o_ps[u % 2][:, head * P:(head + 1) * P], prob_t[u % 2][:, src:src + P],
                            v[:, ds(tile + j, 1), pair * P:(pair + 1) * P].rearrange("p a f -> p (a f)"),
                            start=(j == 0), stop=(j == w - 1))
                last.then_inc(pv_ok, 1)

            def output(n):
                pe.wait_ge(o_ok, UNITS * (n + 1))
                pe.wait_ge(t_act, output_turn(n))
                pe.wait_ge(t_dve, dve_output_turn(n))
                for k in range(KD):
                    last = nc.tensor.transpose(t_ps[:, k * P:(k + 1) * P], o[:, k * P:(k + 1) * P], ident_sb[:])
                last.then_inc(t_ok, 1)

            def step(n, u):
                first = isinstance(n, int) and n == 0
                scores(n, u)
                if not (first and u < 1):
                    transposes(*before(n, u))
                if not (first and u < 2):
                    values(*before(*before(n, u)))
                if u == 2 and not first:
                    output(n - 1)

            def last():
                transposes(TILES, UNITS - 1)
                values(TILES, UNITS - 2)
                values(TILES, UNITS - 1)
                output(TILES)

            pe.wait_ge(const_ld, 64)
            pe.wait_ge(zero_ok, CLEARED)
            run(pe, step, last)

        @block.scalar
        def _(act):
            nc.scalar.preload_act_table_set("natural_log_exp_and_others")

            def split(n):
                act.wait_ge(ld, 64 * (n + 1))
                if not isinstance(n, int) or n:
                    act.wait_ge(s_ok, UNITS * (n - 1) + A_UNITS)
                for i in range(2):
                    part = slice(i * HEAD, (i + 1) * HEAD)
                    nc.scalar.activation(q_hi[part, i:A_UNITS:2, :], raw[part, 0:PAIRS_A, :], ACT.Copy)\
                        .then_inc(hi_ok, 1)
                c = SEQ + P if isinstance(n, int) and n == 0 else (n - 1) * P
                nc.scalar.activation(k_hi[:, :, ds(c, P)], raw[:, PAIRS_A:, :], ACT.Copy).then_inc(hi_ok, 1)

            def split_b(n):
                act.wait_ge(ld_b, 16 * (n + 1))
                if not isinstance(n, int) or n:
                    act.wait_ge(s_ok, UNITS * n)
                for i in range(2):
                    part = slice(i * HEAD, (i + 1) * HEAD)
                    nc.scalar.activation(q_hi[part, A_UNITS + i:2 * NQ:2, :], raw_b[part, :, :], ACT.Copy)\
                        .then_inc(hi_b_ok, 1)

            def exps(n, u):
                k = UNITS * n + u
                act.wait_ge(max_ok, k + 1)
                ps, sb = scores_of(n, u)
                if not isinstance(n, int) or k > 1:
                    act.wait_ge(t_ok, turns(*before(n, u)))
                if not isinstance(n, int) or k > 3:
                    act.wait_ge(o_ok, k - 3)
                if u < A_UNITS:
                    nc.scalar.activation(sb, ps, ACT.Exp, bias=nmax[u % 2][:, 0:1], accum_out=den[u % 4][:, 0:1])\
                        .then_inc(exp_ok, 1)
                else:
                    for i in range(2):
                        nc.scalar.activation(sb[:, i, :], ps[:, i, :], ACT.Exp, bias=nmax[u % 2][:, i:i + 1],
                                             accum_out=den[u % 4][:, i:i + 1])
                    nc.scalar.activation(s_exp[u % 4][:], s_arg[u % 2][:], ACT.Exp).then_inc(exp_ok, 1)

            def copy_t(n, u):
                k = UNITS * n + u
                act.wait_ge(t_ok, turns(n, u) + 1)
                if not isinstance(n, int) or k > 1:
                    act.wait_ge(pv_ok, k - 1)
                w = min(512, window(n, "a")[1] if u < A_UNITS else 2 * window(n, "b")[1])
                nc.scalar.activation(prob_t[u % 2][:, 0:w], t_ps[:, 0:w], ACT.Copy).then_inc(t_act, 1)

            def copy_o(n):
                act.wait_ge(t_ok, output_turn(n) + 1)
                if not isinstance(n, int) or n:
                    act.wait_ge(o_st, 16 * n)
                nc.scalar.activation(o_t[:, 0:4, :], t_ps[:, 0:512], ACT.Copy).then_inc(t_act, 1)

            def step(n, u):
                first = isinstance(n, int) and n == 0
                if not (first and u < 1):
                    copy_t(*before(n, u))
                exps(n, u)
                if u == 2 and not first:
                    copy_o(n - 1)
                if u == 3:
                    split_b(n)
                if u == 9 and not (isinstance(n, int) and n == TILES):
                    split(n + 1)

            act.wait_ge(cache_ld, 64)
            nc.scalar.activation(k_hi[:, :, SEQ:SEQ + P], raw[:, PAIRS_A:, :], ACT.Copy).then_inc(k0_hi, 1)
            act.wait_ge(zero_ok, CLEARED)
            split(0)
            for n in range(LOOP):
                for u in range(UNITS):
                    step(n, u)
            with nc.scalar.Fori(LOOP, TILES) as n:
                for u in range(UNITS):
                    step(n, u)
            for u in range(UNITS):
                step(TILES, u)
            copy_t(TILES, UNITS - 1)
            copy_o(TILES)

        @block.vector
        def _(dve):
            def split(n):
                for i in range(2):
                    part = slice(i * HEAD, (i + 1) * HEAD)
                    dve.wait_ge(hi_ok, 3 * n + i + 1)
                    nc.vector.tensor_tensor(q_lo[part, i:A_UNITS:2, :], raw[part, 0:PAIRS_A, :],
                                            q_hi[part, i:A_UNITS:2, :].bitcast(F32), ALU.subtract)
                dve.wait_ge(hi_ok, 3 * n + 3)
                c = SEQ + P if isinstance(n, int) and n == 0 else (n - 1) * P
                nc.vector.tensor_tensor(k_lo[:, :, ds(c, P)], raw[:, PAIRS_A:, :],
                                        k_hi[:, :, ds(c, P)].bitcast(F32), ALU.subtract).then_inc(qk_ok, 1)

            def split_b(n):
                for i in range(2):
                    part = slice(i * HEAD, (i + 1) * HEAD)
                    dve.wait_ge(hi_b_ok, 2 * n + i + 1)
                    last = nc.vector.tensor_tensor(q_lo[part, A_UNITS + i:2 * NQ:2, :], raw_b[part, :, :],
                                                   q_hi[part, A_UNITS + i:2 * NQ:2, :].bitcast(F32), ALU.subtract)
                last.then_inc(qb_ok, 1)

            def maxima(n, u):
                k = UNITS * n + u
                dve.wait_ge(s_ok, k + 1)
                ps, _ = scores_of(n, u)
                if u < A_UNITS:
                    w = window(n, "a")[1]
                    near = min(w, NEAR)
                    at = s_ps[u % 2][:, 1, HALF - NEAR:HALF] if is_whole(n, u) else s_ps[u % 2][:, 0, w - near:w]
                    nc.vector.tensor_tensor(at, at, bias[:, u, NEAR - near:], ALU.add).then_inc(biased, 1)
                    dve.wait_ge(biased, A_UNITS * n + u + 1)
                    axis = AX.XY if is_whole(n, u) else AX.X
                    nc.vector.tensor_reduce(nmax[u % 2][:, 0:1], ps, axis, ALU.max, negate=True).then_inc(max_ok, 1)
                else:
                    b = PAIRS_B * n + u - A_UNITS
                    pair = slice(2 * (u - A_UNITS), 2 * (u - A_UNITS) + 2)
                    nc.vector.tensor_reduce(nmax_raw[:], ps, AX.X, ALU.max, negate=True).then_inc(red_ok, 1)
                    dve.wait_ge(red_ok, b + 1)
                    nc.vector.tensor_tensor(nmax[u % 2][:], nmax_raw[:], neg_sink[:, pair], ALU.min).then_inc(min_ok, 1)
                    dve.wait_ge(min_ok, b + 1)
                    nc.vector.tensor_tensor(s_arg[u % 2][:], sink[:, pair], nmax[u % 2][:], ALU.add).then_inc(max_ok, 1)

            def copy_t(n, u):
                if is_whole(n, u):
                    dve.wait_ge(t_ok, turns(n, u) + 1)
                    dve.wait_ge(pv_ok, UNITS * n + u - 1)
                    nc.vector.tensor_copy(prob_t[u % 2][:, 512:], t_ps[:, 512:FULL * P]).then_inc(t_dve, 1)

            def copy_o(n):
                dve.wait_ge(t_ok, output_turn(n) + 1)
                if not isinstance(n, int) or n:
                    dve.wait_ge(o_st, 16 * n)
                nc.vector.tensor_copy(o_t[:, 4:8, :], t_ps[:, 512:1024].rearrange("p (k n) -> p k n", k=4))\
                    .then_inc(t_dve, 1)

            def divide(n, u):
                k = UNITS * n + u
                dve.wait_ge(pv_ok, k + 1)
                if u < A_UNITS:
                    heads, total = ((u, u % 2, 0),), den[u % 4][:, 0:1]
                else:
                    i = u - A_UNITS
                    heads, total = ((HEADS + i, 0, 0), (HEADS + PAIRS_B + i, 3, 1)), dsum[:]
                    nc.vector.tensor_tensor(dsum[:], den[u % 4][:], s_exp[u % 4][:], ALU.add).then_inc(dsum_ok, 1)
                    dve.wait_ge(dsum_ok, PAIRS_B * n + i + 1)
                if not isinstance(n, int) or k:
                    dve.wait_ge(o_ok, k)
                nc.vector.reciprocal(rden[:, 0:len(heads)], total).then_inc(rden_ok, 1)
                dve.wait_ge(rden_ok, k + 1)
                if not isinstance(n, int) or n:
                    dve.wait_ge(t_ok, turns(n, 2))
                for head, half, i in heads:
                    last = nc.vector.tensor_scalar(o[:, head * HEAD:(head + 1) * HEAD],
                                                   o_ps[u % 2][:, half * HEAD:(half + 1) * HEAD],
                                                   rden[:, i:i + 1], None, ALU.mult)
                last.then_inc(o_ok, 1)

            def step(n, u):
                first = isinstance(n, int) and n == 0
                maxima(n, u)
                if not (first and u < 1):
                    copy_t(*before(n, u))
                if not (first and u < 2):
                    divide(*before(*before(n, u)))
                if u == 2 and not first:
                    copy_o(n - 1)
                if u == 3:
                    split_b(n)
                if u == 9 and not (isinstance(n, int) and n == TILES):
                    split(n + 1)

            dve.wait_ge(k0_hi, 1)
            nc.vector.tensor_tensor(k_lo[:, :, SEQ:SEQ + P], raw[:, PAIRS_A:, :],
                                    k_hi[:, :, SEQ:SEQ + P].bitcast(F32), ALU.subtract).then_inc(k0_ok, 1)
            dve.wait_ge(const_ld, 64)
            for h in range(HEADS):
                nc.vector.tensor_scalar(bias[:, h, :], bias[:, h, :], far[:, h, 0:1], None, ALU.subtract)\
                    .then_inc(bias_sub, 1)
            nc.vector.tensor_scalar(neg_sink[:], sink[:], -1.0, None, ALU.mult).then_inc(bias_sub, 1)
            dve.wait_ge(bias_sub, HEADS + 1)
            nc.vector.memset(bias[0:CHUNK, :, NEAR - CHUNK:], NEG).then_inc(bias_set, 1)
            dve.wait_ge(bias_set, 1)
            split(0)
            for n in range(LOOP):
                for u in range(UNITS):
                    step(n, u)
            with nc.vector.Fori(LOOP, TILES) as n:
                for u in range(UNITS):
                    step(n, u)
            for u in range(UNITS):
                step(TILES, u)
            copy_t(TILES, UNITS - 1)
            divide(TILES, UNITS - 2)
            divide(TILES, UNITS - 1)
            copy_o(TILES)


def combine(nc, oT, xT, w_o, gains, all_ones, x1T, h2T):
    PAIRS = KD // 2
    LAST = N_BLOCKS - 1
    KS = KD // 2
    with ExitStack() as ctx:
        m = Memory(nc, ctx, "combine")
        o_raw = [m.sbuf(f"o_raw{i}", [P, 2, BLOCK]) for i in range(2)]
        o_hi = [m.sbuf(f"o_hi{i}", [P, KD, BLOCK], F32R) for i in range(2)]
        o_lo = [m.sbuf(f"o_lo{i}", [P, KD, BLOCK], F32R) for i in range(2)]
        x1 = [m.sbuf(f"x1{i}", [P, KD, BLOCK]) for i in range(2)]
        x_sq = m.sbuf("x_sq", [P, KD, SUB])
        ssq = m.sbuf("ssq", [P, BLOCK])
        n_t = m.sbuf("n_t", [P, SUBS, SUB])
        n_r = m.sbuf("n_r", [P, SUBS, SUB])
        n_r2 = m.sbuf("n_r2", [P, SUBS, SUB])
        n_c = m.sbuf("n_c", [P, SUBS, SUB])
        h2 = [m.sbuf(f"h2{i}", [P, BLOCK]) for i in range(2)]
        w_raw = [m.sbuf(f"w_raw{s}", [P, KD, P]) for s in range(2)]
        w_hi = [m.sbuf(f"w_hi{s}", [P, KD, P], F32R) for s in range(2)]
        w_lo = [m.sbuf(f"w_lo{s}", [P, KD, P], F32R) for s in range(2)]
        g_in = m.sbuf("g_in", [P, KD])
        g_x = m.sbuf("g_x", [P, KD])
        eps = m.sbuf("eps", [P, 1])
        ones_sb = m.sbuf("ones", [P, P])
        z = [[m.psum(f"z{s}{i}", [P, 512]) for i in range(2)] for s in range(2)]
        ms = m.psum("ms", [P, SUBS, 512])

        const_ld = m.sem("const_ld")
        o_ld, x_ld, w_ld = ([m.sem(f"{n}{i}") for i in range(2)] for n in ("o_ld", "x_ld", "w_ld"))
        w_hi_ok, w_lo_ok = ([m.sem(f"{n}{s}") for s in range(2)] for n in ("w_hi_ok", "w_lo_ok"))
        z_ok = [[m.sem(f"z_ok{s}{i}") for i in range(2)] for s in range(2)]
        x1_ok = [[m.sem(f"x1_ok{s}{i}") for i in range(2)] for s in range(2)]
        o_hi_ok, o_lo_ok = m.sem("o_hi_ok"), m.sem("o_lo_ok")
        eps_ok, gains_ok = m.sem("eps_ok"), m.sem("gains_ok")
        sq_ok, ssq_ok, ms_ok = m.sem("sq_ok"), m.sem("ssq_ok"), m.sem("ms_ok")
        ln_ok, r_ok, r2_ok, t_ok, c_ok = (m.sem(n) for n in ("ln_ok", "r_ok", "r2_ok", "t_ok", "c_ok"))
        h2_ok, x1_st = m.sem("h2_ok"), m.sem("x1_st")
        h2_st = [m.sem(f"h2_st{i}") for i in range(2)]

        block = ctx.enter_context(nc.Block())

        @block.sync
        def _(sp):
            def load_pair(g, src):
                for s in range(2):
                    sp.wait_ge(w_lo_ok[s], g)
                    sp.dma_start(w_raw[s][:], src(s)).then_inc(w_ld[s], 16)

            load_pair(0, lambda s: w_o[0, s])
            for b in range(N_BLOCKS):
                with sp.Fori(1, PAIRS) as i:
                    load_pair(b * PAIRS + i, lambda s: w_o[ds(i, 1), s].rearrange("a p k n -> p (a k) n"))
                if b < LAST:
                    load_pair((b + 1) * PAIRS, lambda s: w_o[0, s])

        @block.gpsimd
        def _(pool):
            def load_x(b):
                pool.dma_start(x1[b % 2][:], xT[:, :, b * BLOCK:(b + 1) * BLOCK].rearrange("k p n -> p k n"))\
                    .then_inc(x_ld[b % 2], 16)

            def load_o(b):
                for q in range(KS):
                    n = KS * b + q
                    if n > 1:
                        pool.wait_ge(o_lo_ok, 2 * (n - 1))
                    pool.dma_start(o_raw[n % 2][:], oT[2 * q:2 * q + 2, :, b * BLOCK:(b + 1) * BLOCK]
                                   .rearrange("k p n -> p k n")).then_inc(o_ld[n % 2], 16)

            pool.dma_start(g_in[:], gains).then_inc(const_ld, 16)
            pool.dma_start(ones_sb[:], all_ones).then_inc(const_ld, 16)
            load_o(0)
            load_x(0)
            load_x(1)
            load_o(1)
            for b in range(N_BLOCKS):
                cols = slice(b * BLOCK, (b + 1) * BLOCK)
                for s in range(2):
                    for j in range(SUBS):
                        pool.wait_ge(x1_ok[s][j], PAIRS * (b + 1))
                pool.dma_start(x1T[:, :, cols].rearrange("k p n -> p k n"), x1[b % 2][:]).then_inc(x1_st, 16)
                if b + 2 < N_BLOCKS:
                    load_o(b + 2)
                for k in range(KD):
                    pool.wait_ge(h2_ok, KD * b + k + 1)
                    pool.dma_start(h2T[k, :, cols], h2[k % 2][:]).then_inc(h2_st[k % 2], 16)
                if b + 2 < N_BLOCKS:
                    pool.wait_ge(x1_st, 16 * (b + 1))
                    load_x(b + 2)
            pool.wait_ge(x1_st, 16 * N_BLOCKS)
            for i in range(2):
                pool.wait_ge(h2_st[i], 16 * N_BLOCKS * KD // 2)

        @block.tensor
        def _(pe):
            def pair(b, i):
                g = b * PAIRS + i
                for s in range(2):
                    pe.wait_ge(w_lo_ok[s], g + 1)
                    for j in range(SUBS):
                        pe.wait_ge(x1_ok[s][j], g)
                        cols = slice(j * SUB, (j + 1) * SUB)
                        dense(nc, z[s][j][:, 0:SUB], (lambda k: w_hi[s][:, k, :], lambda k: w_lo[s][:, k, :]),
                              (lambda k: o_hi[b % 2][:, k, cols], lambda k: o_lo[b % 2][:, k, cols]), KD)\
                            .then_inc(z_ok[s][j], 1)

            def mean_square(b):
                pe.wait_ge(ssq_ok, SUBS * (b + 1))
                if b:
                    pe.wait_ge(c_ok, b)
                for j in range(SUBS):
                    last = nc.tensor.matmul(ms[:, j, 0:SUB], ones_sb[:], ssq[:, j * SUB:(j + 1) * SUB],
                                            start=True, stop=True)
                last.then_inc(ms_ok, 1)

            pe.wait_ge(const_ld, 32)
            for b in range(N_BLOCKS):
                pe.wait_ge(o_lo_ok, KD * (b + 1))
                pair(b, 0)
                if b:
                    mean_square(b - 1)
                with pe.Fori(1, PAIRS) as i:
                    pair(b, i)
            mean_square(LAST)

        @block.scalar
        def _(act):
            nc.scalar.preload_act_table_set("natural_log_exp_and_others")

            def split_hi(s, g):
                act.wait_ge(w_ld[s], 16 * (g + 1))
                act.wait_ge(z_ok[s][1], g)
                nc.scalar.activation(w_hi[s][:], w_raw[s][:], ACT.Copy).then_inc(w_hi_ok[s], 1)

            def split_o(b):
                if b > 1:
                    act.wait_ge(z_ok[1][1], PAIRS * (b - 1))
                for k in range(KD):
                    n = KS * b + k // 2
                    act.wait_ge(o_ld[n % 2], 16 * (n // 2 + 1))
                    nc.scalar.activation(o_hi[b % 2][:, k, :], o_raw[n % 2][:, k % 2, :], ACT.Copy)\
                        .then_inc(o_hi_ok, 1)

            def squares(b):
                for s in range(2):
                    for j in range(SUBS):
                        act.wait_ge(x1_ok[s][j], PAIRS * (b + 1))
                for j in range(SUBS):
                    if b or j:
                        act.wait_ge(ssq_ok, SUBS * b + j)
                    nc.scalar.activation(x_sq[:], x1[b % 2][:, :, j * SUB:(j + 1) * SUB], ACT.Square)\
                        .then_inc(sq_ok, 1)

            def root(b):
                act.wait_ge(ms_ok, b + 1)
                if b:
                    act.wait_ge(c_ok, b)
                nc.scalar.activation(n_t[:], ms[:, :, 0:SUB], ACT.Ln, bias=eps[:, 0:1]).then_inc(ln_ok, 1)
                act.wait_ge(ln_ok, b + 1)
                nc.scalar.activation(n_r[:], n_t[:], ACT.Exp, scale=-0.5).then_inc(r_ok, 1)
                act.wait_ge(r_ok, b + 1)
                nc.scalar.activation(n_r2[:], n_r[:], ACT.Square).then_inc(r2_ok, 1)

            act.wait_ge(eps_ok, 1)
            split_hi(0, 0)
            split_o(0)
            split_hi(1, 0)
            for b in range(N_BLOCKS):
                n = PAIRS - 1 if b == LAST else PAIRS
                if b + 1 < N_BLOCKS:
                    split_o(b + 1)
                if b:
                    split_hi(0, b * PAIRS + 1)
                    split_hi(1, b * PAIRS + 1)
                    root(b - 1)
                with nc.scalar.Fori(1 if b else 0, n) as i:
                    split_hi(0, b * PAIRS + i + 1)
                    split_hi(1, b * PAIRS + i + 1)
                squares(b)
            root(LAST)

        @block.vector
        def _(dve):
            def split_lo(s, g):
                dve.wait_ge(w_hi_ok[s], g + 1)
                nc.vector.tensor_tensor(w_lo[s][:], w_raw[s][:], w_hi[s][:].bitcast(F32), ALU.subtract)\
                    .then_inc(w_lo_ok[s], 1)

            def split_o(b):
                for k in range(KD):
                    n = KS * b + k // 2
                    dve.wait_ge(o_hi_ok, b * KD + k + 1)
                    nc.vector.tensor_tensor(o_lo[b % 2][:, k, :], o_raw[n % 2][:, k % 2, :],
                                            o_hi[b % 2][:, k, :].bitcast(F32), ALU.subtract).then_inc(o_lo_ok, 1)

            def add(b, i, s, j):
                dve.wait_ge(z_ok[s][j], b * PAIRS + i + 1)
                part = x1[b % 2][:, ds(2 * i + s, 1), j * SUB:(j + 1) * SUB].rearrange("p a n -> p (a n)")
                nc.vector.tensor_tensor(part, part, z[s][j][:, 0:SUB], ALU.add).then_inc(x1_ok[s][j], 1)

            def pair(b, i, prefetch):
                for s in range(2):
                    add(b, i, s, 0)
                    add(b, i, s, 1)
                    if prefetch:
                        split_lo(s, b * PAIRS + i + 1)

            def sums(b):
                if b:
                    dve.wait_ge(ms_ok, b)
                for j in range(SUBS):
                    dve.wait_ge(sq_ok, SUBS * b + j + 1)
                    nc.vector.tensor_reduce(ssq[:, j * SUB:(j + 1) * SUB], x_sq[:].rearrange("p k n -> p n k"),
                                            AX.X, ALU.add).then_inc(ssq_ok, 1)

            def normed(b):
                dve.wait_ge(r2_ok, b + 1)
                nc.vector.scalar_tensor_tensor(n_t[:], ms[:, :, 0:SUB], eps[:, 0:1], n_r2[:], ALU.add, ALU.mult)\
                    .then_inc(t_ok, 1)
                dve.wait_ge(t_ok, b + 1)
                if b:
                    dve.wait_ge(h2_ok, KD * b)
                nc.vector.scalar_tensor_tensor(n_c[:], n_t[:], 3.0, n_r[:], ALU.subtract, ALU.mult)\
                    .then_inc(c_ok, 1)
                dve.wait_ge(c_ok, b + 1)
                for k in range(KD):
                    n = KD * b + k
                    if n > 1:
                        dve.wait_ge(h2_st[k % 2], 16 * (n // 2))
                    nc.vector.scalar_tensor_tensor(h2[k % 2][:], x1[b % 2][:, k, :], g_x[:, k:k + 1],
                                                   n_c[:].rearrange("p a n -> p (a n)"), ALU.mult, ALU.mult)\
                        .then_inc(h2_ok, 1)

            nc.vector.memset(eps[:], EPS).then_inc(eps_ok, 1)
            dve.wait_ge(const_ld, 32)
            nc.vector.tensor_scalar(g_x[:], g_in[:], -0.5, None, ALU.mult).then_inc(gains_ok, 1)
            dve.wait_ge(gains_ok, 1)
            dve.wait_ge(eps_ok, 1)
            split_lo(0, 0)
            split_o(0)
            split_lo(1, 0)
            for b in range(N_BLOCKS):
                if b + 1 < N_BLOCKS:
                    split_o(b + 1)
                dve.wait_ge(x_ld[b % 2], 16 * (b // 2 + 1))
                if b:
                    pair(b, 0, True)
                    normed(b - 1)
                with nc.vector.Fori(1 if b else 0, PAIRS - 1) as i:
                    pair(b, i, True)
                pair(b, PAIRS - 1, b < LAST)
                sums(b)
            normed(LAST)


def ffn(nc, h2T, x1T, w_gu, w_dn, conv, state, yT, gate_prompt, gate_sample):
    F_TILES = D_FF // P
    PARTS = 2
    KF = F_TILES // PARTS
    DOWN = KD // 2
    PAIRS = KF + DOWN
    LAST = N_BLOCKS - 1
    CUT = SEQ - LAST * BLOCK
    H = 2
    with ExitStack() as ctx:
        m = Memory(nc, ctx, "ffn")
        h_raw = [m.sbuf(f"h_raw{i}", [P, BLOCK]) for i in range(2)]
        h_hi = m.sbuf("h_hi", [P, KD, BLOCK], F32R)
        h_lo = m.sbuf("h_lo", [P, KD, BLOCK], F32R)
        y_hi = m.sbuf("y_hi", [P, KF, BLOCK], F32R)
        y_lo = m.sbuf("y_lo", [P, KF, BLOCK], F32R)
        acc = m.sbuf("acc", [P, KD, BLOCK])
        w_raw = [m.sbuf(f"w_raw{s}", [P, KF, P]) for s in range(2)]
        w_hi = [m.sbuf(f"w_hi{s}", [P, KF, P], F32R) for s in range(2)]
        w_lo = [m.sbuf(f"w_lo{s}", [P, KF, P], F32R) for s in range(2)]
        gate = m.sbuf("gate", [P, H + BLOCK])
        gate_s = m.sbuf("gate_s", [P, H + DEC])
        c1 = [m.sbuf(f"c1{j}", [P, SUB]) for j in range(SUBS)]
        c2 = [m.sbuf(f"c2{j}", [P, SUB]) for j in range(SUBS)]
        silu = [m.sbuf(f"silu{j}", [P, SUB]) for j in range(SUBS)]
        y = [m.sbuf(f"y{j}", [P, SUB]) for j in range(SUBS)]
        conv_sb = m.sbuf("conv", [P, F_TILES, 4])
        state_sb = m.sbuf("state", [P, F_TILES, H])
        carry = m.sbuf("carry", [P, F_TILES, H])
        tail = m.sbuf("tail", [P, F_TILES, H])
        z = [[m.psum(f"z{s}{i}", [P, 512]) for i in range(2)] for s in range(2)]

        const_ld, acc_ld, y_st = m.sem("const_ld"), m.sem("acc_ld"), m.sem("y_st")
        h_ld, w_ld = ([m.sem(f"{n}{i}") for i in range(2)] for n in ("h_ld", "w_ld"))
        w_hi_ok, w_lo_ok = ([m.sem(f"{n}{s}") for s in range(2)] for n in ("w_hi_ok", "w_lo_ok"))
        z_ok = [[m.sem(f"z_ok{s}{i}") for i in range(2)] for s in range(2)]
        z_free = [[m.sem(f"z_free{s}{i}") for i in range(2)] for s in range(2)]
        h_hi_ok, h_lo_ok, zero_ok = m.sem("h_hi_ok"), m.sem("h_lo_ok"), m.sem("zero_ok")
        c1_ok, c2_ok, conv_ok, silu_ok, y_hi_ok, y_lo_ok = (
            [m.sem(f"{n}{i}") for i in range(2)] for n in ("c1_ok", "c2_ok", "conv_ok", "silu_ok", "y_hi_ok", "y_lo_ok"))
        halo_ok, carry_ok, s_gate_ok, s1_ok, s2_ok, tail_ok, gate_st = (
            m.sem(n) for n in ("halo_ok", "carry_ok", "s_gate_ok", "s1_ok", "s2_ok", "tail_ok", "gate_st"))

        block = ctx.enter_context(nc.Block())

        @block.sync
        def _(sp):
            def load_pair(g, src, k):
                for s in range(2):
                    sp.wait_ge(w_lo_ok[s], g)
                    sp.dma_start(w_raw[s][:, 0:k, :], src(s)).then_inc(w_ld[s], 16)

            def at(w, i):
                return lambda s: w[ds(i, 1), s].rearrange("a p k n -> p (a k) n")

            sp.dma_start(conv_sb[:], conv).then_inc(const_ld, 16)
            sp.dma_start(state_sb[:], state).then_inc(const_ld, 16)
            for b in range(N_BLOCKS):
                for part in range(PARTS):
                    g0 = (b * PARTS + part) * PAIRS
                    with sp.Fori(0, KF) as i:
                        load_pair(g0 + i, at(w_gu, part * KF + i), KD)
                    load_pair(g0 + KF, at(w_dn, part * DOWN), KF)
                    with sp.Fori(1, DOWN) as i:
                        load_pair(g0 + KF + i, at(w_dn, part * DOWN + i), KF)

        @block.gpsimd
        def _(pool):
            def load_h(b):
                for k in range(KD):
                    if b or k > 1:
                        pool.wait_ge(h_lo_ok, KD * b + k - 1)
                    pool.dma_start(h_raw[k % 2][:], h2T[k, :, b * BLOCK:(b + 1) * BLOCK]).then_inc(h_ld[k % 2], 16)

            def load_acc(b):
                if b:
                    pool.wait_ge(y_st, 16 * KD * b)
                pool.dma_start(acc[:], x1T[:, :, b * BLOCK:(b + 1) * BLOCK].rearrange("k p n -> p k n"))\
                    .then_inc(acc_ld, 16)

            load_h(0)
            load_acc(0)
            for b in range(N_BLOCKS):
                if b < LAST:
                    load_h(b + 1)
                g1 = (b * PARTS + PARTS - 1) * PAIRS + KF
                for d in range(KD):
                    for j in range(SUBS):
                        pool.wait_ge(z_free[d % 2][j], g1 + d // 2 + 1)
                    pool.dma_start(yT[d, :, b * BLOCK:(b + 1) * BLOCK], acc[:, d, :]).then_inc(y_st, 16)
                if b < LAST:
                    load_acc(b + 1)
            pool.wait_ge(carry_ok, N_BLOCKS * F_TILES)
            pool.wait_ge(tail_ok, F_TILES)
            pool.dma_start(gate_sample, carry[:]).then_inc(gate_st, 16)
            pool.dma_start(gate_prompt, tail[:]).then_inc(gate_st, 16)
            pool.wait_ge(gate_st, 32)
            pool.wait_ge(y_st, 16 * KD * N_BLOCKS)

        @block.tensor
        def _(pe):
            def pair(g, hi, lo, n_k, last_wait=None):
                for s in range(2):
                    pe.wait_ge(w_lo_ok[s], g + 1)
                    for j in range(SUBS):
                        pe.wait_ge(z_free[s][j], g)
                        cols = slice(j * SUB, (j + 1) * SUB)
                        dense(nc, z[s][j][:, 0:SUB], (lambda k: w_hi[s][:, k, :], lambda k: w_lo[s][:, k, :]),
                              (lambda k: hi[:, k, cols], lambda k: lo[:, k, cols]), n_k,
                              last_wait and (lambda: last_wait(j))).then_inc(z_ok[s][j], 1)

            for b in range(N_BLOCKS):
                pe.wait_ge(h_lo_ok, KD * (b + 1))
                for part in range(PARTS):
                    n = b * PARTS + part
                    g0 = n * PAIRS
                    with pe.Fori(0, KF) as i:
                        pair(g0 + i, h_hi, h_lo, KD)
                    for j in range(SUBS):
                        pe.wait_ge(y_lo_ok[j], KF * (n + 1) - 1)
                    pair(g0 + KF, y_hi, y_lo, KF, lambda j: pe.wait_ge(y_lo_ok[j], KF * (n + 1)))
                    with pe.Fori(1, DOWN) as i:
                        pair(g0 + KF + i, y_hi, y_lo, KF)

        @block.scalar
        def _(act):
            def split_hi(s, g, n_k):
                act.wait_ge(w_ld[s], 16 * (g + 1))
                act.wait_ge(z_ok[s][1], g)
                nc.scalar.activation(w_hi[s][:, 0:n_k, :], w_raw[s][:, 0:n_k, :], ACT.Copy).then_inc(w_hi_ok[s], 1)

            def split_h(b):
                for k in range(KD):
                    act.wait_ge(h_ld[k % 2], 16 * ((KD * b + k) // 2 + 1))
                    nc.scalar.activation(h_hi[:, k, :], h_raw[k % 2][:], ACT.Copy).then_inc(h_hi_ok, 1)

            def gate_up(b, g, c, n_k):
                for j in range(SUBS):
                    act.wait_ge(z_ok[0][j], g + 1)
                    if j == 0:
                        act.wait_ge(carry_ok, c)
                    nc.scalar.activation(gate[:, H + j * SUB:H + (j + 1) * SUB], z[0][j][:, 0:SUB], ACT.Copy)\
                        .then_inc(z_free[0][j], 1)
                split_hi(0, g + 1, n_k)
                for j in range(SUBS):
                    act.wait_ge(conv_ok[j], c + 1)
                    nc.scalar.activation(silu[j][:], c1[j][:], ACT.Silu).then_inc(silu_ok[j], 1)
                split_hi(1, g + 1, n_k)

            split_hi(0, 0, KD)
            split_h(0)
            split_hi(1, 0, KD)
            for b in range(N_BLOCKS):
                for part in range(PARTS):
                    n = b * PARTS + part
                    g0, c0 = n * PAIRS, n * KF
                    with nc.scalar.Fori(0, KF - 1) as i:
                        gate_up(b, g0 + i, c0 + i, KD)
                    gate_up(b, g0 + KF - 1, c0 + KF - 1, KF)
                    if part == PARTS - 1 and b < LAST:
                        act.wait_ge(z_ok[1][1], g0 + KF)
                        split_h(b + 1)
                    with nc.scalar.Fori(0, DOWN - 1) as i:
                        split_hi(0, g0 + KF + i + 1, KF)
                        split_hi(1, g0 + KF + i + 1, KF)
                    if n + 1 < N_BLOCKS * PARTS:
                        split_hi(0, g0 + PAIRS, KD)
                        split_hi(1, g0 + PAIRS, KD)

        @block.vector
        def _(dve):
            def split_lo(s, g, n_k):
                dve.wait_ge(w_hi_ok[s], g + 1)
                nc.vector.tensor_tensor(w_lo[s][:, 0:n_k, :], w_raw[s][:, 0:n_k, :],
                                        w_hi[s][:, 0:n_k, :].bitcast(F32), ALU.subtract).then_inc(w_lo_ok[s], 1)

            def split_h(b):
                for k in range(KD):
                    dve.wait_ge(h_hi_ok, b * KD + k + 1)
                    nc.vector.tensor_tensor(h_lo[:, k, :], h_raw[k % 2][:], h_hi[:, k, :].bitcast(F32), ALU.subtract)\
                        .then_inc(h_lo_ok, 1)

            def of(ap, i):
                return ap[:, ds(i, 1), :].rearrange("p a n -> p (a n)")

            def convolve(dst, tmp, src, taps, n, waits, done):
                nc.vector.tensor_scalar(dst, src[:, H:H + n], taps[:, 2:3], taps[:, 3:4], ALU.mult, ALU.add)\
                    .then_inc(done[0], 1)
                dve.wait_ge(done[0], waits + 1)
                nc.vector.scalar_tensor_tensor(tmp, src[:, 1:1 + n], taps[:, 1:2], dst, ALU.mult, ALU.add)\
                    .then_inc(done[1], 1)
                dve.wait_ge(done[1], waits + 1)
                nc.vector.scalar_tensor_tensor(dst, src[:, 0:n], taps[:, 0:1], tmp, ALU.mult, ALU.add)\
                    .then_inc(done[2], 1)

            def gate_up(b, g, f, c, jf, n_k):
                taps = of(conv_sb, f)
                dve.wait_ge(carry_ok, c)
                nc.vector.tensor_scalar(gate[:, 0:H], of(carry, f), 1.0, None, ALU.mult).then_inc(halo_ok, 1)
                dve.wait_ge(halo_ok, c + 1)
                for j in range(SUBS):
                    dve.wait_ge(z_free[0][j], g + 1)
                    dve.wait_ge(silu_ok[j], c)
                    n = CUT - j * SUB if b == LAST and j else SUB
                    convolve(c1[j][:, 0:n], c2[j][:, 0:n], gate[:, j * SUB:H + (j + 1) * SUB], taps, n, c,
                             (c1_ok[j], c2_ok[j], conv_ok[j] if n == SUB else s_gate_ok))
                if b == LAST:
                    cs = c - LAST * F_TILES
                    nc.vector.tensor_scalar(gate_s[:, 0:H], of(state_sb, f), 1.0, None, ALU.mult).then_inc(s_gate_ok, 1)
                    nc.vector.tensor_scalar(gate_s[:, H:], gate[:, H + CUT:], 1.0, None, ALU.mult).then_inc(s_gate_ok, 1)
                    dve.wait_ge(s_gate_ok, 3 * cs + 3)
                    n = CUT - SUB
                    convolve(c1[1][:, n:], c2[1][:, n:], gate_s, taps, DEC, cs, (s1_ok, s2_ok, conv_ok[1]))
                    nc.vector.tensor_scalar(of(tail, f), gate[:, CUT:H + CUT], 1.0, None, ALU.mult).then_inc(tail_ok, 1)
                split_lo(0, g + 1, n_k)
                nc.vector.tensor_scalar(of(carry, f), gate[:, BLOCK:H + BLOCK], 1.0, None, ALU.mult).then_inc(carry_ok, 1)
                for j in range(SUBS):
                    cols = slice(j * SUB, (j + 1) * SUB)
                    dve.wait_ge(silu_ok[j], c + 1)
                    dve.wait_ge(z_ok[1][j], g + 1)
                    dve.wait_ge(y_lo_ok[j], c)
                    nc.vector.tensor_tensor(y[j][:], silu[j][:], z[1][j][:, 0:SUB], ALU.mult).then_inc(z_free[1][j], 1)
                    dve.wait_ge(z_free[1][j], g + 1)
                    hi, lo = (ap[:, ds(jf, 1), cols].rearrange("p a n -> p (a n)") for ap in (y_hi, y_lo))
                    nc.vector.tensor_scalar(hi, y[j][:], 1.0, None, ALU.mult).then_inc(y_hi_ok[j], 1)
                    dve.wait_ge(y_hi_ok[j], c + 1)
                    nc.vector.tensor_tensor(lo, y[j][:], hi.bitcast(F32), ALU.subtract).then_inc(y_lo_ok[j], 1)
                split_lo(1, g + 1, n_k)

            def down(g, i, n_k):
                for s in range(2):
                    for j in range(SUBS):
                        dve.wait_ge(z_ok[s][j], g + 1)
                        part = acc[:, ds(2 * i + s, 1), j * SUB:(j + 1) * SUB].rearrange("p a n -> p (a n)")
                        nc.vector.tensor_tensor(part, part, z[s][j][:, 0:SUB], ALU.add).then_inc(z_free[s][j], 1)
                    if n_k:
                        split_lo(s, g + 1, n_k)

            nc.vector.memset(carry[:], 0.0).then_inc(zero_ok, 1)
            dve.wait_ge(zero_ok, 1)
            dve.wait_ge(const_ld, 32)
            split_lo(0, 0, KD)
            split_h(0)
            split_lo(1, 0, KD)
            for b in range(N_BLOCKS):
                for part in range(PARTS):
                    n = b * PARTS + part
                    g0, c0, f0 = n * PAIRS, n * KF, part * KF
                    with nc.vector.Fori(0, KF - 1) as i:
                        gate_up(b, g0 + i, f0 + i, c0 + i, i, KD)
                    gate_up(b, g0 + KF - 1, f0 + KF - 1, c0 + KF - 1, KF - 1, KF)
                    if part == PARTS - 1 and b < LAST:
                        split_h(b + 1)
                    if part == 0:
                        dve.wait_ge(acc_ld, 16 * (b + 1))
                    with nc.vector.Fori(0, DOWN - 1) as i:
                        down(g0 + KF + i, i, KF)
                    down(g0 + PAIRS - 1, DOWN - 1, KD if n + 1 < N_BLOCKS * PARTS else 0)


def encoder_step(nc, a):
    scratch = {name: nc.dram_tensor(f"{name}_scratch", shape, F32, kind="Internal").ap()
               for name, shape in (("q_a", (4, P, TOKENS)), ("rel_rows", (P, HEADS, 3 * P)), ("oT", (KD, P, TOKENS)),
                                   ("x1T", (KD, P, TOKENS)), ("h2T", (KD, P, TOKENS)))}
    project(nc, a["xT"], a["w_qk"], a["w_rv"], a["gains_in"], a["rope_cos"], a["rope_sin"], a["swap"],
            a["head_ones"], a["all_ones"], a["ident"], a["rel"],
            scratch["q_a"], a["k_a"], a["qk_b"], a["v_all"], scratch["rel_rows"])
    attend(nc, scratch["q_a"], a["k_a"], a["qk_b"], a["v_all"], a["ka_cache"], a["kb_cache"], a["va_cache"],
           a["vb_cache"], scratch["rel_rows"], a["sinks"], a["ident"], scratch["oT"])
    combine(nc, scratch["oT"], a["xT"], a["w_o"], a["gains_ffn"], a["all_ones"], scratch["x1T"], scratch["h2T"])
    ffn(nc, scratch["h2T"], scratch["x1T"], a["w_gu"], a["w_dn"], a["conv"], a["state"],
        a["yT"], a["gate_prompt"], a["gate_sample"])


def kernel(**inputs):
    import numpy as np
    import concourse.bacc as bacc
    from concourse.bass_utils import run_bass_kernel_spmd

    x = {name: np.asarray(value) for name, value in inputs.items()}

    def tiles(w):
        k, n = w.shape
        return w.reshape(k // P, P, n // P, P).transpose(2, 1, 0, 3)

    def head_pairs(w):
        return w.reshape(w.shape[0], 2, HEADS // 2, HEAD).transpose(0, 2, 1, 3).reshape(w.shape[0], -1)

    width = HEADS * HEAD
    qa, ka, va, qb, kb, vb = np.split(x["w_in"][0], [width, 2 * width, 3 * width, 4 * width, 4 * width + P], axis=1)
    cols = lambda g: g[0].reshape(-1, P).T
    by_head = lambda g: np.tile(g[0], 2)[:, None]
    gate, up = np.split(x["w_gate_up"][0], 2, axis=1)
    rel = x["rel_bias_a"][0][:, ::-1]

    pos = np.concatenate([np.arange(SEQ), PAST + np.arange(DEC)]).astype(np.float32)
    inv = np.power(np.float32(10000.0), -np.arange(HEAD // 2, dtype=np.float32) / np.float32(HEAD // 2))
    angle = (pos[None, :] * inv[:, None]).astype(np.float32)
    cos, sin = np.cos(angle), np.sin(angle)
    swap = np.zeros((P, P), np.float32)
    swap[np.arange(P) ^ (HEAD // 2), np.arange(P)] = 1
    head_ones = np.kron(np.eye(2), np.full((HEAD, HEAD), 1 / HEAD))

    arrays = dict(
        xT=np.concatenate([x["x_prompt"][0], x["x_sample"][0]]).T.reshape(KD, P, TOKENS),
        w_qk=np.stack([tiles(qa), tiles(ka)], 1),
        w_rv=np.stack([tiles(np.concatenate([head_pairs(qb), kb], 1)), tiles(np.concatenate([va, vb], 1))], 1),
        gains_in=np.concatenate([cols(x["norm_attn"]), by_head(x["q_norm_a"]), by_head(x["k_norm_a"]),
                                 by_head(x["q_norm_b"]), by_head(x["k_norm_b"])], 1),
        rope_cos=np.tile(cos, (4, 1)), rope_sin=np.tile(np.concatenate([-sin, sin]), (2, 1)),
        swap=swap, head_ones=head_ones, all_ones=np.full((P, P), 1 / D_MODEL), ident=np.eye(P),
        ka_cache=x["cache_a_k"].reshape(PAST, width).T.reshape(-1, P, PAST),
        kb_cache=x["cache_b_k"].reshape(PAST, P).T,
        va_cache=x["cache_a_v"].reshape(PAST, width), vb_cache=x["cache_b_v"].reshape(PAST, P),
        rel=np.concatenate([np.repeat(rel[:, :1], MAX_REL - 1, 1), rel], 1),
        sinks=x["sinks_b"].reshape(2, HEADS // 2).T.reshape(-1),
        w_o=tiles(x["w_out"][0]).reshape(KD // 2, 2, P, KD, P), gains_ffn=cols(x["norm_ffn"]),
        w_gu=np.stack([tiles(gate), tiles(up)], 1),
        w_dn=x["w_down"][0].reshape(2, KF // 2, P, KD // 2, 2, P).transpose(0, 3, 4, 2, 1, 5)
            .reshape(KD, 2, P, KF // 2, P),
        conv=np.concatenate([x["conv_w"][0], x["conv_b"]]).reshape(4, KF, P).transpose(2, 1, 0),
        state=x["state_conv"].reshape(2, KF, P).transpose(2, 1, 0))
    returned = dict(k_a=(4, P, TOKENS), qk_b=(5, P, TOKENS), v_all=(TOKENS, 5 * P), yT=(KD, P, TOKENS),
                    gate_prompt=(P, KF, 2), gate_sample=(P, KF, 2))

    nc = bacc.Bacc("TRN2", target_bir_lowering=False, num_devices=1)
    arrays = {name: np.ascontiguousarray(value, dtype=np.float32) for name, value in arrays.items()}
    drams = {name: nc.dram_tensor(name, value.shape, F32, kind="ExternalInput").ap() for name, value in arrays.items()}
    drams |= {name: nc.dram_tensor(name, shape, F32, kind="ExternalOutput").ap() for name, shape in returned.items()}
    encoder_step(nc, drams)
    got = run_bass_kernel_spmd(nc, [arrays], core_ids=[0]).results[0]

    y = got["yT"].reshape(D_MODEL, TOKENS).T
    k_a, k_b = got["k_a"].reshape(width, TOKENS).T, got["qk_b"][4].T
    v_a, v_b = got["v_all"][:, :width], got["v_all"][:, width:]
    last_a, last_b = slice(SEQ - 8 * CHUNK, SEQ), slice(SEQ - 2 * CHUNK, SEQ)
    heads = lambda t, rows: t[rows].reshape(1, 1, -1, t.shape[1] // HEAD, HEAD)
    conv_rows = lambda t: t.transpose(2, 1, 0).reshape(1, 1, 2, D_FF)
    sample = slice(SEQ, TOKENS)
    return tuple(np.ascontiguousarray(t) for t in (
        y[None, :SEQ], y[None, SEQ:],
        heads(k_a, last_a), heads(v_a, last_a), heads(k_b, last_b), heads(v_b, last_b),
        conv_rows(got["gate_prompt"]),
        heads(k_a, sample), heads(v_a, sample), heads(k_b, sample), heads(v_b, sample),
        conv_rows(got["gate_sample"])))
```

```python
from contextlib import ExitStack

import concourse.bass as bass
from concourse import mybir
from concourse.alu_op_type import AluOpType as ALU

F32 = mybir.dt.float32
F32R = mybir.dt.float32r
BF16 = mybir.dt.bfloat16
ACT = mybir.ActivationFunctionType
AX = mybir.AxisListType

P = 128
D_MODEL = 1024
SEQ = 2048
DEC = 64
PAST = 128
TOKENS = SEQ + DEC
CHUNK = 64
HEAD = 64
HEADS = 8
D_FF = 2816
EPS = 1e-6
NEG = -1e30
SCALE = HEAD ** -0.5
MAX_REL = 128
KD = D_MODEL // P
N_BLOCKS = 3
BLOCK = TOKENS // N_BLOCKS
KF = D_FF // P
SUBS = 2
SUB = BLOCK // SUBS
PASSES = ((0, 0), (0, 1), (1, 0))
ds = bass.ds


class Memory:

    def __init__(self, nc, ctx, stage):
        self.nc, self.ctx, self.stage, self.sems = nc, ctx, stage, []
        ctx.callback(self.clear)

    def clear(self):
        self.nc.clear_and_free_semaphores(self.sems)
        self.nc.all_engine_barrier()

    def sbuf(self, name, shape, dtype=F32):
        return self.ctx.enter_context(self.nc.sbuf_tensor(f"{self.stage}_{name}", shape, dtype))

    def psum(self, name, shape, dtype=F32):
        return self.ctx.enter_context(self.nc.psum_tensor(f"{self.stage}_{name}", shape, dtype))

    def sem(self, name):
        self.sems.append(self.nc.alloc_semaphore(f"{self.stage}_{name}"))
        return self.sems[-1]


def dense(nc, out, w_parts, act_parts, n_k, ready=None):
    for k in range(n_k):
        if ready:
            ready(k)
        for w, a in PASSES:
            last = nc.tensor.matmul(out, w_parts[w](k), act_parts[a](k),
                                    start=(k == 0 and (w, a) == PASSES[0]),
                                    stop=(k == n_k - 1 and (w, a) == PASSES[-1]))
    return last


def project(nc, xT, w_qk, w_rv, gains, rope_cos, rope_sin, swap, head_ones, all_ones, ident,
            rel, q_a, k_a, qk_b, v_all, rel_rows):
    QK_PAIRS, RV_PAIRS = 4, 5
    PAIRS = QK_PAIRS + RV_PAIRS
    VT = 88
    NV = SUB // VT
    with ExitStack() as ctx:
        m = Memory(nc, ctx, "project")
        x_raw = m.sbuf("x_raw", [P, KD, BLOCK])
        x_sq = m.sbuf("x_sq", [P, KD // SUBS, BLOCK])
        x_ssq = m.sbuf("x_ssq", [P, BLOCK])
        h = m.sbuf("h", [P, 2, BLOCK])
        h_hi = [m.sbuf(f"h_hi{i}", [P, KD, BLOCK], F32R) for i in range(2)]
        h_lo = [m.sbuf(f"h_lo{i}", [P, KD, BLOCK], F32R) for i in range(2)]
        n_r = m.sbuf("n_r", [P, SUBS, SUB])
        n_r2 = m.sbuf("n_r2", [P, SUBS, SUB])
        n_t = m.sbuf("n_t", [P, SUBS, SUB])
        n_c = m.sbuf("n_c", [P, SUBS, SUB])
        w_raw = [m.sbuf(f"w_raw{s}", [P, KD, P]) for s in range(2)]
        w_hi = [m.sbuf(f"w_hi{s}", [P, KD, P], F32R) for s in range(2)]
        w_lo = [m.sbuf(f"w_lo{s}", [P, KD, P], F32R) for s in range(2)]
        g_x = m.sbuf("g_x", [P, KD])
        g_q = m.sbuf("g_q", [P, 2])
        g_r = m.sbuf("g_r", [P, 2])
        g_in = m.sbuf("g_in", [P, KD + 4])
        eps = m.sbuf("eps", [P, 1])
        cos_sb = m.sbuf("cos", [P, BLOCK])
        sin_sb = m.sbuf("sin", [P, BLOCK])
        swap_sb = m.sbuf("swap", [P, P])
        head_ones_sb = m.sbuf("head_ones", [P, P])
        all_ones_sb = m.sbuf("all_ones", [P, P])
        ident_sb = m.sbuf("ident", [P, P])
        sq = [m.sbuf(f"sq{i}", [P, SUB]) for i in range(2)]
        ln = [m.sbuf(f"ln{i}", [P, SUB]) for i in range(2)]
        r0 = [m.sbuf(f"r0{i}", [P, SUB]) for i in range(2)]
        r2 = [m.sbuf(f"r2{i}", [P, SUB]) for i in range(2)]
        tmp = [m.sbuf(f"tmp{i}", [P, SUB]) for i in range(2)]
        corr = [m.sbuf(f"corr{i}", [P, SUB]) for i in range(2)]
        zg = [m.sbuf(f"zg{i}", [P, SUB]) for i in range(2)]
        zc = m.sbuf("zc", [P, SUB])
        zs = m.sbuf("zs", [P, SUB])
        zr = m.sbuf("zr", [P, SUB])
        out_t = [[m.sbuf(f"out{s}{i}", [P, SUB]) for i in range(2)] for s in range(2)]
        v_f = [m.sbuf(f"v_f{i}", [P, SUB]) for i in range(2)]
        v_t = [m.sbuf(f"v_t{i}", [VT, NV, P]) for i in range(2)]

        z = [[m.psum(f"z{s}{i}", [P, 512]) for i in range(2)] for s in range(2)]
        st = m.psum("stat", [P, SUBS, 512])
        rv_banks = m.psum("rv_banks", [P, 2, 512])
        rot = rv_banks[:, 0, 0:SUB]
        vtr = rv_banks[0:VT, 1, :].rearrange("p (c f) -> p c f", c=NV)

        x0_ld = [m.sem(f"x0_ld{k}") for k in range(KD)]
        const_ld, x_ld, cs_ld, rel_st = (m.sem(n) for n in ("const_ld", "x_ld", "cs_ld", "rel_st"))
        w_ld = [m.sem(f"w_ld{s}") for s in range(2)]
        w_hi_ok = [m.sem(f"w_hi_ok{s}") for s in range(2)]
        w_lo_ok = [m.sem(f"w_lo_ok{s}") for s in range(2)]
        z_ok = [[m.sem(f"z_ok{s}{i}") for i in range(2)] for s in range(2)]
        out_ok = [[m.sem(f"out_ok{s}{i}") for i in range(2)] for s in range(2)]
        stored = [[m.sem(f"stored{s}{i}") for i in range(2)] for s in range(2)]
        gains_ok, eps_ok = m.sem("gains_ok"), m.sem("eps_ok")
        x_sq_ok, x_part_ok, x_ms_ok = m.sem("x_sq_ok"), m.sem("x_part_ok"), m.sem("x_ms_ok")
        p_sq_ok, p_sum_ok, p_h_ok, p_hi_ok, p_lo_ok, p_g_ok = (
            m.sem(n) for n in ("p_sq_ok", "p_sum_ok", "p_h_ok", "p_hi_ok", "p_lo_ok", "p_g_ok"))
        x_ln_ok, x_r_ok, x_r2_ok, x_t_ok, x_c_ok = (m.sem(n) for n in ("x_ln_ok", "x_r_ok", "x_r2_ok", "x_t_ok", "x_c_ok"))
        h_ok, h_hi_ok, h_lo_ok = m.sem("h_ok"), m.sem("h_hi_ok"), m.sem("h_lo_ok")
        sq_ok, st_ok, ln_ok, r0_ok, r2_ok, corr_ok, zg_ok, rot_ok, rotated, vf_ok, vtr_ok = (
            [m.sem(f"{n}{i}") for i in range(2)] for n in
            ("sq_ok", "st_ok", "ln_ok", "r0_ok", "r2_ok", "corr_ok", "zg_ok", "rot_ok", "rotated", "vf_ok", "vtr_ok"))
        tmp_ok, zc_ok, zr_ok = m.sem("tmp_ok"), m.sem("zc_ok"), m.sem("zr_ok")

        NORMS = QK_PAIRS * 2 + RV_PAIRS
        LAST = N_BLOCKS - 1

        def loop(eng, b, count, body):
            if b == 0:
                body(0)
            with eng.Fori(1 if b == 0 else 0, count) as i:
                body(i)

        def rv_loop(eng, b, body):
            loop(eng, b, RV_PAIRS - 1, lambda i: body(i, 0, True))
            body(RV_PAIRS - 1, 1, b < LAST)

        def at(ap, i):
            return ap[i] if isinstance(i, int) else ap[ds(i, 1)].rearrange("a p n -> p (a n)")

        block = ctx.enter_context(nc.Block())

        @block.sync
        def _(sp):
            def load_x(b):
                t0 = b * BLOCK
                if b == 0:
                    for k in range(KD):
                        sp.dma_start(x_raw[:, k, :], xT[k, :, t0:t0 + BLOCK]).then_inc(x0_ld[k], 16)
                    return
                sp.wait_ge(h_ok if b == 1 else p_h_ok, KD * max(1, b - 1))
                sp.dma_start(x_raw[:], xT[:, :, t0:t0 + BLOCK].rearrange("k p n -> p k n")).then_inc(x_ld, 16)

            def load_pair(g, src):
                for s in range(2):
                    sp.wait_ge(w_lo_ok[s], g)
                    sp.dma_start(w_raw[s][:], src(s)).then_inc(w_ld[s], 16)

            def store(s, j, g, dst, src):
                sp.wait_ge(out_ok[s][j], g + 1)
                sp.dma_start(dst, src).then_inc(stored[s][j], 16)

            load_x(0)
            load_pair(0, lambda s: w_qk[0, s])
            load_x(1)
            sp.dma_start(rel_rows, bass.AP(rel.tensor, 0, [[0, P], [rel.shape[1], rel.shape[0]], [1, rel.shape[1]]]))\
                .then_inc(rel_st, 16)
            for b in range(N_BLOCKS):
                t0 = b * BLOCK
                halves = [slice(t0 + j * SUB, t0 + (j + 1) * SUB) for j in range(SUBS)]
                for j in range(SUBS):
                    if b:
                        sp.wait_ge(zr_ok, 2 * b * RV_PAIRS)
                sp.dma_start(cos_sb[:], rope_cos[:, t0:t0 + BLOCK]).then_inc(cs_ld, 16)
                sp.dma_start(sin_sb[:], rope_sin[:, t0:t0 + BLOCK]).then_inc(cs_ld, 16)

                def qk(i, g, nxt):
                    load_pair(g + 1, nxt)
                    for s, dst in ((0, q_a), (1, k_a)):
                        for j in range(SUBS):
                            store(s, j, g, at(dst[:, :, halves[j]], i), out_t[s][j][:])

                def next_of(w, i):
                    if isinstance(i, int):
                        return lambda s: w[i + 1, s]
                    return lambda s: w[ds(i + 1, 1), s].rearrange("a p k n -> p (a k) n")

                loop(sp, b, QK_PAIRS - 1, lambda i: qk(i, b * PAIRS + i, next_of(w_qk, i)))
                qk(QK_PAIRS - 1, b * PAIRS + QK_PAIRS - 1, lambda s: w_rv[0, s])

                def rv(i, g, nxt):
                    if nxt:
                        load_pair(g + 1, nxt)
                    for j in range(SUBS):
                        store(0, j, g, at(qk_b[:, :, halves[j]], i), out_t[0][j][:])
                    for j in range(SUBS):
                        store(1, j, g, v_all[halves[j], ds(i * P, P)].rearrange("(c p) f -> p c f", p=VT), v_t[j][:])

                loop(sp, b, RV_PAIRS - 1, lambda i: rv(i, b * PAIRS + QK_PAIRS + i, next_of(w_rv, i)))
                rv(RV_PAIRS - 1, b * PAIRS + PAIRS - 1, (lambda s: w_qk[0, s]) if b < LAST else None)
                if b + 2 < N_BLOCKS:
                    load_x(b + 2)
            sp.wait_ge(rel_st, 16)
            for s in range(2):
                for j in range(SUBS):
                    sp.wait_ge(stored[s][j], 16 * N_BLOCKS * PAIRS)

        @block.tensor
        def _(pe):
            def tile(s, j, b, g):
                if j == 0:
                    pe.wait_ge(w_lo_ok[s], g + 1)
                pe.wait_ge(out_ok[s][j], g)
                cols = slice(j * SUB, (j + 1) * SUB)
                hh, hl = h_hi[b % 2], h_lo[b % 2]
                ready = (lambda k: pe.wait_ge(h_lo_ok, k + 1)) if b == 0 and s == 0 and j == 0 else None
                dense(nc, z[s][j][:, 0:SUB], (lambda k: w_hi[s][:, k, :], lambda k: w_lo[s][:, k, :]),
                      (lambda k: hh[:, k, cols], lambda k: hl[:, k, cols]), KD, ready).then_inc(z_ok[s][j], 1)

            def stat(j, n):
                pe.wait_ge(sq_ok[j], n + 1)
                pe.wait_ge(corr_ok[j], n)
                nc.tensor.matmul(st[:, j, 0:SUB], head_ones_sb[:], sq[j][:], start=True, stop=True)\
                    .then_inc(st_ok[j], 1)

            def swapped(j, r):
                pe.wait_ge(zg_ok[j], r + 1)
                pe.wait_ge(rotated[1 - j], r + j)
                nc.tensor.matmul(rot, swap_sb[:], zg[j][:], start=True, stop=True).then_inc(rot_ok[j], 1)

            def values(j, r, g):
                pe.wait_ge(vf_ok[j], r + 1)
                pe.wait_ge(out_ok[1][1 - j], g + j)
                for c in range(NV):
                    last = nc.tensor.transpose(vtr[:, c, :], v_f[j][:, c * VT:(c + 1) * VT], ident_sb[:])
                last.then_inc(vtr_ok[j], 1)

            def x_stat(b):
                if b == 0:
                    for k in range(KD):
                        pe.wait_ge(x_sq_ok, k + 1)
                        for j in range(SUBS):
                            last = nc.tensor.matmul(rv_banks[:, j, 0:SUB], all_ones_sb[:],
                                                    x_sq[:, k % (KD // SUBS), j * SUB:(j + 1) * SUB],
                                                    start=k == 0, stop=k == KD - 1)
                        if k < KD - 1:
                            last.then_inc(x_part_ok, 1)
                else:
                    pe.wait_ge(p_sum_ok, (KD - 1) * b)
                    for j in range(SUBS):
                        last = nc.tensor.matmul(rv_banks[:, j, 0:SUB], all_ones_sb[:],
                                                x_ssq[:, j * SUB:(j + 1) * SUB], start=True, stop=True)
                last.then_inc(x_ms_ok, 1)

            pe.wait_ge(const_ld, 5 * 16)
            x_stat(0)
            for b in range(N_BLOCKS):
                if b:
                    pe.wait_ge(p_lo_ok, KD * b)

                def qk(i):
                    g, n = b * PAIRS + i, b * NORMS + 2 * i
                    tile(0, 0, b, g)
                    tile(0, 1, b, g)
                    stat(0, n)
                    tile(1, 0, b, g)
                    stat(1, n)
                    tile(1, 1, b, g)
                    stat(0, n + 1)
                    stat(1, n + 1)

                loop(pe, b, QK_PAIRS, qk)
                if b < LAST:
                    for j in range(SUBS):
                        pe.wait_ge(rotated[j], b * RV_PAIRS)
                        pe.wait_ge(out_ok[1][j], b * PAIRS)
                    x_stat(b + 1)

                def rv(i, first=False):
                    g, n, r = b * PAIRS + QK_PAIRS + i, b * NORMS + 2 * QK_PAIRS + i, b * RV_PAIRS + i
                    tile(0, 0, b, g)
                    if not first:
                        values(1, r - 1, g - 1)
                    tile(0, 1, b, g)
                    stat(0, n)
                    if b < LAST:
                        pe.wait_ge(x_c_ok, b + 2)
                    swapped(0, r)
                    tile(1, 0, b, g)
                    stat(1, n)
                    swapped(1, r)
                    tile(1, 1, b, g)
                    values(0, r, g)

                rv(0, True)
                with pe.Fori(1, RV_PAIRS) as i:
                    rv(i)
                values(1, (b + 1) * RV_PAIRS - 1, (b + 1) * PAIRS - 1)

        @block.scalar
        def _(act):
            nc.scalar.preload_act_table_set("natural_log_exp_and_others")

            def split_hi(s, g):
                act.wait_ge(w_ld[s], 16 * (g + 1))
                act.wait_ge(z_ok[s][1], g)
                nc.scalar.activation(w_hi[s][:], w_raw[s][:], ACT.Copy).then_inc(w_hi_ok[s], 1)

            def square(s, j, g, n):
                act.wait_ge(z_ok[s][j], g + 1)
                act.wait_ge(st_ok[j], n)
                nc.scalar.activation(sq[j][:], z[s][j][:, 0:SUB], ACT.Square).then_inc(sq_ok[j], 1)

            def root(j, n):
                act.wait_ge(st_ok[j], n + 1)
                act.wait_ge(corr_ok[j], n)
                nc.scalar.activation(ln[j][:], st[:, j, 0:SUB], ACT.Ln, bias=eps[:, 0:1]).then_inc(ln_ok[j], 1)
                act.wait_ge(ln_ok[j], n + 1)
                nc.scalar.activation(r0[j][:], ln[j][:], ACT.Exp, scale=-0.5).then_inc(r0_ok[j], 1)
                act.wait_ge(r0_ok[j], n + 1)
                nc.scalar.activation(r2[j][:], r0[j][:], ACT.Square).then_inc(r2_ok[j], 1)

            def x_square():
                for k in range(KD):
                    act.wait_ge(x0_ld[k], 16)
                    if k >= KD // SUBS:
                        act.wait_ge(x_part_ok, k - KD // SUBS + 1)
                    nc.scalar.activation(x_sq[:, k % (KD // SUBS), :], x_raw[:, k, :], ACT.Square).then_inc(x_sq_ok, 1)

            def x_root(b):
                act.wait_ge(x_ms_ok, b + 1)
                if b:
                    act.wait_ge(x_c_ok, b)
                nc.scalar.activation(n_t[:], rv_banks[:, :, 0:SUB], ACT.Ln, bias=eps[:, 0:1]).then_inc(x_ln_ok, 1)
                act.wait_ge(x_ln_ok, b + 1)
                nc.scalar.activation(n_r[:], n_t[:], ACT.Exp, scale=-0.5).then_inc(x_r_ok, 1)
                act.wait_ge(x_r_ok, b + 1)
                nc.scalar.activation(n_r2[:], n_r[:], ACT.Square).then_inc(x_r2_ok, 1)

            def h_split():
                for k in range(KD):
                    act.wait_ge(h_ok, k + 1)
                    nc.scalar.activation(h_hi[0][:, k, :], h[:, k % 2, :], ACT.Copy).then_inc(h_hi_ok, 1)

            nc.scalar.dma_start(g_in[:], gains).then_inc(const_ld, 16)
            nc.scalar.dma_start(all_ones_sb[:], all_ones).then_inc(const_ld, 16)
            nc.scalar.dma_start(head_ones_sb[:], head_ones).then_inc(const_ld, 16)
            nc.scalar.dma_start(swap_sb[:], swap).then_inc(const_ld, 16)
            nc.scalar.dma_start(ident_sb[:], ident).then_inc(const_ld, 16)
            act.wait_ge(eps_ok, 1)
            x_square()
            for s in range(2):
                act.wait_ge(w_ld[s], 16)
                nc.scalar.activation(w_hi[s][:], w_raw[s][:], ACT.Copy).then_inc(w_hi_ok[s], 1)
            x_root(0)
            h_split()
            for b in range(N_BLOCKS):
                def qk(i):
                    g, n = b * PAIRS + i, b * NORMS + 2 * i
                    square(0, 0, g, n)
                    square(0, 1, g, n)
                    root(0, n)
                    split_hi(0, g + 1)
                    square(1, 0, g, n + 1)
                    root(1, n)
                    square(1, 1, g, n + 1)
                    root(0, n + 1)
                    split_hi(1, g + 1)
                    root(1, n + 1)

                loop(nc.scalar, b, QK_PAIRS, qk)
                if b < LAST:
                    x_root(b + 1)

                def rv(i, gain, prefetch):
                    g, n, r = b * PAIRS + QK_PAIRS + i, b * NORMS + 2 * QK_PAIRS + i, b * RV_PAIRS + i
                    for j in range(SUBS):
                        square(0, j, g, n)
                        act.wait_ge(rotated[j], r)
                        nc.scalar.activation(zg[j][:], z[0][j][:, 0:SUB], ACT.Copy, scale=g_r[:, gain:gain + 1])\
                            .then_inc(zg_ok[j], 1)
                    root(0, n)
                    if prefetch:
                        split_hi(0, g + 1)
                    for j in range(SUBS):
                        act.wait_ge(z_ok[1][j], g + 1)
                        act.wait_ge(vtr_ok[j], r)
                        nc.scalar.activation(v_f[j][:], z[1][j][:, 0:SUB], ACT.Copy).then_inc(vf_ok[j], 1)
                        if j == 0:
                            root(1, n)
                    if prefetch:
                        split_hi(1, g + 1)

                rv_loop(nc.scalar, b, rv)

        @block.vector
        def _(dve):
            def split_lo(s, g):
                dve.wait_ge(w_hi_ok[s], g + 1)
                nc.vector.tensor_tensor(w_lo[s][:], w_raw[s][:], w_hi[s][:].bitcast(F32), ALU.subtract)\
                    .then_inc(w_lo_ok[s], 1)

            def correction(j, n, m_, before, count):
                dve.wait_ge(r2_ok[j], n + 1)
                nc.vector.scalar_tensor_tensor(tmp[j][:], st[:, j, 0:SUB], eps[:, 0:1], r2[j][:], ALU.add, ALU.mult)\
                    .then_inc(tmp_ok, 1)
                dve.wait_ge(before[j], count)
                dve.wait_ge(tmp_ok, m_ + 1)
                nc.vector.scalar_tensor_tensor(corr[j][:], tmp[j][:], 3.0, r0[j][:], ALU.subtract, ALU.mult)\
                    .then_inc(corr_ok[j], 1)

            def norm(s, j, g, n, m_):
                correction(j, n, m_, out_ok[1 - s], g + s)
                dve.wait_ge(stored[s][j], 16 * g)
                dve.wait_ge(corr_ok[j], n + 1)
                nc.vector.scalar_tensor_tensor(out_t[s][j][:], z[s][j][:, 0:SUB], g_q[:, s:s + 1], corr[j][:],
                                               ALU.mult, ALU.mult).then_inc(out_ok[s][j], 1)

            def norm_rotary(j, g, n, m_, r):
                cols = slice(j * SUB, (j + 1) * SUB)
                correction(j, n, m_, out_ok[1], g)
                dve.wait_ge(zr_ok, 2 * r + j)
                dve.wait_ge(zg_ok[j], r + 1)
                nc.vector.tensor_tensor(zc[:], zg[j][:], cos_sb[:, cols], ALU.mult).then_inc(zc_ok, 1)
                dve.wait_ge(rot_ok[j], r + 1)
                nc.vector.tensor_tensor(zs[:], rot, sin_sb[:, cols], ALU.mult).then_inc(rotated[j], 1)
                dve.wait_ge(zc_ok, 2 * r + j + 1)
                dve.wait_ge(rotated[j], r + 1)
                dve.wait_ge(out_ok[0][1 - j], g + j)
                nc.vector.tensor_tensor(zr[:], zc[:], zs[:], ALU.add).then_inc(zr_ok, 1)
                dve.wait_ge(stored[0][j], 16 * g)
                dve.wait_ge(corr_ok[j], n + 1)
                dve.wait_ge(zr_ok, 2 * r + j + 1)
                nc.vector.scalar_tensor_tensor(out_t[0][j][:], zr[:], -0.5, corr[j][:], ALU.mult, ALU.mult)\
                    .then_inc(out_ok[0][j], 1)

            def value(j, g, r):
                dve.wait_ge(vtr_ok[j], r + 1)
                dve.wait_ge(stored[1][j], 16 * g)
                nc.vector.tensor_copy(v_t[j][:], vtr).then_inc(out_ok[1][j], 1)

            def x_correction(b):
                dve.wait_ge(x_r2_ok, b + 1)
                nc.vector.scalar_tensor_tensor(n_t[:], rv_banks[:, :, 0:SUB], eps[:, 0:1], n_r2[:], ALU.add, ALU.mult)\
                    .then_inc(x_t_ok, 1)
                dve.wait_ge(x_t_ok, b + 1)
                if b > 1:
                    dve.wait_ge(p_h_ok, KD * (b - 1))
                nc.vector.scalar_tensor_tensor(n_c[:], n_t[:], 3.0, n_r[:], ALU.subtract, ALU.mult)\
                    .then_inc(x_c_ok, 1)

            def h_make():
                x_correction(0)
                dve.wait_ge(x_c_ok, 1)
                c = n_c[:].rearrange("p a n -> p (a n)")

                def low(k):
                    dve.wait_ge(h_hi_ok, k + 1)
                    nc.vector.tensor_tensor(h_lo[0][:, k, :], h[:, k % 2, :],
                                            h_hi[0][:, k, :].bitcast(F32), ALU.subtract).then_inc(h_lo_ok, 1)

                for k in range(KD):
                    if k > 1:
                        dve.wait_ge(h_lo_ok, k - 1)
                    nc.vector.scalar_tensor_tensor(h[:, k % 2, :], x_raw[:, k, :], g_x[:, k:k + 1], c,
                                                   ALU.mult, ALU.mult).then_inc(h_ok, 1)
                    if k:
                        low(k - 1)
                low(KD - 1)

            nc.vector.memset(eps[:], EPS).then_inc(eps_ok, 1)
            dve.wait_ge(const_ld, 5 * 16)
            for out, src, by in ((g_x[:], g_in[:, 0:KD], -0.5), (g_q[:, 0:1], g_in[:, KD:KD + 1], -0.5 * SCALE),
                                 (g_q[:, 1:2], g_in[:, KD + 1:KD + 2], -0.5),
                                 (g_r[:, 0:1], g_in[:, KD + 2:KD + 3], SCALE),
                                 (g_r[:, 1:2], g_in[:, KD + 3:KD + 4], 1.0)):
                nc.vector.tensor_scalar(out, src, by, None, ALU.mult).then_inc(gains_ok, 1)
            dve.wait_ge(gains_ok, 5)
            dve.wait_ge(eps_ok, 1)
            for s in range(2):
                split_lo(s, 0)
            h_make()
            for b in range(N_BLOCKS):
                m0 = 2 * b * NORMS

                def qk(i):
                    g, n, m_ = b * PAIRS + i, b * NORMS + 2 * i, m0 + 4 * i
                    norm(0, 0, g, n, m_)
                    split_lo(0, g + 1)
                    norm(0, 1, g, n, m_ + 1)
                    norm(1, 0, g, n + 1, m_ + 2)
                    split_lo(1, g + 1)
                    norm(1, 1, g, n + 1, m_ + 3)

                loop(nc.vector, b, QK_PAIRS, qk)
                if b < LAST:
                    x_correction(b + 1)
                dve.wait_ge(cs_ld, 32 * (b + 1))

                def rv(i, gain, prefetch):
                    g, n, r = b * PAIRS + QK_PAIRS + i, b * NORMS + 2 * QK_PAIRS + i, b * RV_PAIRS + i
                    m_ = m0 + 4 * QK_PAIRS + 2 * i
                    norm_rotary(0, g, n, m_, r)
                    if prefetch:
                        split_lo(0, g + 1)
                    norm_rotary(1, g, n, m_ + 1, r)
                    value(0, g, r)
                    if prefetch:
                        split_lo(1, g + 1)
                    value(1, g, r)

                rv_loop(nc.vector, b, rv)

        @block.gpsimd
        def _(pool):
            for b in range(1, N_BLOCKS):
                done, out = KD * (b - 1), b % 2
                pool.wait_ge(x_ld, 16 * b)
                if b == 1:
                    pool.wait_ge(x_part_ok, KD - 1)
                    pool.wait_ge(x_ms_ok, 1)
                else:
                    pool.wait_ge(x_ms_ok, b)
                for k in range(KD):
                    if k > 1:
                        pool.wait_ge(p_sum_ok, (KD - 1) * (b - 1) + k - 1)
                    square = x_ssq if k == 0 else x_sq[:, k % 2, :]
                    nc.gpsimd.tensor_tensor(square[:] if k == 0 else square, x_raw[:, k, :], x_raw[:, k, :], ALU.mult)\
                        .then_inc(p_sq_ok, 1)
                    if k:
                        pool.wait_ge(p_sq_ok, done + k + 1)
                        nc.gpsimd.tensor_tensor(x_ssq[:], x_ssq[:], x_sq[:, k % 2, :], ALU.add).then_inc(p_sum_ok, 1)
                pool.wait_ge(x_c_ok, b + 1)
                c = n_c[:].rearrange("p a n -> p (a n)")
                for k in range(KD):
                    if k:
                        pool.wait_ge(p_lo_ok, done + k)
                    else:
                        pool.wait_ge(p_sum_ok, (KD - 1) * b)
                    nc.gpsimd.tensor_scalar(x_sq[:, 0, :], x_raw[:, k, :], g_x[:, k:k + 1], None, ALU.mult)\
                        .then_inc(p_g_ok, 1)
                    pool.wait_ge(p_g_ok, done + k + 1)
                    nc.gpsimd.tensor_tensor(h[:, 0, :], x_sq[:, 0, :], c, ALU.mult).then_inc(p_h_ok, 1)
                    pool.wait_ge(p_h_ok, done + k + 1)
                    nc.gpsimd.tensor_scalar(h_hi[out][:, k, :], h[:, 0, :], 1.0, None, ALU.mult).then_inc(p_hi_ok, 1)
                    pool.wait_ge(p_hi_ok, done + k + 1)
                    nc.gpsimd.tensor_tensor(h_lo[out][:, k, :], h[:, 0, :], h_hi[out][:, k, :].bitcast(F32),
                                            ALU.subtract).then_inc(p_lo_ok, 1)



def attend(nc, q_a, k_a, qk_b, v_all, ka_cache, kb_cache, va_cache, vb_cache, rel_rows, sinks, ident, oT):
    TILES = SEQ // P
    UNITS, A_UNITS = 12, HEADS
    FULL = 5
    NEAR = 2 * P
    HALF = FULL * P // 2
    LOOP = FULL + 1
    KEYS = SEQ + 2 * P
    KV_A, KV_B = HEADS, 2
    NKEY = KV_A + KV_B
    PAIRS_A, PAIRS_B = 4, 4
    V_FEATURES = PAIRS_A * P + P
    CLEARED = 10
    with ExitStack() as ctx:
        m = Memory(nc, ctx, "attend")
        keys = m.sbuf("keys", [P, NKEY, KEYS], F32R)
        v = m.sbuf("v", [P, TILES + 2, V_FEATURES])
        raw = m.sbuf("raw", [P, HEADS + NKEY, P])
        raw_b = m.sbuf("raw_b", [P, HEADS, P])
        raw_cache = m.sbuf("raw_cache", [P, NKEY, P])
        q_hi = m.sbuf("q_hi", [P, 2 * HEADS, P], F32R)
        q_lo = m.sbuf("q_lo", [P, 2 * HEADS, P], F32R)
        bias = m.sbuf("bias", [P, HEADS, NEAR])
        far = m.sbuf("far", [P, HEADS, 2])
        sink = m.sbuf("sink", [1, HEADS])
        ones = m.sbuf("ones", [1, P])
        mask_q = m.sbuf("mask_q", [P, P], BF16)
        mask_k = m.sbuf("mask_k", [P, NEAR], BF16)
        ident_sb = m.sbuf("ident", [P, P])
        prob = [m.sbuf(f"prob{i}", [P, FULL * P]) for i in range(2)]
        prob_t = [m.sbuf(f"prob_t{i}", [P, FULL * P]) for i in range(2)]
        nmax = [m.sbuf(f"nmax{i}", [P, 2]) for i in range(2)]
        den = [m.sbuf(f"den{i}", [P, 2]) for i in range(4)]
        rden = m.sbuf("rden", [P, 2])
        o = m.sbuf("o", [P, 2 * HEADS, HEAD])
        o_t = [m.sbuf(f"o_t{i}", [P, KD // 2, P]) for i in range(2)]
        s_ps = [m.psum(f"s{i}", [P, 2, 512]) for i in range(2)]
        t_ps = m.psum("t", [P, 1024])
        ot_ps = t_ps[:, 512:1024]
        o_ps = [m.psum(f"o{i}", [P, 512]) for i in range(2)]

        ld, ld_b, const_ld, cache_ld = m.sem("ld"), m.sem("ld_b"), m.sem("const_ld"), m.sem("cache_ld")
        zero_ok, bias_sub, bias_set, k0_hi, k0_ok = (
            m.sem(n) for n in ("zero_ok", "bias_sub", "bias_set", "k0_hi", "k0_ok"))
        hi_ok, hi_b_ok, lo_ok, lo_b_ok = (m.sem(n) for n in ("hi_ok", "hi_b_ok", "lo_ok", "lo_b_ok"))
        s_ok, biased, max_ok, exp_ok, t_ok, t_act, t_dve, pv_ok, rden_ok, o_ok = (
            m.sem(n) for n in ("s_ok", "biased", "max_ok", "exp_ok", "t_ok", "t_act", "t_dve", "pv_ok", "rden_ok", "o_ok"))
        ot_ok, ot_out, o_st = ([m.sem(f"{n}_{x}") for x in "ab"] for n in ("ot_ok", "ot_out", "o_st"))

        def window(n, mixer):
            if isinstance(n, int) and n == 0:
                return SEQ, 2 * P
            w = FULL if mixer == "a" else 2
            if isinstance(n, int):
                w = min(n, w)
            return (n - w) * P, w * P

        def first_tile(n, mixer):
            return TILES if isinstance(n, int) and n == 0 else n - window(n, mixer)[1] // P

        def before(n, u, by=1):
            return (n, u - by) if u >= by else (n - 1, u + UNITS - by)

        def is_whole(n, u):
            return u < A_UNITS and window(n, "a")[1] == FULL * P

        def whole_before(n, u):
            return 0 if isinstance(n, int) and n < FULL else A_UNITS * (n - FULL) + min(u, A_UNITS)

        def scores_of(n, u):
            ps, sb = s_ps[u % 2], prob[u % 2]
            halves = sb[:].rearrange("p (a n) -> p a n", a=2)
            if is_whole(n, u):
                return ps[:, :, 0:HALF], halves
            w = window(n, "a" if u < A_UNITS else "b")[1]
            if u < A_UNITS:
                return ps[:, 0, 0:w], sb[:, 0:w]
            return ps[:, :, 0:w + 1], halves[:, :, 0:w + 1]

        def prob_blocks(n, u):
            if u < A_UNITS:
                return [j * P for j in range(window(n, "a")[1] // P)]
            return [i * HALF + j * P for i in range(2) for j in range(window(n, "b")[1] // P)]

        def run(eng, step, last):
            for n in range(LOOP):
                for u in range(UNITS):
                    step(n, u)
            with eng.Fori(LOOP, TILES + 1) as n:
                for u in range(UNITS):
                    step(n, u)
            last()

        block = ctx.enter_context(nc.Block())

        @block.sync
        def _(sp):
            by_heads = "f (a p) n -> p (f a) n"

            def twice(dst, src, sem):
                for i in range(2):
                    sp.dma_start(dst[i * HEAD:(i + 1) * HEAD], src).then_inc(sem, 16)

            def load(n):
                c, w = (SEQ, DEC) if isinstance(n, int) and n == 0 else ((n - 1) * P, P)
                tile = TILES + 1 if isinstance(n, int) and n == 0 else n - 1
                twice(raw[:, 0:HEADS, 0:w], q_a[:, :, ds(c, w)].rearrange(by_heads, p=HEAD), ld)
                twice(raw[:, HEADS:HEADS + KV_A, 0:w], k_a[:, :, ds(c, w)].rearrange(by_heads, p=HEAD), ld)
                twice(raw[:, HEADS + KV_A:, 0:w], qk_b[PAIRS_B:, :, ds(c, w)].rearrange(by_heads, p=HEAD), ld)
                sp.dma_start(v[0:w, ds(tile, 1), :].rearrange("p a f -> p (a f)"), v_all[ds(c, w), :]).then_inc(ld, 16)

            def load_b(n):
                c, w = (SEQ, DEC) if isinstance(n, int) and n == 0 else ((n - 1) * P, P)
                twice(raw_b[:, :, 0:w], qk_b[0:PAIRS_B, :, ds(c, w)].rearrange(by_heads, p=HEAD), ld_b)

            def store(n, mixer):
                c, w = (SEQ, DEC) if isinstance(n, int) and n == 0 else ((n - 1) * P, P)
                sp.wait_ge(ot_out[mixer], n + 1)
                half = slice(mixer * KD // 2, (mixer + 1) * KD // 2)
                sp.dma_start(oT[half, :, ds(c, w)].rearrange("k p n -> p k n"), o_t[mixer][:, :, 0:w])\
                    .then_inc(o_st[mixer], 16)

            load(0)
            twice(raw_cache[:, 0:KV_A, :], ka_cache.rearrange(by_heads, p=HEAD), cache_ld)
            twice(raw_cache[:, KV_A:, :], kb_cache.rearrange("(a p) n -> p a n", p=HEAD), cache_ld)
            load_b(0)
            for n in range(LOOP - 1):
                sp.wait_ge(lo_ok, 2 * (n + 1))
                load(n + 1)
                if n:
                    store(n - 1, 1)
                sp.wait_ge(lo_b_ok, n + 1)
                load_b(n + 1)
                store(n, 0)
            with sp.Fori(LOOP - 1, TILES) as n:
                sp.wait_ge(lo_ok, 2 * (n + 1))
                load(n + 1)
                store(n - 1, 1)
                sp.wait_ge(lo_b_ok, n + 1)
                load_b(n + 1)
                store(n, 0)
            store(TILES - 1, 1)
            store(TILES, 0)
            store(TILES, 1)
            for mixer in range(2):
                sp.wait_ge(o_st[mixer], 16 * (TILES + 1))

        @block.gpsimd
        def _(pool):
            for done, (out, value) in enumerate((
                    (raw[:, :, DEC:], 0.0), (raw_b[:, :, DEC:], 0.0), (ones[:], 1.0), (mask_q[:], 0.0), (mask_k[:], 0.0),
                    (mask_q[0:1, CHUNK:], 1.0), (mask_q[32:33, 0:CHUNK], 1.0),
                    (mask_k[0:1, 0:CHUNK], NEG), (mask_k[32:33, NEAR - CHUNK:], NEG), (v[DEC:, TILES + 1, :], 0.0))):
                if done:
                    pool.wait_ge(zero_ok, done)
                nc.gpsimd.memset(out, value).then_inc(zero_ok, 1)
            low = slice(HEAD, P)

            pool.wait_ge(zero_ok, CLEARED)

            def split(n):
                if not isinstance(n, int) or n:
                    pool.wait_ge(lo_b_ok, n)
                pool.wait_ge(hi_ok, 2 * n + 1)
                nc.gpsimd.tensor_tensor(q_lo[:, 0:HEADS, :], raw[:, 0:HEADS, :], q_hi[:, 0:HEADS, :].bitcast(F32),
                                        ALU.subtract).then_inc(lo_ok, 1)
                pool.wait_ge(lo_ok, 2 * n + 1)
                pool.wait_ge(hi_ok, 2 * n + 2)
                c = SEQ + P if isinstance(n, int) and n == 0 else (n - 1) * P
                nc.gpsimd.tensor_tensor(keys[low, :, ds(c, P)], raw[low, HEADS:, :], keys[low, :, ds(c, P)].bitcast(F32),
                                        ALU.subtract).then_inc(lo_ok, 1)

            def split_b(n):
                pool.wait_ge(lo_ok, 2 * n + 2)
                pool.wait_ge(hi_b_ok, n + 1)
                nc.gpsimd.tensor_tensor(q_lo[:, HEADS:, :], raw_b[:], q_hi[:, HEADS:, :].bitcast(F32), ALU.subtract)\
                    .then_inc(lo_b_ok, 1)

            split(0)
            split_b(0)
            for n in range(1, LOOP):
                split(n)
                split_b(n)
            with nc.gpsimd.Fori(LOOP, TILES + 1) as n:
                split(n)
                split_b(n)

        @block.tensor
        def _(pe):
            def scores(n, u):
                if u == 0:
                    pe.wait_ge(lo_ok, 2 * (n + 1))
                if u == A_UNITS:
                    pe.wait_ge(lo_b_ok, n + 1)
                k = UNITS * n + u
                if not isinstance(n, int) or k > 1:
                    pe.wait_ge(exp_ok, k - 1)
                ps = s_ps[u % 2]
                c, w = window(n, "a" if u < A_UNITS else "b")
                if is_whole(n, u):
                    parts = [(0, u, u, 0, HALF), (1, u, u, HALF, HALF)]
                elif u < A_UNITS:
                    parts = [(0, u, u, 0, w)]
                else:
                    parts = [(i, 2 * u - A_UNITS + i, KV_A + i, 0, w) for i in range(2)]
                for bank, query, key, first, width in parts:
                    begun = False
                    if u >= A_UNITS:
                        head = 2 * (u - A_UNITS) + bank
                        nc.tensor.matmul(ps[:, bank, w:w + 1], ones[:], sink[:, head:head + 1], start=True, stop=False,
                                         skip_group_check=True)
                        nc.tensor.matmul(ps[:, bank, 0:w], mask_q[:], mask_k[:, NEAR - w:], start=False, stop=False,
                                         skip_group_check=True)
                        begun = True
                    elif is_whole(n, u) and bank == 0:
                        nc.tensor.matmul(ps[:, 0, 0:CHUNK], mask_q[:], mask_k[:, 0:CHUNK], start=True, stop=False,
                                         skip_group_check=True)
                        begun = True
                    for q in (q_hi, q_lo):
                        last = nc.tensor.matmul(ps[:, bank, 0:width], q[:, query, :], keys[:, key, ds(c + first, width)],
                                                start=q is q_hi and not begun, stop=q is q_lo, skip_group_check=begun)
                last.then_inc(s_ok, 1)

            def transposes(n, u):
                k = UNITS * n + u
                pe.wait_ge(exp_ok, k + 1)
                if not isinstance(n, int) or k:
                    pe.wait_ge(t_act, k)
                for j, first in enumerate(prob_blocks(n, u)):
                    if j == FULL - 1:
                        if u == 0:
                            pe.wait_ge(ot_out[0], n)
                        elif u == 3:
                            pe.wait_ge(ot_out[1], n)
                        else:
                            pe.wait_ge(t_dve, whole_before(n, u))
                    last = nc.tensor.transpose(t_ps[:, j * P:(j + 1) * P], prob[u % 2][:, first:first + P], ident_sb[:])
                last.then_inc(t_ok, 1)

            def values(n, u):
                k = UNITS * n + u
                pe.wait_ge(t_act, k + 1)
                if is_whole(n, u):
                    pe.wait_ge(t_dve, whole_before(n, u) + 1)
                if not isinstance(n, int) or k > 1:
                    pe.wait_ge(o_ok, k - 1)
                mixer = "a" if u < A_UNITS else "b"
                tile, w = first_tile(n, mixer), window(n, mixer)[1] // P
                pair = u // 2 if u < A_UNITS else PAIRS_A
                for head in range(1 if u < A_UNITS else 2):
                    for j in range(w):
                        src = (head * w + j) * P
                        last = nc.tensor.matmul(
                            o_ps[u % 2][:, head * P:(head + 1) * P], prob_t[u % 2][:, src:src + P],
                            v[:, ds(tile + j, 1), pair * P:(pair + 1) * P].rearrange("p a f -> p (a f)"),
                            start=(j == 0), stop=(j == w - 1))
                last.then_inc(pv_ok, 1)

            def output(n, mixer):
                if mixer:
                    pe.wait_ge(o_ok, UNITS * (n + 1))
                    if isinstance(n, int) and n == TILES:
                        pe.wait_ge(ot_out[0], n + 1)
                    elif isinstance(n, int) and n + 1 < FULL:
                        pe.wait_ge(ot_out[0], n + 1)
                    else:
                        pe.wait_ge(t_dve, whole_before(n + 1, 3))
                else:
                    pe.wait_ge(o_ok, UNITS * n + A_UNITS)
                    if not isinstance(n, int) or n >= FULL:
                        pe.wait_ge(t_dve, whole_before(n, A_UNITS))
                    elif n:
                        pe.wait_ge(ot_out[1], n)
                for k in range(KD // 2):
                    heads = slice(HEADS * mixer + 2 * k, HEADS * mixer + 2 * k + 2)
                    last = nc.tensor.transpose(ot_ps[:, k * P:(k + 1) * P],
                                               o[:, heads, :].rearrange("p a f -> p (a f)"), ident_sb[:])
                last.then_inc(ot_ok[mixer], 1)

            def step(n, u):
                first = isinstance(n, int) and n == 0
                scores(n, u)
                if u == 4 and not first:
                    output(n - 1, 1)
                if not (first and u < 3):
                    values(*before(n, u, 3))
                if not (first and u < 1):
                    transposes(*before(n, u))
                if u == 11:
                    output(n, 0)

            def last():
                values(TILES, UNITS - 3)
                transposes(TILES, UNITS - 1)
                values(TILES, UNITS - 2)
                values(TILES, UNITS - 1)
                output(TILES, 1)

            pe.wait_ge(const_ld, 6 * 16)
            pe.wait_ge(zero_ok, CLEARED)
            pe.wait_ge(k0_ok, 1)
            run(pe, step, last)

        @block.scalar
        def _(act):
            nc.scalar.preload_act_table_set("natural_log_exp_and_others")

            def split(n):
                act.wait_ge(ld, 7 * 16 * (n + 1))
                if not isinstance(n, int) or n:
                    act.wait_ge(s_ok, UNITS * (n - 1) + A_UNITS)
                nc.scalar.activation(q_hi[:, 0:HEADS, :], raw[:, 0:HEADS, :], ACT.Copy).then_inc(hi_ok, 1)
                c = SEQ + P if isinstance(n, int) and n == 0 else (n - 1) * P
                nc.scalar.activation(keys[:, :, ds(c, P)], raw[:, HEADS:, :], ACT.Copy).then_inc(hi_ok, 1)

            def split_b(n):
                act.wait_ge(ld_b, 2 * 16 * (n + 1))
                if not isinstance(n, int) or n:
                    act.wait_ge(s_ok, UNITS * n)
                nc.scalar.activation(q_hi[:, HEADS:, :], raw_b[:], ACT.Copy).then_inc(hi_b_ok, 1)

            def exps(n, u):
                k = UNITS * n + u
                ps, sb = scores_of(n, u)
                if not isinstance(n, int) or k > 1:
                    act.wait_ge(t_ok, k - 1)
                if not isinstance(n, int) or k > 3:
                    act.wait_ge(o_ok, k - 3)
                act.wait_ge(max_ok, k + 1)
                if u < A_UNITS:
                    nc.scalar.activation(sb, ps, ACT.Exp, bias=nmax[u % 2][:, 0:1], accum_out=den[u % 4][:, 0:1])\
                        .then_inc(exp_ok, 1)
                else:
                    for i in range(2):
                        last = nc.scalar.activation(sb[:, i, :], ps[:, i, :], ACT.Exp, bias=nmax[u % 2][:, i:i + 1],
                                                    accum_out=den[u % 4][:, i:i + 1])
                    last.then_inc(exp_ok, 1)

            def copy_t(n, u):
                k = UNITS * n + u
                if not isinstance(n, int) or k > 1:
                    act.wait_ge(pv_ok, k - 1)
                act.wait_ge(t_ok, k + 1)
                w = min(512, P * len(prob_blocks(n, u)))
                nc.scalar.activation(prob_t[u % 2][:, 0:w], t_ps[:, 0:w], ACT.Copy).then_inc(t_act, 1)

            def step(n, u):
                first = isinstance(n, int) and n == 0
                if not (first and u < 1):
                    copy_t(*before(n, u))
                exps(n, u)
                if u == 3:
                    split_b(n)
                if u == 8 and not (isinstance(n, int) and n == TILES):
                    split(n + 1)

            nc.scalar.dma_start(ident_sb[:], ident).then_inc(const_ld, 16)
            row = rel_rows.shape[1] * rel_rows.shape[2]
            nc.scalar.dma_start(bias[:], bass.AP(rel_rows.tensor, P - 1, [[row - 1, P], [rel_rows.shape[2], HEADS], [1, NEAR]]))\
                .then_inc(const_ld, 16)
            nc.scalar.dma_start(far[:], rel_rows[:, :, 0:2]).then_inc(const_ld, 16)
            nc.scalar.dma_start(sink[:], sinks.rearrange("(a n) -> a n", a=1)).then_inc(const_ld, 16)
            nc.scalar.dma_start(v[:, TILES, 0:PAIRS_A * P], va_cache).then_inc(const_ld, 16)
            nc.scalar.dma_start(v[:, TILES, PAIRS_A * P:], vb_cache).then_inc(const_ld, 16)
            act.wait_ge(zero_ok, 2)
            split(0)
            act.wait_ge(cache_ld, 64)
            nc.scalar.activation(keys[:, :, SEQ:SEQ + P], raw_cache[:], ACT.Copy).then_inc(k0_hi, 1)
            for n in range(LOOP):
                for u in range(UNITS):
                    step(n, u)
            with nc.scalar.Fori(LOOP, TILES) as n:
                for u in range(UNITS):
                    step(n, u)
            for u in range(UNITS):
                step(TILES, u)
            copy_t(TILES, UNITS - 1)

        @block.vector
        def _(dve):
            def maxima(n, u):
                k = UNITS * n + u
                dve.wait_ge(s_ok, k + 1)
                ps, _ = scores_of(n, u)
                if u < A_UNITS:
                    w = window(n, "a")[1]
                    near = min(w, NEAR)
                    at = s_ps[u % 2][:, 1, HALF - NEAR:HALF] if is_whole(n, u) else s_ps[u % 2][:, 0, w - near:w]
                    nc.vector.tensor_tensor(at, at, bias[:, u, NEAR - near:], ALU.add).then_inc(biased, 1)
                    dve.wait_ge(biased, A_UNITS * n + u + 1)
                    axis = AX.XY if is_whole(n, u) else AX.X
                    nc.vector.tensor_reduce(nmax[u % 2][:, 0:1], ps, axis, ALU.max, negate=True).then_inc(max_ok, 1)
                else:
                    nc.vector.tensor_reduce(nmax[u % 2][:], ps, AX.X, ALU.max, negate=True).then_inc(max_ok, 1)

            def copy_t(n, u):
                if is_whole(n, u):
                    dve.wait_ge(pv_ok, UNITS * n + u - 1)
                    dve.wait_ge(t_ok, UNITS * n + u + 1)
                    nc.vector.tensor_copy(prob_t[u % 2][:, 512:], t_ps[:, 512:FULL * P]).then_inc(t_dve, 1)

            def copy_o(n, mixer):
                if not isinstance(n, int) or n:
                    dve.wait_ge(o_st[mixer], 16 * n)
                dve.wait_ge(ot_ok[mixer], n + 1)
                nc.vector.tensor_copy(o_t[mixer][:].rearrange("p k n -> p (k n)"), ot_ps)\
                    .then_inc(ot_out[mixer], 1)

            def divide(n, u):
                k = UNITS * n + u
                if not isinstance(n, int) or k:
                    dve.wait_ge(o_ok, k)
                dve.wait_ge(pv_ok, k + 1)
                heads = 1 if u < A_UNITS else 2
                nc.vector.reciprocal(rden[:, 0:heads], den[u % 4][:, 0:heads]).then_inc(rden_ok, 1)
                if not isinstance(n, int) or n:
                    dve.wait_ge(ot_ok[u // A_UNITS], n)
                dve.wait_ge(rden_ok, k + 1)
                if u < A_UNITS:
                    nc.vector.tensor_scalar(o[:, u, :], o_ps[u % 2][:, u % 2 * HEAD:(u % 2 + 1) * HEAD],
                                            rden[:, 0:1], None, ALU.mult).then_inc(o_ok, 1)
                else:
                    pair_out = o_ps[u % 2][:, 0:6 * HEAD].rearrange("p (a f) -> p a f", f=3 * HEAD)[:, :, 0:HEAD]
                    nc.vector.tensor_tensor(o[:, HEADS + u - A_UNITS::PAIRS_B, :], pair_out, rden[:].unsqueeze(2).broadcast_to([P, 2, HEAD]),
                                            ALU.mult).then_inc(o_ok, 1)

            def step(n, u):
                first = isinstance(n, int) and n == 0
                if u == 4 and not first:
                    copy_o(n - 1, 1)
                maxima(n, u)
                if not (first and u < 3):
                    divide(*before(n, u, 3))
                if not (first and u < 1):
                    copy_t(*before(n, u))
                if u == UNITS - 1:
                    copy_o(n, 0)

            dve.wait_ge(k0_hi, 1)
            nc.vector.tensor_tensor(keys[HEAD:, :, SEQ:SEQ + P], raw_cache[HEAD:, :, :],
                                    keys[HEAD:, :, SEQ:SEQ + P].bitcast(F32), ALU.subtract).then_inc(k0_ok, 1)
            dve.wait_ge(const_ld, 6 * 16)
            for h in range(HEADS):
                nc.vector.tensor_scalar(bias[:, h, :], bias[:, h, :], far[:, h, 0:1], None, ALU.subtract)\
                    .then_inc(bias_sub, 1)
            dve.wait_ge(bias_sub, HEADS)
            nc.vector.memset(bias[0:CHUNK, :, NEAR - CHUNK:], NEG).then_inc(bias_set, 1)
            dve.wait_ge(bias_set, 1)
            for n in range(LOOP):
                for u in range(UNITS):
                    step(n, u)
            with nc.vector.Fori(LOOP, TILES + 1) as n:
                for u in range(UNITS):
                    step(n, u)
            divide(TILES, UNITS - 3)
            copy_t(TILES, UNITS - 1)
            divide(TILES, UNITS - 2)
            divide(TILES, UNITS - 1)
            copy_o(TILES, 1)


def combine(nc, oT, xT, w_o, gains, all_ones, x1T, h2T):
    PAIRS = KD // 2
    LAST = N_BLOCKS - 1
    KS = KD // 2
    with ExitStack() as ctx:
        m = Memory(nc, ctx, "combine")
        o_raw = [m.sbuf(f"o_raw{i}", [P, 2, BLOCK]) for i in range(2)]
        o_hi = [m.sbuf(f"o_hi{i}", [P, KD, BLOCK], F32R) for i in range(2)]
        o_lo = [m.sbuf(f"o_lo{i}", [P, KD, BLOCK], F32R) for i in range(2)]
        x1 = [m.sbuf(f"x1{i}", [P, KD, BLOCK]) for i in range(2)]
        x_sq = m.sbuf("x_sq", [P, KD, SUB])
        ssq = m.sbuf("ssq", [P, BLOCK])
        n_t = m.sbuf("n_t", [P, SUBS, SUB])
        n_r = m.sbuf("n_r", [P, SUBS, SUB])
        n_r2 = m.sbuf("n_r2", [P, SUBS, SUB])
        n_c = m.sbuf("n_c", [P, SUBS, SUB])
        h2 = [m.sbuf(f"h2{i}", [P, BLOCK]) for i in range(2)]
        w_raw = [m.sbuf(f"w_raw{s}", [P, KD, P]) for s in range(2)]
        w_hi = [m.sbuf(f"w_hi{s}", [P, KD, P], F32R) for s in range(2)]
        w_lo = [m.sbuf(f"w_lo{s}", [P, KD, P], F32R) for s in range(2)]
        g_in = m.sbuf("g_in", [P, KD])
        g_x = m.sbuf("g_x", [P, KD])
        eps = m.sbuf("eps", [P, 1])
        ones_sb = m.sbuf("ones", [P, P])
        z = [[m.psum(f"z{s}{i}", [P, 512]) for i in range(2)] for s in range(2)]
        ms = m.psum("ms", [P, SUBS, 512])

        const_ld = m.sem("const_ld")
        o_ld, x_ld, w_ld = ([m.sem(f"{n}{i}") for i in range(2)] for n in ("o_ld", "x_ld", "w_ld"))
        w_hi_ok, w_lo_ok = ([m.sem(f"{n}{s}") for s in range(2)] for n in ("w_hi_ok", "w_lo_ok"))
        z_ok = [[m.sem(f"z_ok{s}{i}") for i in range(2)] for s in range(2)]
        x1_ok = [[m.sem(f"x1_ok{s}{i}") for i in range(2)] for s in range(2)]
        o_hi_ok, o_lo_ok = m.sem("o_hi_ok"), m.sem("o_lo_ok")
        eps_ok, gains_ok = m.sem("eps_ok"), m.sem("gains_ok")
        sq_ok, ssq_ok, ms_ok = m.sem("sq_ok"), m.sem("ssq_ok"), m.sem("ms_ok")
        ln_ok, r_ok, r2_ok, t_ok, c_ok = (m.sem(n) for n in ("ln_ok", "r_ok", "r2_ok", "t_ok", "c_ok"))
        h2_ok, x1_st = m.sem("h2_ok"), m.sem("x1_st")
        h2_st = [m.sem(f"h2_st{i}") for i in range(2)]

        block = ctx.enter_context(nc.Block())

        @block.sync
        def _(sp):
            def load_pair(g, src):
                for s in range(2):
                    sp.wait_ge(w_lo_ok[s], g)
                    sp.dma_start(w_raw[s][:], src(s)).then_inc(w_ld[s], 16)

            load_pair(0, lambda s: w_o[0, s])
            for b in range(N_BLOCKS):
                with sp.Fori(1, PAIRS) as i:
                    load_pair(b * PAIRS + i, lambda s: w_o[ds(i, 1), s].rearrange("a p k n -> p (a k) n"))
                if b < LAST:
                    load_pair((b + 1) * PAIRS, lambda s: w_o[0, s])

        @block.gpsimd
        def _(pool):
            def load_x(b):
                pool.dma_start(x1[b % 2][:], xT[:, :, b * BLOCK:(b + 1) * BLOCK].rearrange("k p n -> p k n"))\
                    .then_inc(x_ld[b % 2], 16)

            def load_o(b):
                for q in range(KS):
                    n = KS * b + q
                    if n > 1:
                        pool.wait_ge(o_lo_ok, 2 * (n - 1))
                    pool.dma_start(o_raw[n % 2][:], oT[2 * q:2 * q + 2, :, b * BLOCK:(b + 1) * BLOCK]
                                   .rearrange("k p n -> p k n")).then_inc(o_ld[n % 2], 16)

            pool.dma_start(g_in[:], gains).then_inc(const_ld, 16)
            pool.dma_start(ones_sb[:], all_ones).then_inc(const_ld, 16)
            load_o(0)
            load_x(0)
            load_x(1)
            load_o(1)
            for b in range(N_BLOCKS):
                cols = slice(b * BLOCK, (b + 1) * BLOCK)
                for s in range(2):
                    for j in range(SUBS):
                        pool.wait_ge(x1_ok[s][j], PAIRS * (b + 1))
                pool.dma_start(x1T[:, :, cols].rearrange("k p n -> p k n"), x1[b % 2][:]).then_inc(x1_st, 16)
                if b + 2 < N_BLOCKS:
                    load_o(b + 2)
                for k in range(KD):
                    pool.wait_ge(h2_ok, KD * b + k + 1)
                    pool.dma_start(h2T[k, :, cols], h2[k % 2][:]).then_inc(h2_st[k % 2], 16)
                if b + 2 < N_BLOCKS:
                    pool.wait_ge(x1_st, 16 * (b + 1))
                    load_x(b + 2)
            pool.wait_ge(x1_st, 16 * N_BLOCKS)
            for i in range(2):
                pool.wait_ge(h2_st[i], 16 * N_BLOCKS * KD // 2)

        @block.tensor
        def _(pe):
            def pair(b, i):
                g = b * PAIRS + i
                for s in range(2):
                    pe.wait_ge(w_lo_ok[s], g + 1)
                    for j in range(SUBS):
                        pe.wait_ge(x1_ok[s][j], g)
                        cols = slice(j * SUB, (j + 1) * SUB)
                        dense(nc, z[s][j][:, 0:SUB], (lambda k: w_hi[s][:, k, :], lambda k: w_lo[s][:, k, :]),
                              (lambda k: o_hi[b % 2][:, k, cols], lambda k: o_lo[b % 2][:, k, cols]), KD)\
                            .then_inc(z_ok[s][j], 1)

            def mean_square(b):
                pe.wait_ge(ssq_ok, SUBS * (b + 1))
                if b:
                    pe.wait_ge(c_ok, b)
                for j in range(SUBS):
                    last = nc.tensor.matmul(ms[:, j, 0:SUB], ones_sb[:], ssq[:, j * SUB:(j + 1) * SUB],
                                            start=True, stop=True)
                last.then_inc(ms_ok, 1)

            pe.wait_ge(const_ld, 32)
            for b in range(N_BLOCKS):
                pe.wait_ge(o_lo_ok, KD * (b + 1))
                pair(b, 0)
                if b:
                    mean_square(b - 1)
                with pe.Fori(1, PAIRS) as i:
                    pair(b, i)
            mean_square(LAST)

        @block.scalar
        def _(act):
            nc.scalar.preload_act_table_set("natural_log_exp_and_others")

            def split_hi(s, g):
                act.wait_ge(w_ld[s], 16 * (g + 1))
                act.wait_ge(z_ok[s][1], g)
                nc.scalar.activation(w_hi[s][:], w_raw[s][:], ACT.Copy).then_inc(w_hi_ok[s], 1)

            def split_o(b):
                if b > 1:
                    act.wait_ge(z_ok[1][1], PAIRS * (b - 1))
                for k in range(KD):
                    n = KS * b + k // 2
                    act.wait_ge(o_ld[n % 2], 16 * (n // 2 + 1))
                    nc.scalar.activation(o_hi[b % 2][:, k, :], o_raw[n % 2][:, k % 2, :], ACT.Copy)\
                        .then_inc(o_hi_ok, 1)

            def squares(b):
                for s in range(2):
                    for j in range(SUBS):
                        act.wait_ge(x1_ok[s][j], PAIRS * (b + 1))
                for j in range(SUBS):
                    if b or j:
                        act.wait_ge(ssq_ok, SUBS * b + j)
                    nc.scalar.activation(x_sq[:], x1[b % 2][:, :, j * SUB:(j + 1) * SUB], ACT.Square)\
                        .then_inc(sq_ok, 1)

            def root(b):
                act.wait_ge(ms_ok, b + 1)
                if b:
                    act.wait_ge(c_ok, b)
                nc.scalar.activation(n_t[:], ms[:, :, 0:SUB], ACT.Ln, bias=eps[:, 0:1]).then_inc(ln_ok, 1)
                act.wait_ge(ln_ok, b + 1)
                nc.scalar.activation(n_r[:], n_t[:], ACT.Exp, scale=-0.5).then_inc(r_ok, 1)
                act.wait_ge(r_ok, b + 1)
                nc.scalar.activation(n_r2[:], n_r[:], ACT.Square).then_inc(r2_ok, 1)

            act.wait_ge(eps_ok, 1)
            split_hi(0, 0)
            split_o(0)
            split_hi(1, 0)
            for b in range(N_BLOCKS):
                n = PAIRS - 1 if b == LAST else PAIRS
                if b + 1 < N_BLOCKS:
                    split_o(b + 1)
                if b:
                    split_hi(0, b * PAIRS + 1)
                    split_hi(1, b * PAIRS + 1)
                    root(b - 1)
                with nc.scalar.Fori(1 if b else 0, n) as i:
                    split_hi(0, b * PAIRS + i + 1)
                    split_hi(1, b * PAIRS + i + 1)
                squares(b)
            root(LAST)

        @block.vector
        def _(dve):
            def split_lo(s, g):
                dve.wait_ge(w_hi_ok[s], g + 1)
                nc.vector.tensor_tensor(w_lo[s][:], w_raw[s][:], w_hi[s][:].bitcast(F32), ALU.subtract)\
                    .then_inc(w_lo_ok[s], 1)

            def split_o(b):
                for k in range(KD):
                    n = KS * b + k // 2
                    dve.wait_ge(o_hi_ok, b * KD + k + 1)
                    nc.vector.tensor_tensor(o_lo[b % 2][:, k, :], o_raw[n % 2][:, k % 2, :],
                                            o_hi[b % 2][:, k, :].bitcast(F32), ALU.subtract).then_inc(o_lo_ok, 1)

            def add(b, i, s, j):
                dve.wait_ge(z_ok[s][j], b * PAIRS + i + 1)
                part = x1[b % 2][:, ds(2 * i + s, 1), j * SUB:(j + 1) * SUB].rearrange("p a n -> p (a n)")
                nc.vector.tensor_tensor(part, part, z[s][j][:, 0:SUB], ALU.add).then_inc(x1_ok[s][j], 1)

            def pair(b, i, prefetch):
                for s in range(2):
                    add(b, i, s, 0)
                    add(b, i, s, 1)
                    if prefetch:
                        split_lo(s, b * PAIRS + i + 1)

            def sums(b):
                if b:
                    dve.wait_ge(ms_ok, b)
                for j in range(SUBS):
                    dve.wait_ge(sq_ok, SUBS * b + j + 1)
                    nc.vector.tensor_reduce(ssq[:, j * SUB:(j + 1) * SUB], x_sq[:].rearrange("p k n -> p n k"),
                                            AX.X, ALU.add).then_inc(ssq_ok, 1)

            def normed(b):
                dve.wait_ge(r2_ok, b + 1)
                nc.vector.scalar_tensor_tensor(n_t[:], ms[:, :, 0:SUB], eps[:, 0:1], n_r2[:], ALU.add, ALU.mult)\
                    .then_inc(t_ok, 1)
                dve.wait_ge(t_ok, b + 1)
                if b:
                    dve.wait_ge(h2_ok, KD * b)
                nc.vector.scalar_tensor_tensor(n_c[:], n_t[:], 3.0, n_r[:], ALU.subtract, ALU.mult)\
                    .then_inc(c_ok, 1)
                dve.wait_ge(c_ok, b + 1)
                for k in range(KD):
                    n = KD * b + k
                    if n > 1:
                        dve.wait_ge(h2_st[k % 2], 16 * (n // 2))
                    nc.vector.scalar_tensor_tensor(h2[k % 2][:], x1[b % 2][:, k, :], g_x[:, k:k + 1],
                                                   n_c[:].rearrange("p a n -> p (a n)"), ALU.mult, ALU.mult)\
                        .then_inc(h2_ok, 1)

            nc.vector.memset(eps[:], EPS).then_inc(eps_ok, 1)
            dve.wait_ge(const_ld, 32)
            nc.vector.tensor_scalar(g_x[:], g_in[:], -0.5, None, ALU.mult).then_inc(gains_ok, 1)
            dve.wait_ge(gains_ok, 1)
            dve.wait_ge(eps_ok, 1)
            split_lo(0, 0)
            split_o(0)
            split_lo(1, 0)
            for b in range(N_BLOCKS):
                if b + 1 < N_BLOCKS:
                    split_o(b + 1)
                dve.wait_ge(x_ld[b % 2], 16 * (b // 2 + 1))
                if b:
                    pair(b, 0, True)
                    normed(b - 1)
                with nc.vector.Fori(1 if b else 0, PAIRS - 1) as i:
                    pair(b, i, True)
                pair(b, PAIRS - 1, b < LAST)
                sums(b)
            normed(LAST)


def ffn(nc, h2T, x1T, w_gu, w_dn, conv, state, yT, gate_prompt, gate_sample):
    F_TILES = D_FF // P
    PARTS = 2
    KF = F_TILES // PARTS
    DOWN = KD // 2
    PAIRS = KF + DOWN
    LAST = N_BLOCKS - 1
    CUT = SEQ - LAST * BLOCK
    H = 2
    with ExitStack() as ctx:
        m = Memory(nc, ctx, "ffn")
        h_raw = [m.sbuf(f"h_raw{i}", [P, BLOCK]) for i in range(2)]
        h_hi = m.sbuf("h_hi", [P, KD, BLOCK], F32R)
        h_lo = m.sbuf("h_lo", [P, KD, BLOCK], F32R)
        y_hi = m.sbuf("y_hi", [P, KF, BLOCK], F32R)
        y_lo = m.sbuf("y_lo", [P, KF, BLOCK], F32R)
        acc = m.sbuf("acc", [P, KD, BLOCK])
        w_raw = [m.sbuf(f"w_raw{s}", [P, KF, P]) for s in range(2)]
        w_hi = [m.sbuf(f"w_hi{s}", [P, KF, P], F32R) for s in range(2)]
        w_lo = [m.sbuf(f"w_lo{s}", [P, KF, P], F32R) for s in range(2)]
        gate = m.sbuf("gate", [P, H + BLOCK])
        gate_s = m.sbuf("gate_s", [P, H + DEC])
        c1 = [m.sbuf(f"c1{j}", [P, SUB]) for j in range(SUBS)]
        c2 = [m.sbuf(f"c2{j}", [P, SUB]) for j in range(SUBS)]
        silu = [m.sbuf(f"silu{j}", [P, SUB]) for j in range(SUBS)]
        y = [m.sbuf(f"y{j}", [P, SUB]) for j in range(SUBS)]
        conv_sb = m.sbuf("conv", [P, F_TILES, 4])
        state_sb = m.sbuf("state", [P, F_TILES, H])
        carry = m.sbuf("carry", [P, F_TILES, H])
        tail = m.sbuf("tail", [P, F_TILES, H])
        z = [[m.psum(f"z{s}{i}", [P, 512]) for i in range(2)] for s in range(2)]

        const_ld, acc_ld, y_st = m.sem("const_ld"), m.sem("acc_ld"), m.sem("y_st")
        h_ld, w_ld = ([m.sem(f"{n}{i}") for i in range(2)] for n in ("h_ld", "w_ld"))
        w_hi_ok, w_lo_ok = ([m.sem(f"{n}{s}") for s in range(2)] for n in ("w_hi_ok", "w_lo_ok"))
        z_ok = [[m.sem(f"z_ok{s}{i}") for i in range(2)] for s in range(2)]
        z_free = [[m.sem(f"z_free{s}{i}") for i in range(2)] for s in range(2)]
        h_hi_ok, h_lo_ok, zero_ok = m.sem("h_hi_ok"), m.sem("h_lo_ok"), m.sem("zero_ok")
        c1_ok, c2_ok, conv_ok, silu_ok, y_hi_ok, y_lo_ok = (
            [m.sem(f"{n}{i}") for i in range(2)] for n in ("c1_ok", "c2_ok", "conv_ok", "silu_ok", "y_hi_ok", "y_lo_ok"))
        halo_ok, carry_ok, s_gate_ok, s1_ok, s2_ok, tail_ok, gate_st = (
            m.sem(n) for n in ("halo_ok", "carry_ok", "s_gate_ok", "s1_ok", "s2_ok", "tail_ok", "gate_st"))

        block = ctx.enter_context(nc.Block())

        @block.sync
        def _(sp):
            def load_pair(g, src, k):
                for s in range(2):
                    sp.wait_ge(w_lo_ok[s], g)
                    sp.dma_start(w_raw[s][:, 0:k, :], src(s)).then_inc(w_ld[s], 16)

            def at(w, i):
                return lambda s: w[ds(i, 1), s].rearrange("a p k n -> p (a k) n")

            sp.dma_start(conv_sb[:], conv).then_inc(const_ld, 16)
            sp.dma_start(state_sb[:], state).then_inc(const_ld, 16)
            for b in range(N_BLOCKS):
                for part in range(PARTS):
                    g0 = (b * PARTS + part) * PAIRS
                    with sp.Fori(0, KF) as i:
                        load_pair(g0 + i, at(w_gu, part * KF + i), KD)
                    load_pair(g0 + KF, at(w_dn, part * DOWN), KF)
                    with sp.Fori(1, DOWN) as i:
                        load_pair(g0 + KF + i, at(w_dn, part * DOWN + i), KF)

        @block.gpsimd
        def _(pool):
            def load_h(b):
                for k in range(KD):
                    if b or k > 1:
                        pool.wait_ge(h_lo_ok, KD * b + k - 1)
                    pool.dma_start(h_raw[k % 2][:], h2T[k, :, b * BLOCK:(b + 1) * BLOCK]).then_inc(h_ld[k % 2], 16)

            def load_acc(b):
                if b:
                    pool.wait_ge(y_st, 16 * KD * b)
                pool.dma_start(acc[:], x1T[:, :, b * BLOCK:(b + 1) * BLOCK].rearrange("k p n -> p k n"))\
                    .then_inc(acc_ld, 16)

            load_h(0)
            load_acc(0)
            for b in range(N_BLOCKS):
                if b < LAST:
                    load_h(b + 1)
                g1 = (b * PARTS + PARTS - 1) * PAIRS + KF
                for d in range(KD):
                    for j in range(SUBS):
                        pool.wait_ge(z_free[d % 2][j], g1 + d // 2 + 1)
                    pool.dma_start(yT[d, :, b * BLOCK:(b + 1) * BLOCK], acc[:, d, :]).then_inc(y_st, 16)
                if b < LAST:
                    load_acc(b + 1)
            pool.wait_ge(carry_ok, N_BLOCKS * F_TILES)
            pool.wait_ge(tail_ok, F_TILES)
            pool.dma_start(gate_sample, carry[:]).then_inc(gate_st, 16)
            pool.dma_start(gate_prompt, tail[:]).then_inc(gate_st, 16)
            pool.wait_ge(gate_st, 32)
            pool.wait_ge(y_st, 16 * KD * N_BLOCKS)

        @block.tensor
        def _(pe):
            def pair(g, hi, lo, n_k, last_wait=None):
                for s in range(2):
                    pe.wait_ge(w_lo_ok[s], g + 1)
                    for j in range(SUBS):
                        pe.wait_ge(z_free[s][j], g)
                        cols = slice(j * SUB, (j + 1) * SUB)
                        dense(nc, z[s][j][:, 0:SUB], (lambda k: w_hi[s][:, k, :], lambda k: w_lo[s][:, k, :]),
                              (lambda k: hi[:, k, cols], lambda k: lo[:, k, cols]), n_k,
                              last_wait and (lambda k: k == n_k - 1 and last_wait(j))).then_inc(z_ok[s][j], 1)

            for b in range(N_BLOCKS):
                pe.wait_ge(h_lo_ok, KD * (b + 1))
                for part in range(PARTS):
                    n = b * PARTS + part
                    g0 = n * PAIRS
                    with pe.Fori(0, KF) as i:
                        pair(g0 + i, h_hi, h_lo, KD)
                    for j in range(SUBS):
                        pe.wait_ge(y_lo_ok[j], KF * (n + 1) - 1)
                    pair(g0 + KF, y_hi, y_lo, KF, lambda j: pe.wait_ge(y_lo_ok[j], KF * (n + 1)))
                    with pe.Fori(1, DOWN) as i:
                        pair(g0 + KF + i, y_hi, y_lo, KF)

        @block.scalar
        def _(act):
            def split_hi(s, g, n_k):
                act.wait_ge(w_ld[s], 16 * (g + 1))
                act.wait_ge(z_ok[s][1], g)
                nc.scalar.activation(w_hi[s][:, 0:n_k, :], w_raw[s][:, 0:n_k, :], ACT.Copy).then_inc(w_hi_ok[s], 1)

            def split_h(b):
                for k in range(KD):
                    act.wait_ge(h_ld[k % 2], 16 * ((KD * b + k) // 2 + 1))
                    nc.scalar.activation(h_hi[:, k, :], h_raw[k % 2][:], ACT.Copy).then_inc(h_hi_ok, 1)

            def gate_up(b, g, c, n_k):
                for j in range(SUBS):
                    act.wait_ge(z_ok[0][j], g + 1)
                    if j == 0:
                        act.wait_ge(carry_ok, c)
                    nc.scalar.activation(gate[:, H + j * SUB:H + (j + 1) * SUB], z[0][j][:, 0:SUB], ACT.Copy)\
                        .then_inc(z_free[0][j], 1)
                split_hi(0, g + 1, n_k)
                for j in range(SUBS):
                    act.wait_ge(conv_ok[j], c + 1)
                    nc.scalar.activation(silu[j][:], c1[j][:], ACT.Silu).then_inc(silu_ok[j], 1)
                split_hi(1, g + 1, n_k)

            split_hi(0, 0, KD)
            split_h(0)
            split_hi(1, 0, KD)
            for b in range(N_BLOCKS):
                for part in range(PARTS):
                    n = b * PARTS + part
                    g0, c0 = n * PAIRS, n * KF
                    with nc.scalar.Fori(0, KF - 1) as i:
                        gate_up(b, g0 + i, c0 + i, KD)
                    gate_up(b, g0 + KF - 1, c0 + KF - 1, KF)
                    if part == PARTS - 1 and b < LAST:
                        act.wait_ge(z_ok[1][1], g0 + KF)
                        split_h(b + 1)
                    with nc.scalar.Fori(0, DOWN - 1) as i:
                        split_hi(0, g0 + KF + i + 1, KF)
                        split_hi(1, g0 + KF + i + 1, KF)
                    if n + 1 < N_BLOCKS * PARTS:
                        split_hi(0, g0 + PAIRS, KD)
                        split_hi(1, g0 + PAIRS, KD)

        @block.vector
        def _(dve):
            def split_lo(s, g, n_k):
                dve.wait_ge(w_hi_ok[s], g + 1)
                nc.vector.tensor_tensor(w_lo[s][:, 0:n_k, :], w_raw[s][:, 0:n_k, :],
                                        w_hi[s][:, 0:n_k, :].bitcast(F32), ALU.subtract).then_inc(w_lo_ok[s], 1)

            def split_h(b):
                for k in range(KD):
                    dve.wait_ge(h_hi_ok, b * KD + k + 1)
                    nc.vector.tensor_tensor(h_lo[:, k, :], h_raw[k % 2][:], h_hi[:, k, :].bitcast(F32), ALU.subtract)\
                        .then_inc(h_lo_ok, 1)

            def of(ap, i):
                return ap[:, ds(i, 1), :].rearrange("p a n -> p (a n)")

            def convolve(dst, tmp, src, taps, n, waits, done):
                nc.vector.tensor_scalar(dst, src[:, H:H + n], taps[:, 2:3], taps[:, 3:4], ALU.mult, ALU.add)\
                    .then_inc(done[0], 1)
                dve.wait_ge(done[0], waits + 1)
                nc.vector.scalar_tensor_tensor(tmp, src[:, 1:1 + n], taps[:, 1:2], dst, ALU.mult, ALU.add)\
                    .then_inc(done[1], 1)
                dve.wait_ge(done[1], waits + 1)
                nc.vector.scalar_tensor_tensor(dst, src[:, 0:n], taps[:, 0:1], tmp, ALU.mult, ALU.add)\
                    .then_inc(done[2], 1)

            def gate_up(b, g, f, c, jf, n_k):
                taps = of(conv_sb, f)
                dve.wait_ge(carry_ok, c)
                nc.vector.tensor_scalar(gate[:, 0:H], of(carry, f), 1.0, None, ALU.mult).then_inc(halo_ok, 1)
                dve.wait_ge(halo_ok, c + 1)
                for j in range(SUBS):
                    dve.wait_ge(z_free[0][j], g + 1)
                    dve.wait_ge(silu_ok[j], c)
                    n = CUT - j * SUB if b == LAST and j else SUB
                    convolve(c1[j][:, 0:n], c2[j][:, 0:n], gate[:, j * SUB:H + (j + 1) * SUB], taps, n, c,
                             (c1_ok[j], c2_ok[j], conv_ok[j] if n == SUB else s_gate_ok))
                if b == LAST:
                    cs = c - LAST * F_TILES
                    nc.vector.tensor_scalar(gate_s[:, 0:H], of(state_sb, f), 1.0, None, ALU.mult).then_inc(s_gate_ok, 1)
                    nc.vector.tensor_scalar(gate_s[:, H:], gate[:, H + CUT:], 1.0, None, ALU.mult).then_inc(s_gate_ok, 1)
                    dve.wait_ge(s_gate_ok, 3 * cs + 3)
                    n = CUT - SUB
                    convolve(c1[1][:, n:], c2[1][:, n:], gate_s, taps, DEC, cs, (s1_ok, s2_ok, conv_ok[1]))
                    nc.vector.tensor_scalar(of(tail, f), gate[:, CUT:H + CUT], 1.0, None, ALU.mult).then_inc(tail_ok, 1)
                split_lo(0, g + 1, n_k)
                nc.vector.tensor_scalar(of(carry, f), gate[:, BLOCK:H + BLOCK], 1.0, None, ALU.mult).then_inc(carry_ok, 1)
                for j in range(SUBS):
                    cols = slice(j * SUB, (j + 1) * SUB)
                    dve.wait_ge(silu_ok[j], c + 1)
                    dve.wait_ge(z_ok[1][j], g + 1)
                    dve.wait_ge(y_lo_ok[j], c)
                    nc.vector.tensor_tensor(y[j][:], silu[j][:], z[1][j][:, 0:SUB], ALU.mult).then_inc(z_free[1][j], 1)
                    dve.wait_ge(z_free[1][j], g + 1)
                    hi, lo = (ap[:, ds(jf, 1), cols].rearrange("p a n -> p (a n)") for ap in (y_hi, y_lo))
                    nc.vector.tensor_scalar(hi, y[j][:], 1.0, None, ALU.mult).then_inc(y_hi_ok[j], 1)
                    dve.wait_ge(y_hi_ok[j], c + 1)
                    nc.vector.tensor_tensor(lo, y[j][:], hi.bitcast(F32), ALU.subtract).then_inc(y_lo_ok[j], 1)
                split_lo(1, g + 1, n_k)

            def down(g, i, n_k):
                for s in range(2):
                    for j in range(SUBS):
                        dve.wait_ge(z_ok[s][j], g + 1)
                        part = acc[:, ds(2 * i + s, 1), j * SUB:(j + 1) * SUB].rearrange("p a n -> p (a n)")
                        nc.vector.tensor_tensor(part, part, z[s][j][:, 0:SUB], ALU.add).then_inc(z_free[s][j], 1)
                    if n_k:
                        split_lo(s, g + 1, n_k)

            nc.vector.memset(carry[:], 0.0).then_inc(zero_ok, 1)
            dve.wait_ge(zero_ok, 1)
            dve.wait_ge(const_ld, 32)
            split_lo(0, 0, KD)
            split_h(0)
            split_lo(1, 0, KD)
            for b in range(N_BLOCKS):
                for part in range(PARTS):
                    n = b * PARTS + part
                    g0, c0, f0 = n * PAIRS, n * KF, part * KF
                    with nc.vector.Fori(0, KF - 1) as i:
                        gate_up(b, g0 + i, f0 + i, c0 + i, i, KD)
                    gate_up(b, g0 + KF - 1, f0 + KF - 1, c0 + KF - 1, KF - 1, KF)
                    if part == PARTS - 1 and b < LAST:
                        split_h(b + 1)
                    if part == 0:
                        dve.wait_ge(acc_ld, 16 * (b + 1))
                    with nc.vector.Fori(0, DOWN - 1) as i:
                        down(g0 + KF + i, i, KF)
                    down(g0 + PAIRS - 1, DOWN - 1, KD if n + 1 < N_BLOCKS * PARTS else 0)


def encoder_step(nc, a):
    scratch = {name: nc.dram_tensor(f"{name}_scratch", shape, F32, kind="Internal").ap()
               for name, shape in (("q_a", (4, P, TOKENS)), ("rel_rows", (P, HEADS, 3 * P)), ("oT", (KD, P, TOKENS)),
                                   ("x1T", (KD, P, TOKENS)), ("h2T", (KD, P, TOKENS)))}
    project(nc, a["xT"], a["w_qk"], a["w_rv"], a["gains_in"], a["rope_cos"], a["rope_sin"], a["swap"],
            a["head_ones"], a["all_ones"], a["ident"], a["rel"],
            scratch["q_a"], a["k_a"], a["qk_b"], a["v_all"], scratch["rel_rows"])
    attend(nc, scratch["q_a"], a["k_a"], a["qk_b"], a["v_all"], a["ka_cache"], a["kb_cache"], a["va_cache"],
           a["vb_cache"], scratch["rel_rows"], a["sinks"], a["ident"], scratch["oT"])
    combine(nc, scratch["oT"], a["xT"], a["w_o"], a["gains_ffn"], a["all_ones"], scratch["x1T"], scratch["h2T"])
    ffn(nc, scratch["h2T"], scratch["x1T"], a["w_gu"], a["w_dn"], a["conv"], a["state"],
        a["yT"], a["gate_prompt"], a["gate_sample"])


def kernel(**inputs):
    import numpy as np
    import concourse.bacc as bacc
    from concourse.bass_utils import run_bass_kernel_spmd

    x = {name: np.asarray(value) for name, value in inputs.items()}

    def tiles(w):
        k, n = w.shape
        return w.reshape(k // P, P, n // P, P).transpose(2, 1, 0, 3)

    def head_pairs(w):
        return w.reshape(w.shape[0], 2, HEADS // 2, HEAD).transpose(0, 2, 1, 3).reshape(w.shape[0], -1)

    width = HEADS * HEAD
    qa, ka, va, qb, kb, vb = np.split(x["w_in"][0], [width, 2 * width, 3 * width, 4 * width, 4 * width + P], axis=1)
    cols = lambda g: g[0].reshape(-1, P).T
    by_head = lambda g: np.tile(g[0], 2)[:, None]
    gate, up = np.split(x["w_gate_up"][0], 2, axis=1)
    rel = x["rel_bias_a"][0][:, ::-1]

    pos = np.concatenate([np.arange(SEQ), PAST + np.arange(DEC)]).astype(np.float32)
    inv = np.power(10000.0, -np.arange(HEAD // 2) / (HEAD // 2)).astype(np.float32)
    angle = (pos[None, :] * inv[:, None]).astype(np.float32)
    cos, sin = np.cos(angle.astype(np.float64)), np.sin(angle.astype(np.float64))
    swap = np.zeros((P, P), np.float32)
    swap[np.arange(P) ^ (HEAD // 2), np.arange(P)] = 1
    head_ones = np.kron(np.eye(2), np.full((HEAD, HEAD), 1 / HEAD))

    arrays = dict(
        xT=np.concatenate([x["x_prompt"][0], x["x_sample"][0]]).T.reshape(KD, P, TOKENS),
        w_qk=np.stack([tiles(qa), tiles(ka)], 1),
        w_rv=np.stack([tiles(np.concatenate([head_pairs(qb), kb], 1)), tiles(np.concatenate([va, vb], 1))], 1),
        gains_in=np.concatenate([cols(x["norm_attn"]), by_head(x["q_norm_a"]), by_head(x["k_norm_a"]),
                                 by_head(x["q_norm_b"]), by_head(x["k_norm_b"])], 1),
        rope_cos=np.tile(cos, (4, 1)), rope_sin=np.tile(np.concatenate([-sin, sin]), (2, 1)),
        swap=swap, head_ones=head_ones, all_ones=np.full((P, P), 1 / D_MODEL), ident=np.eye(P),
        ka_cache=x["cache_a_k"].reshape(PAST, width).T.reshape(-1, P, PAST),
        kb_cache=x["cache_b_k"].reshape(PAST, P).T,
        va_cache=x["cache_a_v"].reshape(PAST, width), vb_cache=x["cache_b_v"].reshape(PAST, P),
        rel=np.concatenate([np.repeat(rel[:, :1], MAX_REL - 1, 1), rel], 1),
        sinks=x["sinks_b"].reshape(2, HEADS // 2).T.reshape(-1),
        w_o=tiles(x["w_out"][0]).reshape(KD // 2, 2, P, KD, P), gains_ffn=cols(x["norm_ffn"]),
        w_gu=np.stack([tiles(gate), tiles(up)], 1),
        w_dn=x["w_down"][0].reshape(2, KF // 2, P, KD // 2, 2, P).transpose(0, 3, 4, 2, 1, 5)
            .reshape(KD, 2, P, KF // 2, P),
        conv=np.concatenate([x["conv_w"][0], x["conv_b"]]).reshape(4, KF, P).transpose(2, 1, 0),
        state=x["state_conv"].reshape(2, KF, P).transpose(2, 1, 0))
    returned = dict(k_a=(4, P, TOKENS), qk_b=(5, P, TOKENS), v_all=(TOKENS, 5 * P), yT=(KD, P, TOKENS),
                    gate_prompt=(P, KF, 2), gate_sample=(P, KF, 2))

    nc = bacc.Bacc("TRN2", target_bir_lowering=False, num_devices=1)
    arrays = {name: np.ascontiguousarray(value, dtype=np.float32) for name, value in arrays.items()}
    drams = {name: nc.dram_tensor(name, value.shape, F32, kind="ExternalInput").ap() for name, value in arrays.items()}
    drams |= {name: nc.dram_tensor(name, shape, F32, kind="ExternalOutput").ap() for name, shape in returned.items()}
    encoder_step(nc, drams)
    got = run_bass_kernel_spmd(nc, [arrays], core_ids=[0]).results[0]

    y = got["yT"].reshape(D_MODEL, TOKENS).T
    k_a, k_b = got["k_a"].reshape(width, TOKENS).T, got["qk_b"][4].T
    v_a, v_b = got["v_all"][:, :width], got["v_all"][:, width:]
    last_a, last_b = slice(SEQ - 8 * CHUNK, SEQ), slice(SEQ - 2 * CHUNK, SEQ)
    heads = lambda t, rows: t[rows].reshape(1, 1, -1, t.shape[1] // HEAD, HEAD)
    conv_rows = lambda t: t.transpose(2, 1, 0).reshape(1, 1, 2, D_FF)
    sample = slice(SEQ, TOKENS)
    return tuple(np.ascontiguousarray(t) for t in (
        y[None, :SEQ], y[None, SEQ:],
        heads(k_a, last_a), heads(v_a, last_a), heads(k_b, last_b), heads(v_b, last_b),
        conv_rows(got["gate_prompt"]),
        heads(k_a, sample), heads(v_a, sample), heads(k_b, sample), heads(v_b, sample),
        conv_rows(got["gate_sample"])))
```

```python
from contextlib import ExitStack

import concourse.bass as bass
from concourse import mybir
from concourse.alu_op_type import AluOpType as ALU

F32 = mybir.dt.float32
F32R = mybir.dt.float32r
BF16 = mybir.dt.bfloat16
ACT = mybir.ActivationFunctionType
AX = mybir.AxisListType

P = 128
D_MODEL = 1024
SEQ = 2048
DEC = 64
PAST = 128
TOKENS = SEQ + DEC
CHUNK = 64
HEAD = 64
HALF_HEAD = HEAD // 2
HEADS = 8
D_FF = 2816
EPS = 1e-6
NEG = -1e30
SCALE = HEAD ** -0.5
MAX_REL = 128
KD = D_MODEL // P
N_BLOCKS = 3
BLOCK = TOKENS // N_BLOCKS
KF = D_FF // P
SUBS = 2
SUB = BLOCK // SUBS
PASSES = ((0, 0), (0, 1), (1, 0))
ds = bass.ds


class Memory:

    def __init__(self, nc, ctx, stage):
        self.nc, self.ctx, self.stage, self.sems = nc, ctx, stage, []
        ctx.callback(self.clear)

    def clear(self):
        self.nc.clear_and_free_semaphores(self.sems)
        self.nc.all_engine_barrier()

    def sbuf(self, name, shape, dtype=F32):
        return self.ctx.enter_context(self.nc.sbuf_tensor(f"{self.stage}_{name}", shape, dtype))

    def psum(self, name, shape, dtype=F32):
        return self.ctx.enter_context(self.nc.psum_tensor(f"{self.stage}_{name}", shape, dtype))

    def sem(self, name):
        self.sems.append(self.nc.alloc_semaphore(f"{self.stage}_{name}"))
        return self.sems[-1]


def dense(nc, out, w_parts, act_parts, n_k, ready=None):
    for k in range(n_k):
        if ready:
            ready(k)
        for w, a in PASSES:
            last = nc.tensor.matmul(out, w_parts[w](k), act_parts[a](k),
                                    start=(k == 0 and (w, a) == PASSES[0]),
                                    stop=(k == n_k - 1 and (w, a) == PASSES[-1]))
    return last


def project(nc, xT, w_qk, w_rv, gains, rope_cos, rope_sin, head_ones, all_ones, ident,
            rel, q_a, k_a, qk_b, v_all, rel_rows):
    QK_PAIRS, RV_PAIRS = 4, 5
    PAIRS = QK_PAIRS + RV_PAIRS
    VT = 88
    NV = SUB // VT
    with ExitStack() as ctx:
        m = Memory(nc, ctx, "project")
        x_raw = m.sbuf("x_raw", [P, KD, BLOCK])
        x_sq = m.sbuf("x_sq", [P, KD // SUBS, BLOCK])
        x_ssq = m.sbuf("x_ssq", [P, BLOCK])
        h = x_sq[:, KD // SUBS - 2:, :]
        h_hi = [m.sbuf(f"h_hi{i}", [P, KD, BLOCK], F32R) for i in range(2)]
        h_lo = [m.sbuf(f"h_lo{i}", [P, KD, BLOCK], F32R) for i in range(2)]
        n_r = m.sbuf("n_r", [P, SUBS, SUB])
        n_r2 = m.sbuf("n_r2", [P, SUBS, SUB])
        n_t = m.sbuf("n_t", [P, SUBS, SUB])
        n_c = m.sbuf("n_c", [P, SUBS, SUB])
        w_raw = [m.sbuf(f"w_raw{s}", [P, KD, P]) for s in range(2)]
        w_hi = [m.sbuf(f"w_hi{s}", [P, KD, P], F32R) for s in range(2)]
        w_lo = [m.sbuf(f"w_lo{s}", [P, KD, P], F32R) for s in range(2)]
        g_x = m.sbuf("g_x", [P, KD])
        g_q = m.sbuf("g_q", [P, 2])
        g_r = m.sbuf("g_r", [P, 2])
        g_in = m.sbuf("g_in", [P, KD + 4])
        eps = m.sbuf("eps", [P, 1])
        cos_sb = m.sbuf("cos", [P, BLOCK])
        sin_sb = m.sbuf("sin", [P, BLOCK])
        head_ones_sb = m.sbuf("head_ones", [P, P])
        head_ones_r = m.sbuf("head_ones_r", [P, P], F32R)
        all_ones_sb = m.sbuf("all_ones", [P, P])
        ident_sb = m.sbuf("ident", [P, P])
        sq = [m.sbuf(f"sq{i}", [P, SUB]) for i in range(2)]
        sq_hi = [m.sbuf(f"sq_hi{i}", [P, SUB], F32R) for i in range(2)]
        sq_lo = [m.sbuf(f"sq_lo{i}", [P, SUB], F32R) for i in range(2)]
        ln = [m.sbuf(f"ln{i}", [P, SUB]) for i in range(2)]
        r0 = [m.sbuf(f"r0{i}", [P, SUB]) for i in range(2)]
        r2 = [m.sbuf(f"r2{i}", [P, SUB]) for i in range(2)]
        tmp = [m.sbuf(f"tmp{i}", [P, SUB]) for i in range(2)]
        corr = [m.sbuf(f"corr{i}", [P, SUB]) for i in range(2)]
        zg = [m.sbuf(f"zg{i}", [P, SUB]) for i in range(2)]
        zc = m.sbuf("zc", [P, SUB])
        zs = m.sbuf("zs", [P, SUB])
        zr = m.sbuf("zr", [P, SUB])
        out_t = [[m.sbuf(f"out{s}{i}", [P, SUB]) for i in range(2)] for s in range(2)]
        v_f = [m.sbuf(f"v_f{i}", [P, SUB]) for i in range(2)]
        v_t = [m.sbuf(f"v_t{i}", [VT, NV, P]) for i in range(2)]

        z = [[m.psum(f"z{s}{i}", [P, 512]) for i in range(2)] for s in range(2)]
        st = m.psum("stat", [P, SUBS, 512])
        v_banks = m.psum("v_banks", [P, SUBS, 512])
        vtr = [v_banks[0:VT, j, :].rearrange("p (c f) -> p c f", c=NV) for j in range(SUBS)]

        x0_ld = [m.sem(f"x0_ld{k}") for k in range(KD)]
        const_ld, x_ld, cs_ld, rel_st = (m.sem(n) for n in ("const_ld", "x_ld", "cs_ld", "rel_st"))
        w_ld = [m.sem(f"w_ld{s}") for s in range(2)]
        w_hi_ok = [m.sem(f"w_hi_ok{s}") for s in range(2)]
        w_lo_ok = [m.sem(f"w_lo_ok{s}") for s in range(2)]
        z_ok = [[m.sem(f"z_ok{s}{i}") for i in range(2)] for s in range(2)]
        out_ok = [[m.sem(f"out_ok{s}{i}") for i in range(2)] for s in range(2)]
        stored = [[m.sem(f"stored{s}{i}") for i in range(2)] for s in range(2)]
        gains_ok, eps_ok = m.sem("gains_ok"), m.sem("eps_ok")
        x_sq_ok, x_part_ok, x_ms_ok = m.sem("x_sq_ok"), m.sem("x_part_ok"), m.sem("x_ms_ok")
        p_sq_ok, p_sum_ok, p_h_ok, p_hi_ok, p_lo_ok, p_g_ok = (
            m.sem(n) for n in ("p_sq_ok", "p_sum_ok", "p_h_ok", "p_hi_ok", "p_lo_ok", "p_g_ok"))
        x_ln_ok, x_r_ok, x_r2_ok, x_t_ok, x_c_ok = (m.sem(n) for n in ("x_ln_ok", "x_r_ok", "x_r2_ok", "x_t_ok", "x_c_ok"))
        h_ok, h_hi_ok, h_lo_ok = m.sem("h_ok"), m.sem("h_hi_ok"), m.sem("h_lo_ok")
        raw_sq_ok, sq_hi_ok, sq_lo_ok, st_ok, ln_ok, r0_ok, r2_ok, corr_ok, zg_ok, rotated, vf_ok, vtr_ok = (
            [m.sem(f"{n}{i}") for i in range(2)] for n in
            ("raw_sq_ok", "sq_hi_ok", "sq_lo_ok", "st_ok", "ln_ok", "r0_ok", "r2_ok", "corr_ok", "zg_ok", "rotated", "vf_ok", "vtr_ok"))
        tmp_ok, zc_ok, zr_ok = m.sem("tmp_ok"), m.sem("zc_ok"), m.sem("zr_ok")

        NORMS = QK_PAIRS * 2 + RV_PAIRS
        LAST = N_BLOCKS - 1

        def loop(eng, b, count, body):
            if b == 0:
                body(0)
            with eng.Fori(1 if b == 0 else 0, count) as i:
                body(i)

        def rv_loop(eng, b, body):
            loop(eng, b, RV_PAIRS - 1, lambda i: body(i, 0, True))
            body(RV_PAIRS - 1, 1, b < LAST)

        def at(ap, i):
            return ap[i] if isinstance(i, int) else ap[ds(i, 1)].rearrange("a p n -> p (a n)")

        block = ctx.enter_context(nc.Block())

        @block.sync
        def _(sp):
            def load_x(b):
                t0 = b * BLOCK
                if b == 0:
                    for k in range(KD):
                        sp.dma_start(x_raw[:, k, :], xT[k, :, t0:t0 + BLOCK]).then_inc(x0_ld[k], 16)
                    return
                sp.wait_ge(h_ok if b == 1 else p_h_ok, KD * max(1, b - 1))
                sp.dma_start(x_raw[:], xT[:, :, t0:t0 + BLOCK].rearrange("k p n -> p k n")).then_inc(x_ld, 16)

            def load_pair(g, src):
                for s in range(2):
                    sp.wait_ge(w_lo_ok[s], g)
                    sp.dma_start(w_raw[s][:], src(s)).then_inc(w_ld[s], 16)

            def store(s, j, g, dst, src):
                sp.wait_ge(out_ok[s][j], g + 1)
                sp.dma_start(dst, src).then_inc(stored[s][j], 16)

            load_x(0)
            load_pair(0, lambda s: w_qk[0, s])
            for b in range(N_BLOCKS):
                t0 = b * BLOCK
                halves = [slice(t0 + j * SUB, t0 + (j + 1) * SUB) for j in range(SUBS)]
                for j in range(SUBS):
                    if b:
                        sp.wait_ge(zr_ok, 2 * b * RV_PAIRS)
                sp.dma_start(cos_sb[:], rope_cos[:, t0:t0 + BLOCK]).then_inc(cs_ld, 16)
                sp.dma_start(sin_sb[:], rope_sin[:, t0:t0 + BLOCK]).then_inc(cs_ld, 16)

                def qk(i, g, nxt):
                    load_pair(g + 1, nxt)
                    if isinstance(i, int) and i == 0 and b < LAST:
                        load_x(b + 1)
                    if isinstance(g, int) and g == 0:
                        sp.dma_start(rel_rows, bass.AP(rel.tensor, 0, [[0, P], [rel.shape[1], rel.shape[0]], [1, rel.shape[1]]]))\
                            .then_inc(rel_st, 16)
                    for s, dst in ((0, q_a), (1, k_a)):
                        for j in range(SUBS):
                            store(s, j, g, at(dst[:, :, halves[j]], i), out_t[s][j][:])

                def next_of(w, i):
                    if isinstance(i, int):
                        return lambda s: w[i + 1, s]
                    return lambda s: w[ds(i + 1, 1), s].rearrange("a p k n -> p (a k) n")

                qk(0, b * PAIRS, next_of(w_qk, 0))
                with sp.Fori(1, QK_PAIRS - 1) as i:
                    qk(i, b * PAIRS + i, next_of(w_qk, i))
                qk(QK_PAIRS - 1, b * PAIRS + QK_PAIRS - 1, lambda s: w_rv[0, s])

                def rv(i, g, nxt):
                    if nxt:
                        load_pair(g + 1, nxt)
                    for j in range(SUBS):
                        store(0, j, g, at(qk_b[:, :, halves[j]], i), out_t[0][j][:])
                    for j in range(SUBS):
                        store(1, j, g, v_all[halves[j], ds(i * P, P)].rearrange("(c p) f -> p c f", p=VT), v_t[j][:])

                loop(sp, b, RV_PAIRS - 1, lambda i: rv(i, b * PAIRS + QK_PAIRS + i, next_of(w_rv, i)))
                rv(RV_PAIRS - 1, b * PAIRS + PAIRS - 1, (lambda s: w_qk[0, s]) if b < LAST else None)
            sp.wait_ge(rel_st, 16)
            for s in range(2):
                for j in range(SUBS):
                    sp.wait_ge(stored[s][j], 16 * N_BLOCKS * PAIRS)

        @block.tensor
        def _(pe):
            def tile(s, j, b, g):
                if j == 0:
                    pe.wait_ge(w_lo_ok[s], g + 1)
                pe.wait_ge(out_ok[s][j], g)
                cols = slice(j * SUB, (j + 1) * SUB)
                hh, hl = h_hi[b % 2], h_lo[b % 2]
                ready = (lambda k: pe.wait_ge(h_lo_ok, k + 1)) if b == 0 and s == 0 and j == 0 else None
                dense(nc, z[s][j][:, 0:SUB], (lambda k: w_hi[s][:, k, :], lambda k: w_lo[s][:, k, :]),
                      (lambda k: hh[:, k, cols], lambda k: hl[:, k, cols]), KD, ready).then_inc(z_ok[s][j], 1)

            def stat(j, n):
                pe.wait_ge(corr_ok[j], n)
                pe.wait_ge(sq_lo_ok[j], n + 1)
                nc.tensor.matmul(st[:, j, 0:SUB], head_ones_r[:], sq_hi[j][:], start=True, stop=False)
                nc.tensor.matmul(st[:, j, 0:SUB], head_ones_r[:], sq_lo[j][:], start=False, stop=True)\
                    .then_inc(st_ok[j], 1)

            def values(j, r, g):
                pe.wait_ge(vf_ok[j], r + 1)
                pe.wait_ge(out_ok[1][j], g)
                for c in range(NV):
                    last = nc.tensor.transpose(vtr[j][:, c, :], v_f[j][:, c * VT:(c + 1) * VT], ident_sb[:])
                last.then_inc(vtr_ok[j], 1)

            def x_stat(b):
                if b == 0:
                    for k in range(KD):
                        pe.wait_ge(x_sq_ok, k + 1)
                        for j in range(SUBS):
                            last = nc.tensor.matmul(v_banks[:, j, 0:SUB], all_ones_sb[:],
                                                    x_sq[:, k % (KD // SUBS), j * SUB:(j + 1) * SUB],
                                                    start=k == 0, stop=k == KD - 1)
                        if k < KD - 1:
                            last.then_inc(x_part_ok, 1)
                else:
                    pe.wait_ge(p_sum_ok, (KD - 1) * b)
                    for j in range(SUBS):
                        last = nc.tensor.matmul(v_banks[:, j, 0:SUB], all_ones_sb[:],
                                                x_ssq[:, j * SUB:(j + 1) * SUB], start=True, stop=True)
                last.then_inc(x_ms_ok, 1)

            pe.wait_ge(const_ld, 4 * 16)
            x_stat(0)
            for b in range(N_BLOCKS):
                if b:
                    pe.wait_ge(p_lo_ok, KD * b)

                def qk(i, first=False):
                    g, n = b * PAIRS + i, b * NORMS + 2 * i
                    tile(0, 0, b, g)
                    if not first:
                        stat(1, n - 1)
                    tile(0, 1, b, g)
                    stat(0, n)
                    tile(1, 0, b, g)
                    stat(1, n)
                    tile(1, 1, b, g)
                    stat(0, n + 1)

                qk(0, True)
                with pe.Fori(1, QK_PAIRS) as i:
                    qk(i)
                stat(1, b * NORMS + 2 * QK_PAIRS - 1)
                if b < LAST:
                    for j in range(SUBS):
                        pe.wait_ge(out_ok[1][j], b * PAIRS)
                    x_stat(b + 1)

                def rv(i, first=False):
                    g, n, r = b * PAIRS + QK_PAIRS + i, b * NORMS + 2 * QK_PAIRS + i, b * RV_PAIRS + i
                    tile(0, 0, b, g)
                    if not first:
                        values(1, r - 1, g - 1)
                    tile(0, 1, b, g)
                    stat(0, n)
                    if b < LAST:
                        pe.wait_ge(x_c_ok, b + 2)
                    tile(1, 0, b, g)
                    stat(1, n)
                    tile(1, 1, b, g)
                    values(0, r, g)

                rv(0, True)
                with pe.Fori(1, RV_PAIRS) as i:
                    rv(i)
                values(1, (b + 1) * RV_PAIRS - 1, (b + 1) * PAIRS - 1)

        @block.scalar
        def _(act):
            nc.scalar.preload_act_table_set("natural_log_exp_and_others")

            def split_hi(s, g):
                act.wait_ge(w_ld[s], 16 * (g + 1))
                act.wait_ge(z_ok[s][1], g)
                nc.scalar.activation(w_hi[s][:], w_raw[s][:], ACT.Copy).then_inc(w_hi_ok[s], 1)

            def square(s, j, g, n):
                act.wait_ge(z_ok[s][j], g + 1)
                act.wait_ge(st_ok[j], n)
                nc.scalar.activation(sq[j][:], z[s][j][:, 0:SUB], ACT.Square).then_inc(raw_sq_ok[j], 1)
                act.wait_ge(raw_sq_ok[j], n + 1)
                nc.scalar.activation(sq_hi[j][:], sq[j][:], ACT.Copy).then_inc(sq_hi_ok[j], 1)

            def root(j, n):
                act.wait_ge(st_ok[j], n + 1)
                act.wait_ge(corr_ok[j], n)
                nc.scalar.activation(ln[j][:], st[:, j, 0:SUB], ACT.Ln, bias=eps[:, 0:1]).then_inc(ln_ok[j], 1)
                act.wait_ge(ln_ok[j], n + 1)
                nc.scalar.activation(r0[j][:], ln[j][:], ACT.Exp, scale=-0.5).then_inc(r0_ok[j], 1)
                act.wait_ge(r0_ok[j], n + 1)
                nc.scalar.activation(r2[j][:], r0[j][:], ACT.Square).then_inc(r2_ok[j], 1)

            def x_square():
                for k in range(KD):
                    act.wait_ge(x0_ld[k], 16)
                    if k >= KD // SUBS:
                        act.wait_ge(x_part_ok, k - KD // SUBS + 1)
                    nc.scalar.activation(x_sq[:, k % (KD // SUBS), :], x_raw[:, k, :], ACT.Square).then_inc(x_sq_ok, 1)

            def x_root(b):
                act.wait_ge(x_ms_ok, b + 1)
                if b:
                    act.wait_ge(x_c_ok, b)
                nc.scalar.activation(n_t[:], v_banks[:, :, 0:SUB], ACT.Ln, bias=eps[:, 0:1]).then_inc(x_ln_ok, 1)
                act.wait_ge(x_ln_ok, b + 1)
                nc.scalar.activation(n_r[:], n_t[:], ACT.Exp, scale=-0.5).then_inc(x_r_ok, 1)
                act.wait_ge(x_r_ok, b + 1)
                nc.scalar.activation(n_r2[:], n_r[:], ACT.Square).then_inc(x_r2_ok, 1)

            def h_split():
                for k in range(KD):
                    act.wait_ge(h_ok, k + 1)
                    nc.scalar.activation(h_hi[0][:, k, :], h[:, k % 2, :], ACT.Copy).then_inc(h_hi_ok, 1)

            nc.scalar.dma_start(g_in[:], gains).then_inc(const_ld, 16)
            nc.scalar.dma_start(all_ones_sb[:], all_ones).then_inc(const_ld, 16)
            nc.scalar.dma_start(head_ones_sb[:], head_ones).then_inc(const_ld, 16)
            nc.scalar.dma_start(ident_sb[:], ident).then_inc(const_ld, 16)
            act.wait_ge(eps_ok, 1)
            x_square()
            for s in range(2):
                act.wait_ge(w_ld[s], 16)
                nc.scalar.activation(w_hi[s][:], w_raw[s][:], ACT.Copy).then_inc(w_hi_ok[s], 1)
            x_root(0)
            h_split()
            for b in range(N_BLOCKS):
                def qk(i):
                    g, n = b * PAIRS + i, b * NORMS + 2 * i
                    square(0, 0, g, n)
                    square(0, 1, g, n)
                    root(0, n)
                    split_hi(0, g + 1)
                    square(1, 0, g, n + 1)
                    root(1, n)
                    square(1, 1, g, n + 1)
                    root(0, n + 1)
                    split_hi(1, g + 1)
                    root(1, n + 1)

                loop(nc.scalar, b, QK_PAIRS, qk)
                if b < LAST:
                    x_root(b + 1)

                def rv(i, gain, prefetch):
                    g, n, r = b * PAIRS + QK_PAIRS + i, b * NORMS + 2 * QK_PAIRS + i, b * RV_PAIRS + i
                    for j in range(SUBS):
                        square(0, j, g, n)
                        act.wait_ge(rotated[j], r)
                        nc.scalar.activation(zg[j][:], z[0][j][:, 0:SUB], ACT.Copy, scale=g_r[:, gain:gain + 1])\
                            .then_inc(zg_ok[j], 1)
                    root(0, n)
                    if prefetch:
                        split_hi(0, g + 1)
                    for j in range(SUBS):
                        act.wait_ge(z_ok[1][j], g + 1)
                        act.wait_ge(vtr_ok[j], r)
                        nc.scalar.activation(v_f[j][:], z[1][j][:, 0:SUB], ACT.Copy).then_inc(vf_ok[j], 1)
                        if j == 0:
                            root(1, n)
                    if prefetch:
                        split_hi(1, g + 1)

                rv_loop(nc.scalar, b, rv)

        @block.vector
        def _(dve):
            def split_lo(s, g):
                dve.wait_ge(w_hi_ok[s], g + 1)
                nc.vector.tensor_tensor(w_lo[s][:], w_raw[s][:], w_hi[s][:].bitcast(F32), ALU.subtract)\
                    .then_inc(w_lo_ok[s], 1)

            def square_low(j, n):
                dve.wait_ge(sq_hi_ok[j], n + 1)
                nc.vector.tensor_tensor(sq_lo[j][:], sq[j][:], sq_hi[j][:].bitcast(F32), ALU.subtract)\
                    .then_inc(sq_lo_ok[j], 1)

            def correction(j, n, m_, before, count):
                dve.wait_ge(r2_ok[j], n + 1)
                nc.vector.scalar_tensor_tensor(tmp[j][:], st[:, j, 0:SUB], eps[:, 0:1], r2[j][:], ALU.add, ALU.mult)\
                    .then_inc(tmp_ok, 1)
                dve.wait_ge(before[j], count)
                dve.wait_ge(tmp_ok, m_ + 1)
                nc.vector.scalar_tensor_tensor(corr[j][:], tmp[j][:], 3.0, r0[j][:], ALU.subtract, ALU.mult)\
                    .then_inc(corr_ok[j], 1)

            def norm(s, j, g, n, m_):
                correction(j, n, m_, out_ok[1 - s], g + s)
                dve.wait_ge(stored[s][j], 16 * g)
                dve.wait_ge(corr_ok[j], n + 1)
                nc.vector.scalar_tensor_tensor(out_t[s][j][:], z[s][j][:, 0:SUB], g_q[:, s:s + 1], corr[j][:],
                                               ALU.mult, ALU.mult).then_inc(out_ok[s][j], 1)

            def rotate(j, g, r):
                cols = slice(j * SUB, (j + 1) * SUB)
                dve.wait_ge(zr_ok, 2 * r + j)
                dve.wait_ge(zg_ok[j], r + 1)
                nc.vector.tensor_tensor(zc[:], zg[j][:], cos_sb[:, cols], ALU.mult).then_inc(zc_ok, 1)
                for half in range(0, P, HALF_HEAD):
                    src, dst = (slice(at, at + HALF_HEAD) for at in (half, half ^ HALF_HEAD))
                    last = nc.vector.tensor_tensor(zs[dst, :], zg[j][src, :], sin_sb[src, cols], ALU.mult)
                last.then_inc(rotated[j], 1)
                dve.wait_ge(zc_ok, 2 * r + j + 1)
                dve.wait_ge(rotated[j], r + 1)
                dve.wait_ge(out_ok[0][1 - j], g + j)
                nc.vector.tensor_tensor(zr[:], zc[:], zs[:], ALU.add).then_inc(zr_ok, 1)

            def norm_rotary(j, g, n, m_, r):
                correction(j, n, m_, out_ok[1], g)
                dve.wait_ge(stored[0][j], 16 * g)
                dve.wait_ge(corr_ok[j], n + 1)
                dve.wait_ge(zr_ok, 2 * r + j + 1)
                nc.vector.scalar_tensor_tensor(out_t[0][j][:], zr[:], -0.5, corr[j][:], ALU.mult, ALU.mult)\
                    .then_inc(out_ok[0][j], 1)

            def value(j, g, r):
                dve.wait_ge(vtr_ok[j], r + 1)
                dve.wait_ge(stored[1][j], 16 * g)
                nc.vector.tensor_copy(v_t[j][:], vtr[j]).then_inc(out_ok[1][j], 1)

            def x_correction(b):
                dve.wait_ge(x_r2_ok, b + 1)
                nc.vector.scalar_tensor_tensor(n_t[:], v_banks[:, :, 0:SUB], eps[:, 0:1], n_r2[:], ALU.add, ALU.mult)\
                    .then_inc(x_t_ok, 1)
                dve.wait_ge(x_t_ok, b + 1)
                if b > 1:
                    dve.wait_ge(p_h_ok, KD * (b - 1))
                nc.vector.scalar_tensor_tensor(n_c[:], n_t[:], 3.0, n_r[:], ALU.subtract, ALU.mult)\
                    .then_inc(x_c_ok, 1)

            def h_make():
                x_correction(0)
                dve.wait_ge(x_c_ok, 1)
                c = n_c[:].rearrange("p a n -> p (a n)")

                def low(k):
                    dve.wait_ge(h_hi_ok, k + 1)
                    nc.vector.tensor_tensor(h_lo[0][:, k, :], h[:, k % 2, :],
                                            h_hi[0][:, k, :].bitcast(F32), ALU.subtract).then_inc(h_lo_ok, 1)

                for k in range(KD):
                    if k > 1:
                        dve.wait_ge(h_lo_ok, k - 1)
                    nc.vector.scalar_tensor_tensor(h[:, k % 2, :], x_raw[:, k, :], g_x[:, k:k + 1], c,
                                                   ALU.mult, ALU.mult).then_inc(h_ok, 1)
                    if k:
                        low(k - 1)
                low(KD - 1)

            nc.vector.memset(eps[:], EPS).then_inc(eps_ok, 1)
            dve.wait_ge(const_ld, 4 * 16)
            for out, src, by in ((g_x[:], g_in[:, 0:KD], -0.5), (g_q[:, 0:1], g_in[:, KD:KD + 1], -0.5 * SCALE),
                                 (g_q[:, 1:2], g_in[:, KD + 1:KD + 2], -0.5),
                                 (g_r[:, 0:1], g_in[:, KD + 2:KD + 3], SCALE),
                                 (g_r[:, 1:2], g_in[:, KD + 3:KD + 4], 1.0)):
                nc.vector.tensor_scalar(out, src, by, None, ALU.mult).then_inc(gains_ok, 1)
            nc.vector.tensor_scalar(head_ones_r[:], head_ones_sb[:], 1.0, None, ALU.mult).then_inc(gains_ok, 1)
            dve.wait_ge(gains_ok, 6)
            dve.wait_ge(eps_ok, 1)
            for s in range(2):
                split_lo(s, 0)
            h_make()
            for b in range(N_BLOCKS):
                m0 = 2 * b * NORMS

                def qk(i):
                    g, n, m_ = b * PAIRS + i, b * NORMS + 2 * i, m0 + 4 * i
                    square_low(0, n)
                    square_low(1, n)
                    norm(0, 0, g, n, m_)
                    split_lo(0, g + 1)
                    square_low(0, n + 1)
                    norm(0, 1, g, n, m_ + 1)
                    square_low(1, n + 1)
                    norm(1, 0, g, n + 1, m_ + 2)
                    split_lo(1, g + 1)
                    norm(1, 1, g, n + 1, m_ + 3)

                loop(nc.vector, b, QK_PAIRS, qk)
                if b < LAST:
                    x_correction(b + 1)
                dve.wait_ge(cs_ld, 32 * (b + 1))

                def rv(i, gain, prefetch):
                    g, n, r = b * PAIRS + QK_PAIRS + i, b * NORMS + 2 * QK_PAIRS + i, b * RV_PAIRS + i
                    m_ = m0 + 4 * QK_PAIRS + 2 * i
                    square_low(0, n)
                    rotate(0, g, r)
                    square_low(1, n)
                    norm_rotary(0, g, n, m_, r)
                    if prefetch:
                        split_lo(0, g + 1)
                    rotate(1, g, r)
                    norm_rotary(1, g, n, m_ + 1, r)
                    value(0, g, r)
                    if prefetch:
                        split_lo(1, g + 1)
                    value(1, g, r)

                rv_loop(nc.vector, b, rv)

        @block.gpsimd
        def _(pool):
            for b in range(1, N_BLOCKS):
                done, out = KD * (b - 1), b % 2
                pool.wait_ge(x_ld, 16 * b)
                if b == 1:
                    pool.wait_ge(x_part_ok, KD - 1)
                    pool.wait_ge(x_ms_ok, 1)
                else:
                    pool.wait_ge(x_ms_ok, b)
                for k in range(KD):
                    if k > 1:
                        pool.wait_ge(p_sum_ok, (KD - 1) * (b - 1) + k - 1)
                    square = x_sq[:, k % 2, :] if k else x_ssq[:]
                    nc.gpsimd.tensor_tensor(square, x_raw[:, k, :], x_raw[:, k, :], ALU.mult)\
                        .then_inc(p_sq_ok, 1)
                    if k:
                        pool.wait_ge(p_sq_ok, done + k + 1)
                        nc.gpsimd.tensor_tensor(x_ssq[:], x_ssq[:], x_sq[:, k % 2, :], ALU.add).then_inc(p_sum_ok, 1)
                pool.wait_ge(x_c_ok, b + 1)
                c = n_c[:].rearrange("p a n -> p (a n)")
                for k in range(KD):
                    if k:
                        pool.wait_ge(p_lo_ok, done + k)
                    else:
                        pool.wait_ge(p_sum_ok, (KD - 1) * b)
                    nc.gpsimd.tensor_scalar(x_sq[:, 0, :], x_raw[:, k, :], g_x[:, k:k + 1], None, ALU.mult)\
                        .then_inc(p_g_ok, 1)
                    pool.wait_ge(p_g_ok, done + k + 1)
                    nc.gpsimd.tensor_tensor(h[:, 0, :], x_sq[:, 0, :], c, ALU.mult).then_inc(p_h_ok, 1)
                    pool.wait_ge(p_h_ok, done + k + 1)
                    nc.gpsimd.tensor_scalar(h_hi[out][:, k, :], h[:, 0, :], 1.0, None, ALU.mult).then_inc(p_hi_ok, 1)
                    pool.wait_ge(p_hi_ok, done + k + 1)
                    nc.gpsimd.tensor_tensor(h_lo[out][:, k, :], h[:, 0, :], h_hi[out][:, k, :].bitcast(F32),
                                            ALU.subtract).then_inc(p_lo_ok, 1)



def attend(nc, q_a, k_a, qk_b, v_all, ka_cache, kb_cache, va_cache, vb_cache, rel_rows, sinks, ident, oT):
    TILES = SEQ // P
    UNITS, A_UNITS = 12, HEADS
    FULL = 5
    NEAR = 2 * P
    HALF = FULL * P // 2
    LOOP = FULL + 1
    KEYS = SEQ + 2 * P
    KV_A, KV_B = HEADS, 2
    NKEY = KV_A + KV_B
    PAIRS_A, PAIRS_B = 4, 4
    V_FEATURES = PAIRS_A * P + P
    CLEARED = 11
    with ExitStack() as ctx:
        m = Memory(nc, ctx, "attend")
        keys = m.sbuf("keys", [P, NKEY, KEYS], F32R)
        v = m.sbuf("v", [P, TILES + 2, V_FEATURES])
        raw = m.sbuf("raw", [P, HEADS + NKEY, P])
        raw_b = m.sbuf("raw_b", [P, HEADS, P])
        raw_cache = m.sbuf("raw_cache", [P, NKEY, P])
        q_hi = m.sbuf("q_hi", [P, 2 * HEADS, P], F32R)
        q_lo = m.sbuf("q_lo", [P, 2 * HEADS, P], F32R)
        bias = m.sbuf("bias", [P, HEADS, NEAR])
        far = m.sbuf("far", [P, HEADS, 2])
        sink = m.sbuf("sink", [1, HEADS])
        sink_part = m.sbuf("sink_part", [1, 3, HEADS], BF16)
        sink_rest = m.sbuf("sink_rest", [1, 2, HEADS])
        mask_q = m.sbuf("mask_q", [P, P], BF16)
        mask_k = m.sbuf("mask_k", [P, HEADS, NEAR + 1], BF16)
        ident_sb = m.sbuf("ident", [P, P])
        prob = [m.sbuf(f"prob{i}", [P, FULL * P]) for i in range(2)]
        prob_t = [m.sbuf(f"prob_t{i}", [P, FULL * P]) for i in range(2)]
        nmax = [m.sbuf(f"nmax{i}", [P, 2]) for i in range(2)]
        den = [m.sbuf(f"den{i}", [P, 2]) for i in range(4)]
        rden = [m.sbuf(f"rden{i}", [P, 2]) for i in range(2)]
        o = m.sbuf("o", [P, 2 * HEADS, HEAD])
        o_t = [m.sbuf(f"o_t{i}", [P, KD // 2, P]) for i in range(2)]
        s_ps = [m.psum(f"s{i}", [P, 2, 512]) for i in range(2)]
        t_ps = m.psum("t", [P, 1024])
        ot_ps = t_ps[:, 512:1024]
        o_ps = [m.psum(f"o{i}", [P, 512]) for i in range(2)]

        ld, ld_b, const_ld, cache_ld = m.sem("ld"), m.sem("ld_b"), m.sem("const_ld"), m.sem("cache_ld")
        bias_ld = m.sem("bias_ld")
        sink_ok, sink_set = m.sem("sink_ok"), m.sem("sink_set")
        zero_ok, bias_sub, bias_set, k0_hi, k0_ok = (
            m.sem(n) for n in ("zero_ok", "bias_sub", "bias_set", "k0_hi", "k0_ok"))
        hi_ok, hi_b_ok, lo_ok, lo_b_ok = (m.sem(n) for n in ("hi_ok", "hi_b_ok", "lo_ok", "lo_b_ok"))
        s_ok, biased, max_ok, exp_ok, t_ok, t_act, t_dve, pv_ok, rden_ok, o_ok = (
            m.sem(n) for n in ("s_ok", "biased", "max_ok", "exp_ok", "t_ok", "t_act", "t_dve", "pv_ok", "rden_ok", "o_ok"))
        ot_ok, ot_out, o_st = ([m.sem(f"{n}_{x}") for x in "ab"] for n in ("ot_ok", "ot_out", "o_st"))

        def window(n, mixer):
            if isinstance(n, int) and n == 0:
                return SEQ, 2 * P
            w = FULL if mixer == "a" else 2
            if isinstance(n, int):
                w = min(n, w)
            return (n - w) * P, w * P

        def first_tile(n, mixer):
            return TILES if isinstance(n, int) and n == 0 else n - window(n, mixer)[1] // P

        def before(n, u, by=1):
            return (n, u - by) if u >= by else (n - 1, u + UNITS - by)

        def is_whole(n, u):
            return u < A_UNITS and window(n, "a")[1] == FULL * P

        def whole_before(n, u):
            return 0 if isinstance(n, int) and n < FULL else A_UNITS * (n - FULL) + min(u, A_UNITS)

        def scores_of(n, u):
            ps, sb = s_ps[u % 2], prob[u % 2]
            halves = sb[:].rearrange("p (a n) -> p a n", a=2)
            if is_whole(n, u):
                return ps[:, :, 0:HALF], halves
            w = window(n, "a" if u < A_UNITS else "b")[1]
            if u < A_UNITS:
                return ps[:, 0, 0:w], sb[:, 0:w]
            return ps[:, :, 0:w + 1], halves[:, :, 0:w + 1]

        def prob_blocks(n, u):
            if u < A_UNITS:
                return [j * P for j in range(window(n, "a")[1] // P)]
            return [i * HALF + j * P for i in range(2) for j in range(window(n, "b")[1] // P)]

        def run(eng, step, last):
            for n in range(LOOP):
                for u in range(UNITS):
                    step(n, u)
            with eng.Fori(LOOP, TILES + 1) as n:
                for u in range(UNITS):
                    step(n, u)
            last()

        block = ctx.enter_context(nc.Block())

        @block.sync
        def _(sp):
            by_heads = "f (a p) n -> p (f a) n"

            def twice(dst, src, sem):
                for i in range(2):
                    sp.dma_start(dst[i * HEAD:(i + 1) * HEAD], src).then_inc(sem, 16)

            def load(n):
                c, w = (SEQ, DEC) if isinstance(n, int) and n == 0 else ((n - 1) * P, P)
                tile = TILES + 1 if isinstance(n, int) and n == 0 else n - 1
                twice(raw[:, 0:HEADS, 0:w], q_a[:, :, ds(c, w)].rearrange(by_heads, p=HEAD), ld)
                twice(raw[:, HEADS:HEADS + KV_A, 0:w], k_a[:, :, ds(c, w)].rearrange(by_heads, p=HEAD), ld)
                twice(raw[:, HEADS + KV_A:, 0:w], qk_b[PAIRS_B:, :, ds(c, w)].rearrange(by_heads, p=HEAD), ld)
                sp.dma_start(v[0:w, ds(tile, 1), :].rearrange("p a f -> p (a f)"), v_all[ds(c, w), :]).then_inc(ld, 16)

            def load_b(n):
                c, w = (SEQ, DEC) if isinstance(n, int) and n == 0 else ((n - 1) * P, P)
                twice(raw_b[:, :, 0:w], qk_b[0:PAIRS_B, :, ds(c, w)].rearrange(by_heads, p=HEAD), ld_b)

            def store(n, mixer):
                c, w = (SEQ, DEC) if isinstance(n, int) and n == 0 else ((n - 1) * P, P)
                sp.wait_ge(ot_out[mixer], n + 1)
                half = slice(mixer * KD // 2, (mixer + 1) * KD // 2)
                sp.dma_start(oT[half, :, ds(c, w)].rearrange("k p n -> p k n"), o_t[mixer][:, :, 0:w])\
                    .then_inc(o_st[mixer], 16)

            load(0)
            twice(raw_cache[:, 0:KV_A, :], ka_cache.rearrange(by_heads, p=HEAD), cache_ld)
            twice(raw_cache[:, KV_A:, :], kb_cache.rearrange("(a p) n -> p a n", p=HEAD), cache_ld)
            sp.dma_start(ident_sb[:], ident).then_inc(const_ld, 16)
            sp.dma_start(sink[:], sinks.rearrange("(a n) -> a n", a=1)).then_inc(const_ld, 16)
            sp.dma_start(v[:, TILES, 0:PAIRS_A * P], va_cache).then_inc(const_ld, 16)
            sp.dma_start(v[:, TILES, PAIRS_A * P:], vb_cache).then_inc(const_ld, 16)
            load_b(0)
            for n in range(LOOP - 1):
                sp.wait_ge(lo_ok, 2 * (n + 1))
                load(n + 1)
                if n:
                    store(n - 1, 1)
                sp.wait_ge(lo_b_ok, n + 1)
                load_b(n + 1)
                store(n, 0)
            with sp.Fori(LOOP - 1, TILES) as n:
                sp.wait_ge(lo_ok, 2 * (n + 1))
                load(n + 1)
                store(n - 1, 1)
                sp.wait_ge(lo_b_ok, n + 1)
                load_b(n + 1)
                store(n, 0)
            store(TILES - 1, 1)
            store(TILES, 0)
            store(TILES, 1)
            for mixer in range(2):
                sp.wait_ge(o_st[mixer], 16 * (TILES + 1))

        @block.gpsimd
        def _(pool):
            for done, (out, value) in enumerate((
                    (raw[:, :, DEC:], 0.0), (raw_b[:, :, DEC:], 0.0), (mask_q[:], 0.0), (mask_k[:], 0.0),
                    (mask_q[0:1, CHUNK:], 1.0), (mask_q[32:33, 0:CHUNK], 1.0),
                    (mask_q[64:65, :], 1.0), (mask_q[96:97, :], 1.0),
                    (mask_k[0:1, :, 0:CHUNK], NEG), (mask_k[32:33, :, NEAR - CHUNK:NEAR], NEG), (v[DEC:, TILES + 1, :], 0.0))):
                if done:
                    pool.wait_ge(zero_ok, done)
                nc.gpsimd.memset(out, value).then_inc(zero_ok, 1)
            low = slice(HEAD, P)

            pool.wait_ge(zero_ok, CLEARED)

            def split(n):
                if not isinstance(n, int) or n:
                    pool.wait_ge(lo_b_ok, n)
                pool.wait_ge(hi_ok, 2 * n + 1)
                c = SEQ + P if isinstance(n, int) and n == 0 else (n - 1) * P
                nc.gpsimd.tensor_tensor(keys[low, :, ds(c, P)], raw[low, HEADS:, :], keys[low, :, ds(c, P)].bitcast(F32),
                                        ALU.subtract).then_inc(lo_ok, 1)
                pool.wait_ge(lo_ok, 2 * n + 1)
                pool.wait_ge(hi_ok, 2 * n + 2)
                nc.gpsimd.tensor_tensor(q_lo[:, 0:HEADS, :], raw[:, 0:HEADS, :], q_hi[:, 0:HEADS, :].bitcast(F32),
                                        ALU.subtract).then_inc(lo_ok, 1)

            def split_b(n):
                pool.wait_ge(lo_ok, 2 * n + 2)
                pool.wait_ge(hi_b_ok, n + 1)
                nc.gpsimd.tensor_tensor(q_lo[:, HEADS:, :], raw_b[:], q_hi[:, HEADS:, :].bitcast(F32), ALU.subtract)\
                    .then_inc(lo_b_ok, 1)

            split_b(0)
            for n in range(1, LOOP):
                split(n)
                split_b(n)
            with nc.gpsimd.Fori(LOOP, TILES + 1) as n:
                split(n)
                split_b(n)

        @block.tensor
        def _(pe):
            def scores(n, u):
                if u == 0:
                    pe.wait_ge(lo_ok, 2 * (n + 1))
                if u == A_UNITS:
                    pe.wait_ge(lo_b_ok, n + 1)
                k = UNITS * n + u
                if not isinstance(n, int) or k > 1:
                    pe.wait_ge(exp_ok, k - 1)
                ps = s_ps[u % 2]
                c, w = window(n, "a" if u < A_UNITS else "b")
                if is_whole(n, u):
                    parts = [(0, u, u, 0, HALF), (1, u, u, HALF, HALF)]
                elif u < A_UNITS:
                    parts = [(0, u, u, 0, w)]
                else:
                    parts = [(i, 2 * u - A_UNITS + i, KV_A + i, 0, w) for i in range(2)]
                for bank, query, key, first, width in parts:
                    begun = False
                    if u >= A_UNITS:
                        head = 2 * (u - A_UNITS) + bank
                        nc.tensor.matmul(ps[:, bank, 0:w + 1], mask_q[:], mask_k[:, head, NEAR - w:], start=True,
                                         stop=False, skip_group_check=True)
                        begun = True
                    elif is_whole(n, u) and bank == 0:
                        nc.tensor.matmul(ps[:, 0, 0:CHUNK], mask_q[:], mask_k[:, 0, 0:CHUNK], start=True, stop=False,
                                         skip_group_check=True)
                        begun = True
                    for q in (q_hi, q_lo):
                        last = nc.tensor.matmul(ps[:, bank, 0:width], q[:, query, :], keys[:, key, ds(c + first, width)],
                                                start=q is q_hi and not begun, stop=q is q_lo, skip_group_check=begun)
                last.then_inc(s_ok, 1)

            def transposes(n, u):
                k = UNITS * n + u
                pe.wait_ge(exp_ok, k + 1)
                if not isinstance(n, int) or k:
                    pe.wait_ge(t_act, k)
                for j, first in enumerate(prob_blocks(n, u)):
                    if j == FULL - 1:
                        if u == 0:
                            pe.wait_ge(ot_out[0], n)
                        elif u == 3:
                            pe.wait_ge(ot_out[1], n)
                        else:
                            pe.wait_ge(t_dve, whole_before(n, u))
                    last = nc.tensor.transpose(t_ps[:, j * P:(j + 1) * P], prob[u % 2][:, first:first + P], ident_sb[:])
                last.then_inc(t_ok, 1)

            def values(n, u):
                k = UNITS * n + u
                pe.wait_ge(t_act, k + 1)
                if is_whole(n, u):
                    pe.wait_ge(t_dve, whole_before(n, u) + 1)
                if not isinstance(n, int) or k > 1:
                    pe.wait_ge(o_ok, k - 1)
                mixer = "a" if u < A_UNITS else "b"
                tile, w = first_tile(n, mixer), window(n, mixer)[1] // P
                pair = u // 2 if u < A_UNITS else PAIRS_A
                for head in range(1 if u < A_UNITS else 2):
                    for j in range(w):
                        src = (head * w + j) * P
                        last = nc.tensor.matmul(
                            o_ps[u % 2][:, head * P:(head + 1) * P], prob_t[u % 2][:, src:src + P],
                            v[:, ds(tile + j, 1), pair * P:(pair + 1) * P].rearrange("p a f -> p (a f)"),
                            start=(j == 0), stop=(j == w - 1))
                last.then_inc(pv_ok, 1)

            def output(n, mixer):
                if mixer:
                    pe.wait_ge(o_ok, UNITS * (n + 1))
                    if isinstance(n, int) and n == TILES:
                        pe.wait_ge(ot_out[0], n + 1)
                    elif isinstance(n, int) and n + 1 < FULL:
                        pe.wait_ge(ot_out[0], n + 1)
                    else:
                        pe.wait_ge(t_dve, whole_before(n + 1, 3))
                else:
                    pe.wait_ge(o_ok, UNITS * n + A_UNITS)
                    if not isinstance(n, int) or n >= FULL:
                        pe.wait_ge(t_dve, whole_before(n, A_UNITS))
                    elif n:
                        pe.wait_ge(ot_out[1], n)
                for k in range(KD // 2):
                    heads = slice(HEADS * mixer + 2 * k, HEADS * mixer + 2 * k + 2)
                    last = nc.tensor.transpose(ot_ps[:, k * P:(k + 1) * P],
                                               o[:, heads, :].rearrange("p a f -> p (a f)"), ident_sb[:])
                last.then_inc(ot_ok[mixer], 1)

            def step(n, u):
                first = isinstance(n, int) and n == 0
                scores(n, u)
                if u == 4 and not first:
                    output(n - 1, 1)
                if first and u == 1:
                    pe.wait_ge(const_ld, 4 * 16)
                    pe.wait_ge(zero_ok, CLEARED)
                if first and u == A_UNITS - 1:
                    pe.wait_ge(sink_set, 4)
                if not (first and u < 3):
                    values(*before(n, u, 3))
                if not (first and u < 1):
                    transposes(*before(n, u))
                if u == 11:
                    output(n, 0)

            def last():
                values(TILES, UNITS - 3)
                transposes(TILES, UNITS - 1)
                values(TILES, UNITS - 2)
                values(TILES, UNITS - 1)
                output(TILES, 1)

            pe.wait_ge(k0_ok, 1)
            run(pe, step, last)

        @block.scalar
        def _(act):
            nc.scalar.preload_act_table_set("natural_log_exp_and_others")

            def split_keys(n):
                c = SEQ + P if isinstance(n, int) and n == 0 else (n - 1) * P
                nc.scalar.activation(keys[:, :, ds(c, P)], raw[:, HEADS:, :], ACT.Copy).then_inc(hi_ok, 1)

            def split_a(n):
                if not isinstance(n, int) or n:
                    act.wait_ge(s_ok, UNITS * (n - 1) + A_UNITS)
                nc.scalar.activation(q_hi[:, 0:HEADS, :], raw[:, 0:HEADS, :], ACT.Copy).then_inc(hi_ok, 1)

            def split_b(n):
                act.wait_ge(ld_b, 2 * 16 * (n + 1))
                if not isinstance(n, int) or n:
                    act.wait_ge(s_ok, UNITS * n)
                nc.scalar.activation(q_hi[:, HEADS:, :], raw_b[:], ACT.Copy).then_inc(hi_b_ok, 1)

            def exps(n, u):
                k = UNITS * n + u
                ps, sb = scores_of(n, u)
                if not isinstance(n, int) or k > 1:
                    act.wait_ge(t_ok, k - 1)
                if not isinstance(n, int) or k > 3:
                    act.wait_ge(o_ok, k - 3)
                act.wait_ge(max_ok, k + 1)
                if u < A_UNITS:
                    nc.scalar.activation(sb, ps, ACT.Exp, bias=nmax[u % 2][:, 0:1], accum_out=den[u % 4][:, 0:1])\
                        .then_inc(exp_ok, 1)
                else:
                    for i in range(2):
                        last = nc.scalar.activation(sb[:, i, :], ps[:, i, :], ACT.Exp, bias=nmax[u % 2][:, i:i + 1],
                                                    accum_out=den[u % 4][:, i:i + 1])
                    last.then_inc(exp_ok, 1)

            def copy_t(n, u):
                k = UNITS * n + u
                if not isinstance(n, int) or k > 1:
                    act.wait_ge(pv_ok, k - 1)
                act.wait_ge(t_ok, k + 1)
                w = min(512, P * len(prob_blocks(n, u)))
                nc.scalar.activation(prob_t[u % 2][:, 0:w], t_ps[:, 0:w], ACT.Copy).then_inc(t_act, 1)

            def step(n, u):
                first = isinstance(n, int) and n == 0
                exps(n, u)
                prefetch = not (isinstance(n, int) and n == TILES)
                if u == 5 and prefetch:
                    act.wait_ge(ld, 7 * 16 * (n + 2))
                if not (first and u < 1):
                    copy_t(*before(n, u))
                if u == 5 and prefetch:
                    split_keys(n + 1)
                if u == 3:
                    split_b(n)
                if u == 8 and prefetch:
                    split_a(n + 1)

            row = rel_rows.shape[1] * rel_rows.shape[2]
            nc.scalar.dma_start(bias[:], bass.AP(rel_rows.tensor, P - 1, [[row - 1, P], [rel_rows.shape[2], HEADS], [1, NEAR]]))\
                .then_inc(bias_ld, 16)
            nc.scalar.dma_start(far[:], rel_rows[:, :, 0:2]).then_inc(bias_ld, 16)
            act.wait_ge(zero_ok, 2)
            act.wait_ge(ld, 7 * 16)
            split_keys(0)
            split_a(0)
            act.wait_ge(cache_ld, 64)
            nc.scalar.activation(keys[:, :, SEQ:SEQ + P], raw_cache[:], ACT.Copy).then_inc(k0_hi, 1)
            for n in range(LOOP):
                for u in range(UNITS):
                    step(n, u)
            with nc.scalar.Fori(LOOP, TILES) as n:
                for u in range(UNITS):
                    step(n, u)
            for u in range(UNITS):
                step(TILES, u)
            copy_t(TILES, UNITS - 1)

        @block.vector
        def _(dve):
            def add_bias(n, u):
                dve.wait_ge(s_ok, UNITS * n + u + 1)
                if u < A_UNITS:
                    w = window(n, "a")[1]
                    near = min(w, NEAR)
                    at = s_ps[u % 2][:, 1, HALF - NEAR:HALF] if is_whole(n, u) else s_ps[u % 2][:, 0, w - near:w]
                    nc.vector.tensor_tensor(at, at, bias[:, u, NEAR - near:], ALU.add).then_inc(biased, 1)

            def maxima(n, u):
                ps, _ = scores_of(n, u)
                if u < A_UNITS:
                    dve.wait_ge(biased, A_UNITS * n + u + 1)
                    axis = AX.XY if is_whole(n, u) else AX.X
                    nc.vector.tensor_reduce(nmax[u % 2][:, 0:1], ps, axis, ALU.max, negate=True).then_inc(max_ok, 1)
                else:
                    nc.vector.tensor_reduce(nmax[u % 2][:], ps, AX.X, ALU.max, negate=True).then_inc(max_ok, 1)

            def invert(n, u):
                k = UNITS * n + u
                if not isinstance(n, int) or k > 1:
                    dve.wait_ge(o_ok, k - 1)
                dve.wait_ge(exp_ok, k + 1)
                heads = 1 if u < A_UNITS else 2
                nc.vector.reciprocal(rden[u % 2][:, 0:heads], den[u % 4][:, 0:heads]).then_inc(rden_ok, 1)

            def copy_t(n, u):
                if is_whole(n, u):
                    dve.wait_ge(pv_ok, UNITS * n + u - 1)
                    dve.wait_ge(t_ok, UNITS * n + u + 1)
                    nc.vector.tensor_copy(prob_t[u % 2][:, 512:], t_ps[:, 512:FULL * P]).then_inc(t_dve, 1)

            def copy_o(n, mixer):
                if not isinstance(n, int) or n:
                    dve.wait_ge(o_st[mixer], 16 * n)
                dve.wait_ge(ot_ok[mixer], n + 1)
                nc.vector.tensor_copy(o_t[mixer][:].rearrange("p k n -> p (k n)"), ot_ps)\
                    .then_inc(ot_out[mixer], 1)

            def divide(n, u):
                k = UNITS * n + u
                dve.wait_ge(pv_ok, k + 1)
                if not isinstance(n, int) or n:
                    dve.wait_ge(ot_ok[u // A_UNITS], n)
                dve.wait_ge(rden_ok, k + 1)
                if u < A_UNITS:
                    nc.vector.tensor_scalar(o[:, u, :], o_ps[u % 2][:, u % 2 * HEAD:(u % 2 + 1) * HEAD],
                                            rden[u % 2][:, 0:1], None, ALU.mult).then_inc(o_ok, 1)
                else:
                    pair_out = o_ps[u % 2][:, 0:6 * HEAD].rearrange("p (a f) -> p a f", f=3 * HEAD)[:, :, 0:HEAD]
                    nc.vector.tensor_tensor(o[:, HEADS + u - A_UNITS::PAIRS_B, :], pair_out, rden[u % 2][:].unsqueeze(2).broadcast_to([P, 2, HEAD]),
                                            ALU.mult).then_inc(o_ok, 1)

            def split_first():
                dve.wait_ge(hi_ok, 1)
                new = slice(SEQ + P, KEYS)
                nc.vector.tensor_tensor(keys[HEAD:, :, new], raw[HEAD:, HEADS:, :], keys[HEAD:, :, new].bitcast(F32),
                                        ALU.subtract).then_inc(lo_ok, 1)
                dve.wait_ge(hi_ok, 2)
                nc.vector.tensor_tensor(q_lo[:, 0:HEADS, :], raw[:, 0:HEADS, :], q_hi[:, 0:HEADS, :].bitcast(F32),
                                        ALU.subtract).then_inc(lo_ok, 1)

            def set_sinks():
                dve.wait_ge(const_ld, 4 * 16)
                rest = sink[:]
                for part in range(3):
                    if part:
                        before_rest, rest = rest, sink_rest[:, part - 1, :]
                        nc.vector.tensor_tensor(rest, before_rest, sink_part[:, part - 1, :], ALU.subtract).then_inc(sink_ok, 1)
                        dve.wait_ge(sink_ok, 2 * part)
                    nc.vector.tensor_scalar(sink_part[:, part, :], rest, 1.0, None, ALU.mult).then_inc(sink_ok, 1)
                    dve.wait_ge(sink_ok, 2 * part + 1)
                dve.wait_ge(zero_ok, CLEARED)
                for row, part in ((64, 0), (96, 1), (0, 2), (32, 2)):
                    nc.vector.tensor_scalar(mask_k[row:row + 1, :, NEAR], sink_part[:, part, :], 1.0, None, ALU.mult)\
                        .then_inc(sink_set, 1)

            def step(n, u):
                first = isinstance(n, int) and n == 0
                if first and u == 5:
                    set_sinks()
                if u == 4 and not first:
                    copy_o(n - 1, 1)
                add_bias(n, u)
                if not (first and u < 2):
                    invert(*before(n, u, 2))
                maxima(n, u)
                if not (first and u < 3):
                    divide(*before(n, u, 3))
                if not (first and u < 1):
                    copy_t(*before(n, u))
                if u == UNITS - 1:
                    copy_o(n, 0)

            dve.wait_ge(bias_ld, 2 * 16)
            for h in range(HEADS):
                nc.vector.tensor_scalar(bias[:, h, :], bias[:, h, :], far[:, h, 0:1], None, ALU.subtract)\
                    .then_inc(bias_sub, 1)
            dve.wait_ge(bias_sub, HEADS)
            nc.vector.memset(bias[0:CHUNK, :, NEAR - CHUNK:], NEG).then_inc(bias_set, 1)
            dve.wait_ge(bias_set, 1)
            split_first()
            dve.wait_ge(k0_hi, 1)
            nc.vector.tensor_tensor(keys[HEAD:, :, SEQ:SEQ + P], raw_cache[HEAD:, :, :],
                                    keys[HEAD:, :, SEQ:SEQ + P].bitcast(F32), ALU.subtract).then_inc(k0_ok, 1)
            for n in range(LOOP):
                for u in range(UNITS):
                    step(n, u)
            with nc.vector.Fori(LOOP, TILES + 1) as n:
                for u in range(UNITS):
                    step(n, u)
            invert(TILES, UNITS - 2)
            divide(TILES, UNITS - 3)
            invert(TILES, UNITS - 1)
            copy_t(TILES, UNITS - 1)
            divide(TILES, UNITS - 2)
            divide(TILES, UNITS - 1)
            copy_o(TILES, 1)


def combine(nc, oT, xT, w_o, gains, all_ones, x1T, h2T):
    PAIRS = KD // 2
    LAST = N_BLOCKS - 1
    NORMED = (None, (0, 2), (2, 5), (5, 8))
    RING = 3
    with ExitStack() as ctx:
        m = Memory(nc, ctx, "combine")
        o_raw = [m.sbuf(f"o_raw{i}", [P, 2, BLOCK]) for i in range(2)]
        o_hi = [m.sbuf(f"o_hi{i}", [P, KD, BLOCK], F32R) for i in range(2)]
        o_lo = [m.sbuf(f"o_lo{i}", [P, KD, BLOCK], F32R) for i in range(2)]
        x1 = [m.sbuf(f"x1{i}", [P, KD, BLOCK]) for i in range(2)]
        x_sq = [m.sbuf(f"x_sq{i}", [P, BLOCK]) for i in range(2)]
        ssq = [m.sbuf(f"ssq{i}", [P, BLOCK]) for i in range(2)]
        n_t = m.sbuf("n_t", [P, SUBS, SUB])
        n_r = m.sbuf("n_r", [P, SUBS, SUB])
        n_r2 = m.sbuf("n_r2", [P, SUBS, SUB])
        n_c = m.sbuf("n_c", [P, SUBS, SUB])
        h2 = [m.sbuf(f"h2{i}", [P, BLOCK]) for i in range(RING)]
        w_raw = [m.sbuf(f"w_raw{s}", [P, KD, P]) for s in range(2)]
        w_hi = [m.sbuf(f"w_hi{s}", [P, KD, P], F32R) for s in range(2)]
        w_lo = [m.sbuf(f"w_lo{s}", [P, KD, P], F32R) for s in range(2)]
        g_in = m.sbuf("g_in", [P, KD])
        g_x = m.sbuf("g_x", [P, KD])
        eps = m.sbuf("eps", [P, 1])
        ones_sb = m.sbuf("ones", [P, P])
        z = [[m.psum(f"z{s}{i}", [P, 512]) for i in range(2)] for s in range(2)]
        ms = m.psum("ms", [P, SUBS, 512])

        const_ld = m.sem("const_ld")
        o_ld, w_ld = ([m.sem(f"{n}{i}") for i in range(2)] for n in ("o_ld", "w_ld"))
        x_ld = [m.sem(f"x_ld{c}") for c in range(PAIRS)]
        w_hi_ok, w_lo_ok = ([m.sem(f"{n}{s}") for s in range(2)] for n in ("w_hi_ok", "w_lo_ok"))
        z_ok = [[m.sem(f"z_ok{s}{i}") for i in range(2)] for s in range(2)]
        x1_ok = [[m.sem(f"x1_ok{s}{i}") for i in range(2)] for s in range(2)]
        o_hi_ok, o_lo_ok = m.sem("o_hi_ok"), m.sem("o_lo_ok")
        eps_ok, gains_ok = m.sem("eps_ok"), m.sem("gains_ok")
        sq_ok, sum_ok, ms_ok = m.sem("sq_ok"), m.sem("sum_ok"), m.sem("ms_ok")
        ln_ok, r_ok, r2_ok, t_ok, c_ok = (m.sem(n) for n in ("ln_ok", "r_ok", "r2_ok", "t_ok", "c_ok"))
        h2_ok, x1_st = m.sem("h2_ok"), m.sem("x1_st")
        h2_st = [m.sem(f"h2_st{i}") for i in range(RING)]
        steps = [(b, i) for b in range(N_BLOCKS) for i in range(PAIRS)]

        def h2_at(b, k):
            return x1[(b + 1) % 2][:, k, :] if b == LAST else h2[(KD * b + k) % RING][:]

        block = ctx.enter_context(nc.Block())

        @block.sync
        def _(sp):
            def cols(b):
                return slice(b * BLOCK, (b + 1) * BLOCK)

            def load_w(g):
                for s in range(2):
                    if g:
                        sp.wait_ge(w_lo_ok[s], g)
                    sp.dma_start(w_raw[s][:], w_o[g % PAIRS, s]).then_inc(w_ld[s], 16)

            def load_o(b, q):
                n = PAIRS * b + q
                if n > 1:
                    sp.wait_ge(o_lo_ok, 2 * (n - 1))
                sp.dma_start(o_raw[n % 2][:], oT[2 * q:2 * q + 2, :, cols(b)].rearrange("k p n -> p k n"))\
                    .then_inc(o_ld[n % 2], 16)

            def load_x(b, c):
                part = slice(2 * c, 2 * c + 2)
                sp.dma_start(x1[b % 2][:, part, :], xT[part, :, cols(b)].rearrange("k p n -> p k n")).then_inc(x_ld[c], 16)

            def store_x1(b, i):
                for s in range(2):
                    for j in range(SUBS):
                        sp.wait_ge(x1_ok[s][j], PAIRS * b + i + 1)
                part = slice(2 * i, 2 * i + 2)
                sp.dma_start(x1T[part, :, cols(b)].rearrange("k p n -> p k n"), x1[b % 2][:, part, :]).then_inc(x1_st, 16)

            def store_h2(b, k):
                n = KD * b + k
                sp.wait_ge(h2_ok, n + 1)
                sp.dma_start(h2T[k, :, cols(b)], h2_at(b, k)).then_inc(h2_st[n % RING], 16)

            load_o(0, 0)
            load_w(0)
            load_o(0, 1)
            sp.dma_start(g_in[:], gains).then_inc(const_ld, 16)
            sp.dma_start(ones_sb[:], all_ones).then_inc(const_ld, 16)
            load_o(0, 2)
            load_x(0, 0)
            load_o(0, 3)
            for c in range(1, PAIRS):
                load_x(0, c)
            for b, i in steps:
                g = PAIRS * b + i
                if (b, i) != steps[-1]:
                    load_w(g + 1)
                if b < LAST:
                    load_o(b + 1, i)
                if b or i:
                    store_x1(*((b, i - 1) if i else (b - 1, PAIRS - 1)))
                if b == 0:
                    load_x(1, i)
                elif i:
                    for k in range(*NORMED[i]):
                        store_h2(b - 1, k)
                    if b < LAST:
                        sp.wait_ge(x1_st, 16 * PAIRS * b)
                        for c in (i - 1,) if i < PAIRS - 1 else (i - 1, i):
                            load_x(b + 1, c)
            store_x1(LAST, PAIRS - 1)
            for k in range(KD):
                store_h2(LAST, k)
            sp.wait_ge(x1_st, 16 * PAIRS * N_BLOCKS)
            for i in range(RING):
                sp.wait_ge(h2_st[i], 16 * len(range(i, N_BLOCKS * KD, RING)))

        @block.tensor
        def _(pe):
            def pair(b, i):
                g = b * PAIRS + i
                for s in range(2):
                    pe.wait_ge(w_lo_ok[s], g + 1)
                    for j in range(SUBS):
                        if not isinstance(i, int) or g:
                            pe.wait_ge(x1_ok[s][j], g)
                        cols = slice(j * SUB, (j + 1) * SUB)
                        ready = (lambda k: pe.wait_ge(o_lo_ok, KD * b + k + 1)) if isinstance(i, int) and s == j == 0 else None
                        dense(nc, z[s][j][:, 0:SUB], (lambda k: w_hi[s][:, k, :], lambda k: w_lo[s][:, k, :]),
                              (lambda k: o_hi[b % 2][:, k, cols], lambda k: o_lo[b % 2][:, k, cols]), KD, ready)\
                            .then_inc(z_ok[s][j], 1)

            def mean_square(b):
                pe.wait_ge(sum_ok, (KD - 1) * (b + 1))
                if b:
                    pe.wait_ge(c_ok, b)
                for j in range(SUBS):
                    last = nc.tensor.matmul(ms[:, j, 0:SUB], ones_sb[:], ssq[b % 2][:, j * SUB:(j + 1) * SUB],
                                            start=True, stop=True)
                last.then_inc(ms_ok, 1)

            for b in range(N_BLOCKS):
                pair(b, 0)
                if b == 1:
                    pe.wait_ge(const_ld, 32)
                if b:
                    mean_square(b - 1)
                with pe.Fori(1, PAIRS) as i:
                    pair(b, i)
            mean_square(LAST)

        @block.scalar
        def _(act):
            nc.scalar.preload_act_table_set("natural_log_exp_and_others")

            def split_hi(s, g):
                act.wait_ge(w_ld[s], 16 * (g + 1))
                if g:
                    act.wait_ge(z_ok[s][1], g)
                nc.scalar.activation(w_hi[s][:], w_raw[s][:], ACT.Copy).then_inc(w_hi_ok[s], 1)

            def split_o(b, k):
                n = PAIRS * b + k // 2
                if b > 1:
                    act.wait_ge(z_ok[1][1], PAIRS * (b - 1))
                act.wait_ge(o_ld[n % 2], 16 * (n // 2 + 1))
                nc.scalar.activation(o_hi[b % 2][:, k, :], o_raw[n % 2][:, k % 2, :], ACT.Copy).then_inc(o_hi_ok, 1)

            def square(b, k):
                for j in range(SUBS):
                    act.wait_ge(x1_ok[k % 2][j], PAIRS * b + k // 2 + 1)
                if k == 0:
                    if b > 1:
                        act.wait_ge(ms_ok, b - 1)
                    out = ssq[b % 2]
                else:
                    n = (KD - 1) * b + k - 1
                    if n > 1:
                        act.wait_ge(sum_ok, n - 1)
                    out = x_sq[n % 2]
                nc.scalar.activation(out[:], x1[b % 2][:, k, :], ACT.Square).then_inc(sq_ok, 1)

            def root(b):
                act.wait_ge(ms_ok, b + 1)
                if b:
                    act.wait_ge(c_ok, b)
                nc.scalar.activation(n_t[:], ms[:, :, 0:SUB], ACT.Ln, bias=eps[:, 0:1]).then_inc(ln_ok, 1)
                act.wait_ge(ln_ok, b + 1)
                nc.scalar.activation(n_r[:], n_t[:], ACT.Exp, scale=-0.5).then_inc(r_ok, 1)
                act.wait_ge(r_ok, b + 1)
                nc.scalar.activation(n_r2[:], n_r[:], ACT.Square).then_inc(r2_ok, 1)

            act.wait_ge(eps_ok, 1)
            split_o(0, 0)
            split_hi(0, 0)
            for k in range(1, KD):
                split_o(0, k)
            split_hi(1, 0)
            for b, i in steps:
                for s in range(2):
                    if (b, i) != steps[-1]:
                        split_hi(s, PAIRS * b + i + 1)
                    for k in range(2):
                        if s == 0 and b < LAST:
                            split_o(b + 1, 2 * i + k)
                    square(b, 2 * i + s)
                    if b and (i, s) == (1, 0):
                        root(b - 1)
            root(LAST)

        @block.vector
        def _(dve):
            def split_lo(s, g):
                dve.wait_ge(w_hi_ok[s], g + 1)
                nc.vector.tensor_tensor(w_lo[s][:], w_raw[s][:], w_hi[s][:].bitcast(F32), ALU.subtract)\
                    .then_inc(w_lo_ok[s], 1)

            def split_o(b, k):
                n = PAIRS * b + k // 2
                dve.wait_ge(o_hi_ok, b * KD + k + 1)
                nc.vector.tensor_tensor(o_lo[b % 2][:, k, :], o_raw[n % 2][:, k % 2, :],
                                        o_hi[b % 2][:, k, :].bitcast(F32), ALU.subtract).then_inc(o_lo_ok, 1)

            def add(b, i, s, j):
                if j == 0:
                    dve.wait_ge(x_ld[i], 16 * (b + 1))
                dve.wait_ge(z_ok[s][j], b * PAIRS + i + 1)
                part = x1[b % 2][:, 2 * i + s, j * SUB:(j + 1) * SUB]
                nc.vector.tensor_tensor(part, part, z[s][j][:, 0:SUB], ALU.add).then_inc(x1_ok[s][j], 1)

            def add_square(b, k):
                if k:
                    n = (KD - 1) * b + k - 1
                    if k > 1:
                        dve.wait_ge(sum_ok, n)
                    dve.wait_ge(sq_ok, KD * b + k + 1)
                    nc.vector.tensor_tensor(ssq[b % 2][:], ssq[b % 2][:], x_sq[n % 2][:], ALU.add).then_inc(sum_ok, 1)

            def correction(b):
                dve.wait_ge(r2_ok, b + 1)
                nc.vector.scalar_tensor_tensor(n_t[:], ms[:, :, 0:SUB], eps[:, 0:1], n_r2[:], ALU.add, ALU.mult)\
                    .then_inc(t_ok, 1)
                dve.wait_ge(t_ok, b + 1)
                if b:
                    dve.wait_ge(h2_ok, KD * b)
                nc.vector.scalar_tensor_tensor(n_c[:], n_t[:], 3.0, n_r[:], ALU.subtract, ALU.mult)\
                    .then_inc(c_ok, 1)
                dve.wait_ge(c_ok, b + 1)

            def normed(b, k):
                n = KD * b + k
                if n >= RING and b < LAST:
                    dve.wait_ge(h2_st[n % RING], 16 * (n // RING))
                nc.vector.scalar_tensor_tensor(h2_at(b, k), x1[b % 2][:, k, :], g_x[:, k:k + 1],
                                               n_c[:].rearrange("p a n -> p (a n)"), ALU.mult, ALU.mult)\
                    .then_inc(h2_ok, 1)

            nc.vector.memset(eps[:], EPS).then_inc(eps_ok, 1)
            split_o(0, 0)
            split_lo(0, 0)
            for k in range(1, KD):
                split_o(0, k)
            split_lo(1, 0)
            dve.wait_ge(const_ld, 32)
            nc.vector.tensor_scalar(g_x[:], g_in[:], -0.5, None, ALU.mult).then_inc(gains_ok, 1)
            dve.wait_ge(gains_ok, 1)
            dve.wait_ge(eps_ok, 1)
            for b, i in steps:
                for s in range(2):
                    add(b, i, s, 0)
                    add(b, i, s, 1)
                    if (b, i) != steps[-1]:
                        split_lo(s, PAIRS * b + i + 1)
                    if s == 0:
                        for k in range(2):
                            if b or i:
                                add_square(*((b, 2 * (i - 1) + k) if i else (b - 1, KD - 2 + k)))
                        for k in range(2):
                            if b < LAST:
                                split_o(b + 1, 2 * i + k)
                    if b and i and s == (i == 1):
                        if i == 1:
                            correction(b - 1)
                        for k in range(*NORMED[i]):
                            normed(b - 1, k)
            for s in range(2):
                add_square(LAST, KD - 2 + s)
            correction(LAST)
            dve.wait_ge(x1_st, 16 * PAIRS * LAST)
            for k in range(KD):
                normed(LAST, k)



def ffn(nc, h2T, x1T, w_gu, w_dn, conv, state, yT, gate_prompt, gate_sample):
    F_TILES = D_FF // P
    PARTS = 2
    KF = F_TILES // PARTS
    DOWN = KD // 2
    PAIRS = KF + DOWN
    LAST = N_BLOCKS - 1
    CUT = SEQ - LAST * BLOCK
    H = 2
    with ExitStack() as ctx:
        m = Memory(nc, ctx, "ffn")
        h_raw = [m.sbuf(f"h_raw{i}", [P, BLOCK]) for i in range(2)]
        h_hi = m.sbuf("h_hi", [P, KD, BLOCK], F32R)
        h_lo = m.sbuf("h_lo", [P, KD, BLOCK], F32R)
        y_hi = m.sbuf("y_hi", [P, KF, BLOCK], F32R)
        y_lo = m.sbuf("y_lo", [P, KF, BLOCK], F32R)
        acc = m.sbuf("acc", [P, KD, BLOCK])
        w_raw = [m.sbuf(f"w_raw{s}", [P, KF, P]) for s in range(2)]
        w_hi = [m.sbuf(f"w_hi{s}", [P, KF, P], F32R) for s in range(2)]
        w_lo = [m.sbuf(f"w_lo{s}", [P, KF, P], F32R) for s in range(2)]
        gate = m.sbuf("gate", [P, H + BLOCK])
        gate_s = m.sbuf("gate_s", [P, H + DEC])
        c1 = [m.sbuf(f"c1{j}", [P, SUB]) for j in range(SUBS)]
        c2 = [m.sbuf(f"c2{j}", [P, SUB]) for j in range(SUBS)]
        silu = [m.sbuf(f"silu{j}", [P, SUB]) for j in range(SUBS)]
        y = [m.sbuf(f"y{j}", [P, SUB]) for j in range(SUBS)]
        conv_sb = m.sbuf("conv", [P, F_TILES, 4])
        state_sb = m.sbuf("state", [P, F_TILES, H])
        carry = m.sbuf("carry", [P, F_TILES, H])
        tail = m.sbuf("tail", [P, F_TILES, H])
        z = [[m.psum(f"z{s}{i}", [P, 512]) for i in range(2)] for s in range(2)]

        const_ld, acc_ld, y_st = m.sem("const_ld"), m.sem("acc_ld"), m.sem("y_st")
        h_ld, w_ld = ([m.sem(f"{n}{i}") for i in range(2)] for n in ("h_ld", "w_ld"))
        w_hi_ok, w_lo_ok = ([m.sem(f"{n}{s}") for s in range(2)] for n in ("w_hi_ok", "w_lo_ok"))
        z_ok = [[m.sem(f"z_ok{s}{i}") for i in range(2)] for s in range(2)]
        z_free = [[m.sem(f"z_free{s}{i}") for i in range(2)] for s in range(2)]
        h0_ld = [m.sem(f"h0_ld{k}") for k in range(KD)]
        h_hi_ok, h_lo_ok, zero_ok = m.sem("h_hi_ok"), m.sem("h_lo_ok"), m.sem("zero_ok")
        p_lo_ok = m.sem("p_lo_ok")
        c1_ok, c2_ok, conv_ok, silu_ok, y_hi_ok, y_lo_ok = (
            [m.sem(f"{n}{i}") for i in range(2)] for n in ("c1_ok", "c2_ok", "conv_ok", "silu_ok", "y_hi_ok", "y_lo_ok"))
        halo_ok, carry_ok, s_gate_ok, s1_ok, s2_ok, tail_ok, gate_st = (
            m.sem(n) for n in ("halo_ok", "carry_ok", "s_gate_ok", "s1_ok", "s2_ok", "tail_ok", "gate_st"))

        def loop(eng, n, count, body):
            if n == 0:
                body(0)
            with eng.Fori(1 if n == 0 else 0, count) as i:
                body(i)

        block = ctx.enter_context(nc.Block())

        @block.sync
        def _(sp):
            def load_pair(g, src, k):
                for s in range(2):
                    sp.wait_ge(w_lo_ok[s], g)
                    sp.dma_start(w_raw[s][:, 0:k, :], src(s)).then_inc(w_ld[s], 16)

            def at(w, i):
                return lambda s: w[ds(i, 1), s].rearrange("a p k n -> p (a k) n")

            for k in range(KD):
                sp.dma_start(acc[:, k, :], h2T[k, :, 0:BLOCK]).then_inc(h0_ld[k], 16)
                if k == 0:
                    sp.dma_start(w_raw[0][:, 0:KD, :], w_gu[0, 0]).then_inc(w_ld[0], 16)
            sp.dma_start(w_raw[1][:, 0:KD, :], w_gu[0, 1]).then_inc(w_ld[1], 16)
            sp.dma_start(conv_sb[:], conv).then_inc(const_ld, 16)
            sp.dma_start(state_sb[:], state).then_inc(const_ld, 16)
            for b in range(N_BLOCKS):
                for part in range(PARTS):
                    g0 = (b * PARTS + part) * PAIRS
                    with sp.Fori(1 if g0 == 0 else 0, KF) as i:
                        load_pair(g0 + i, at(w_gu, part * KF + i), KD)
                    load_pair(g0 + KF, at(w_dn, part * DOWN), KF)
                    with sp.Fori(1, DOWN) as i:
                        load_pair(g0 + KF + i, at(w_dn, part * DOWN + i), KF)

        @block.gpsimd
        def _(pool):
            def load_h(b, k):
                if b > 1 or k > 1:
                    pool.wait_ge(p_lo_ok, KD * (b - 1) + k - 1)
                pool.dma_start(h_raw[k % 2][:], h2T[k, :, b * BLOCK:(b + 1) * BLOCK]).then_inc(h_ld[k % 2], 16)

            def split_h(b):
                for k in range(KD):
                    n = KD * (b - 1) + k
                    pool.wait_ge(h_hi_ok, n + KD + 1)
                    nc.gpsimd.tensor_tensor(h_lo[:, k, :], h_raw[k % 2][:], h_hi[:, k, :].bitcast(F32), ALU.subtract)\
                        .then_inc(p_lo_ok, 1)
                    if k + 2 < KD:
                        load_h(b, k + 2)

            def load_acc(b):
                if b:
                    pool.wait_ge(y_st, 16 * KD * b)
                else:
                    pool.wait_ge(h_lo_ok, KD)
                pool.dma_start(acc[:], x1T[:, :, b * BLOCK:(b + 1) * BLOCK].rearrange("k p n -> p k n"))\
                    .then_inc(acc_ld, 16)

            load_acc(0)
            for b in range(N_BLOCKS):
                if b < LAST:
                    load_h(b + 1, 0)
                    load_h(b + 1, 1)
                    split_h(b + 1)
                g1 = (b * PARTS + PARTS - 1) * PAIRS + KF
                for d in range(KD):
                    for j in range(SUBS):
                        pool.wait_ge(z_free[d % 2][j], g1 + d // 2 + 1)
                    pool.dma_start(yT[d, :, b * BLOCK:(b + 1) * BLOCK], acc[:, d, :]).then_inc(y_st, 16)
                if b < LAST:
                    load_acc(b + 1)
            pool.wait_ge(carry_ok, N_BLOCKS * F_TILES)
            pool.wait_ge(tail_ok, F_TILES)
            pool.dma_start(gate_sample, carry[:]).then_inc(gate_st, 16)
            pool.dma_start(gate_prompt, tail[:]).then_inc(gate_st, 16)
            pool.wait_ge(gate_st, 32)
            pool.wait_ge(y_st, 16 * KD * N_BLOCKS)

        @block.tensor
        def _(pe):
            def pair(g, hi, lo, n_k, ready=None):
                for s in range(2):
                    pe.wait_ge(w_lo_ok[s], g + 1)
                    for j in range(SUBS):
                        pe.wait_ge(z_free[s][j], g)
                        cols = slice(j * SUB, (j + 1) * SUB)
                        dense(nc, z[s][j][:, 0:SUB], (lambda k: w_hi[s][:, k, :], lambda k: w_lo[s][:, k, :]),
                              (lambda k: hi[:, k, cols], lambda k: lo[:, k, cols]), n_k,
                              ready and (lambda k: ready(s, j, k))).then_inc(z_ok[s][j], 1)

            for b in range(N_BLOCKS):
                if b:
                    pe.wait_ge(p_lo_ok, KD * b)
                for part in range(PARTS):
                    n = b * PARTS + part
                    g0 = n * PAIRS
                    if n == 0:
                        pair(0, h_hi, h_lo, KD, lambda s, j, k: s == j == 0 and pe.wait_ge(h_lo_ok, k + 1))
                    with pe.Fori(1 if n == 0 else 0, KF) as i:
                        pair(g0 + i, h_hi, h_lo, KD)
                    for j in range(SUBS):
                        pe.wait_ge(y_lo_ok[j], KF * (n + 1) - 1)
                    pair(g0 + KF, y_hi, y_lo, KF,
                         lambda s, j, k: k == KF - 1 and s == 0 and pe.wait_ge(y_lo_ok[j], KF * (n + 1)))
                    with pe.Fori(1, DOWN) as i:
                        pair(g0 + KF + i, y_hi, y_lo, KF)

        @block.scalar
        def _(act):
            def split_hi(s, g, n_k):
                act.wait_ge(w_ld[s], 16 * (g + 1))
                act.wait_ge(z_ok[s][1], g)
                nc.scalar.activation(w_hi[s][:, 0:n_k, :], w_raw[s][:, 0:n_k, :], ACT.Copy).then_inc(w_hi_ok[s], 1)

            def split_h(b, k):
                if b == 0:
                    act.wait_ge(h0_ld[k], 16)
                    src = acc[:, k, :]
                else:
                    act.wait_ge(h_ld[k % 2], 16 * ((KD * (b - 1) + k) // 2 + 1))
                    src = h_raw[k % 2][:]
                nc.scalar.activation(h_hi[:, k, :], src, ACT.Copy).then_inc(h_hi_ok, 1)

            def gate_up(b, g, c, n_k):
                for j in range(SUBS):
                    act.wait_ge(z_ok[0][j], g + 1)
                    if j == 0:
                        act.wait_ge(carry_ok, c)
                    nc.scalar.activation(gate[:, H + j * SUB:H + (j + 1) * SUB], z[0][j][:, 0:SUB], ACT.Copy)\
                        .then_inc(z_free[0][j], 1)
                split_hi(0, g + 1, n_k)
                for j in range(SUBS):
                    act.wait_ge(conv_ok[j], c + 1)
                    nc.scalar.activation(silu[j][:], c1[j][:], ACT.Silu).then_inc(silu_ok[j], 1)
                split_hi(1, g + 1, n_k)

            split_h(0, 0)
            split_hi(0, 0, KD)
            for k in range(1, KD):
                split_h(0, k)
            split_hi(1, 0, KD)
            for b in range(N_BLOCKS):
                for part in range(PARTS):
                    n = b * PARTS + part
                    g0, c0 = n * PAIRS, n * KF
                    loop(nc.scalar, n, KF - 1, lambda i: gate_up(b, g0 + i, c0 + i, KD))
                    gate_up(b, g0 + KF - 1, c0 + KF - 1, KF)
                    if part == PARTS - 1 and b < LAST:
                        act.wait_ge(z_ok[1][1], g0 + KF)
                        for i in range(DOWN):
                            split_h(b + 1, 2 * i)
                            split_h(b + 1, 2 * i + 1)
                            if i < DOWN - 1:
                                split_hi(0, g0 + KF + i + 1, KF)
                                split_hi(1, g0 + KF + i + 1, KF)
                    else:
                        with nc.scalar.Fori(0, DOWN - 1) as i:
                            split_hi(0, g0 + KF + i + 1, KF)
                            split_hi(1, g0 + KF + i + 1, KF)
                    if n + 1 < N_BLOCKS * PARTS:
                        split_hi(0, g0 + PAIRS, KD)
                        split_hi(1, g0 + PAIRS, KD)

        @block.vector
        def _(dve):
            def split_lo(s, g, n_k):
                dve.wait_ge(w_hi_ok[s], g + 1)
                nc.vector.tensor_tensor(w_lo[s][:, 0:n_k, :], w_raw[s][:, 0:n_k, :],
                                        w_hi[s][:, 0:n_k, :].bitcast(F32), ALU.subtract).then_inc(w_lo_ok[s], 1)

            def split_h(k):
                dve.wait_ge(h_hi_ok, k + 1)
                nc.vector.tensor_tensor(h_lo[:, k, :], acc[:, k, :], h_hi[:, k, :].bitcast(F32), ALU.subtract)\
                    .then_inc(h_lo_ok, 1)

            def of(ap, i):
                return ap[:, ds(i, 1), :].rearrange("p a n -> p (a n)")

            def convolve(dst, tmp, src, taps, n, waits, done):
                nc.vector.tensor_scalar(dst, src[:, H:H + n], taps[:, 2:3], taps[:, 3:4], ALU.mult, ALU.add)\
                    .then_inc(done[0], 1)
                dve.wait_ge(done[0], waits + 1)
                nc.vector.scalar_tensor_tensor(tmp, src[:, 1:1 + n], taps[:, 1:2], dst, ALU.mult, ALU.add)\
                    .then_inc(done[1], 1)
                dve.wait_ge(done[1], waits + 1)
                nc.vector.scalar_tensor_tensor(dst, src[:, 0:n], taps[:, 0:1], tmp, ALU.mult, ALU.add)\
                    .then_inc(done[2], 1)

            def gate_up(b, g, f, c, jf, n_k):
                taps = of(conv_sb, f)
                dve.wait_ge(carry_ok, c)
                nc.vector.tensor_scalar(gate[:, 0:H], of(carry, f), 1.0, None, ALU.mult).then_inc(halo_ok, 1)
                dve.wait_ge(halo_ok, c + 1)
                for j in range(SUBS):
                    dve.wait_ge(z_free[0][j], g + 1)
                    dve.wait_ge(silu_ok[j], c)
                    n = CUT - j * SUB if b == LAST and j else SUB
                    convolve(c1[j][:, 0:n], c2[j][:, 0:n], gate[:, j * SUB:H + (j + 1) * SUB], taps, n, c,
                             (c1_ok[j], c2_ok[j], conv_ok[j] if n == SUB else s_gate_ok))
                if b == LAST:
                    cs = c - LAST * F_TILES
                    nc.vector.tensor_scalar(gate_s[:, 0:H], of(state_sb, f), 1.0, None, ALU.mult).then_inc(s_gate_ok, 1)
                    nc.vector.tensor_scalar(gate_s[:, H:], gate[:, H + CUT:], 1.0, None, ALU.mult).then_inc(s_gate_ok, 1)
                    dve.wait_ge(s_gate_ok, 3 * cs + 3)
                    n = CUT - SUB
                    convolve(c1[1][:, n:], c2[1][:, n:], gate_s, taps, DEC, cs, (s1_ok, s2_ok, conv_ok[1]))
                    nc.vector.tensor_scalar(of(tail, f), gate[:, CUT:H + CUT], 1.0, None, ALU.mult).then_inc(tail_ok, 1)
                split_lo(0, g + 1, n_k)
                nc.vector.tensor_scalar(of(carry, f), gate[:, BLOCK:H + BLOCK], 1.0, None, ALU.mult).then_inc(carry_ok, 1)
                for j in range(SUBS):
                    cols = slice(j * SUB, (j + 1) * SUB)
                    dve.wait_ge(silu_ok[j], c + 1)
                    dve.wait_ge(z_ok[1][j], g + 1)
                    dve.wait_ge(y_lo_ok[j], c)
                    nc.vector.tensor_tensor(y[j][:], silu[j][:], z[1][j][:, 0:SUB], ALU.mult).then_inc(z_free[1][j], 1)
                    dve.wait_ge(z_free[1][j], g + 1)
                    hi, lo = (ap[:, ds(jf, 1), cols].rearrange("p a n -> p (a n)") for ap in (y_hi, y_lo))
                    nc.vector.tensor_scalar(hi, y[j][:], 1.0, None, ALU.mult).then_inc(y_hi_ok[j], 1)
                    dve.wait_ge(y_hi_ok[j], c + 1)
                    nc.vector.tensor_tensor(lo, y[j][:], hi.bitcast(F32), ALU.subtract).then_inc(y_lo_ok[j], 1)
                split_lo(1, g + 1, n_k)

            def down(g, i, n_k):
                for s in range(2):
                    for j in range(SUBS):
                        dve.wait_ge(z_ok[s][j], g + 1)
                        part = acc[:, ds(2 * i + s, 1), j * SUB:(j + 1) * SUB].rearrange("p a n -> p (a n)")
                        nc.vector.tensor_tensor(part, part, z[s][j][:, 0:SUB], ALU.add).then_inc(z_free[s][j], 1)
                    if n_k:
                        split_lo(s, g + 1, n_k)

            nc.vector.memset(carry[:], 0.0).then_inc(zero_ok, 1)
            dve.wait_ge(zero_ok, 1)
            split_h(0)
            split_lo(0, 0, KD)
            for k in range(1, KD):
                split_h(k)
            split_lo(1, 0, KD)
            dve.wait_ge(const_ld, 32)
            for b in range(N_BLOCKS):
                for part in range(PARTS):
                    n = b * PARTS + part
                    g0, c0, f0 = n * PAIRS, n * KF, part * KF
                    loop(nc.vector, n, KF - 1, lambda i: gate_up(b, g0 + i, f0 + i, c0 + i, i, KD))
                    gate_up(b, g0 + KF - 1, f0 + KF - 1, c0 + KF - 1, KF - 1, KF)
                    if part == 0:
                        dve.wait_ge(acc_ld, 16 * (b + 1))
                    with nc.vector.Fori(0, DOWN - 1) as i:
                        down(g0 + KF + i, i, KF)
                    down(g0 + PAIRS - 1, DOWN - 1, KD if n + 1 < N_BLOCKS * PARTS else 0)


def encoder_step(nc, a):
    scratch = {name: nc.dram_tensor(f"{name}_scratch", shape, F32, kind="Internal").ap()
               for name, shape in (("q_a", (4, P, TOKENS)), ("rel_rows", (P, HEADS, 3 * P)), ("oT", (KD, P, TOKENS)),
                                   ("x1T", (KD, P, TOKENS)), ("h2T", (KD, P, TOKENS)))}
    project(nc, a["xT"], a["w_qk"], a["w_rv"], a["gains_in"], a["rope_cos"], a["rope_sin"],
            a["head_ones"], a["all_ones"], a["ident"], a["rel"],
            scratch["q_a"], a["k_a"], a["qk_b"], a["v_all"], scratch["rel_rows"])
    attend(nc, scratch["q_a"], a["k_a"], a["qk_b"], a["v_all"], a["ka_cache"], a["kb_cache"], a["va_cache"],
           a["vb_cache"], scratch["rel_rows"], a["sinks"], a["ident"], scratch["oT"])
    combine(nc, scratch["oT"], a["xT"], a["w_o"], a["gains_ffn"], a["all_ones"], scratch["x1T"], scratch["h2T"])
    ffn(nc, scratch["h2T"], scratch["x1T"], a["w_gu"], a["w_dn"], a["conv"], a["state"],
        a["yT"], a["gate_prompt"], a["gate_sample"])


def kernel(**inputs):
    import numpy as np
    import concourse.bacc as bacc
    from concourse.bass_utils import run_bass_kernel_spmd

    x = {name: np.asarray(value) for name, value in inputs.items()}

    def tiles(w):
        k, n = w.shape
        return w.reshape(k // P, P, n // P, P).transpose(2, 1, 0, 3)

    def head_pairs(w):
        return w.reshape(w.shape[0], 2, HEADS // 2, HEAD).transpose(0, 2, 1, 3).reshape(w.shape[0], -1)

    width = HEADS * HEAD
    qa, ka, va, qb, kb, vb = np.split(x["w_in"][0], [width, 2 * width, 3 * width, 4 * width, 4 * width + P], axis=1)
    cols = lambda g: g[0].reshape(-1, P).T
    by_head = lambda g: np.tile(g[0], 2)[:, None]
    gate, up = np.split(x["w_gate_up"][0], 2, axis=1)
    rel = x["rel_bias_a"][0][:, ::-1]

    pos = np.concatenate([np.arange(SEQ), PAST + np.arange(DEC)]).astype(np.float32)
    inv = np.power(10000.0, -np.arange(HEAD // 2) / (HEAD // 2)).astype(np.float32)
    angle = (pos[None, :] * inv[:, None]).astype(np.float32)
    cos, sin = np.cos(angle.astype(np.float64)), np.sin(angle.astype(np.float64))
    head_ones = np.kron(np.eye(2), np.full((HEAD, HEAD), 1 / HEAD))

    arrays = dict(
        xT=np.concatenate([x["x_prompt"][0], x["x_sample"][0]]).T.reshape(KD, P, TOKENS),
        w_qk=np.stack([tiles(qa), tiles(ka)], 1),
        w_rv=np.stack([tiles(np.concatenate([head_pairs(qb), kb], 1)), tiles(np.concatenate([va, vb], 1))], 1),
        gains_in=np.concatenate([cols(x["norm_attn"]), by_head(x["q_norm_a"]), by_head(x["k_norm_a"]),
                                 by_head(x["q_norm_b"]), by_head(x["k_norm_b"])], 1),
        rope_cos=np.tile(cos, (4, 1)), rope_sin=np.tile(np.concatenate([sin, -sin]), (2, 1)),
        head_ones=head_ones, all_ones=np.full((P, P), 1 / D_MODEL), ident=np.eye(P),
        ka_cache=x["cache_a_k"].reshape(PAST, width).T.reshape(-1, P, PAST),
        kb_cache=x["cache_b_k"].reshape(PAST, P).T,
        va_cache=x["cache_a_v"].reshape(PAST, width), vb_cache=x["cache_b_v"].reshape(PAST, P),
        rel=np.concatenate([np.repeat(rel[:, :1], MAX_REL - 1, 1), rel], 1),
        sinks=x["sinks_b"].reshape(2, HEADS // 2).T.reshape(-1),
        w_o=tiles(x["w_out"][0]).reshape(KD // 2, 2, P, KD, P), gains_ffn=cols(x["norm_ffn"]),
        w_gu=np.stack([tiles(gate), tiles(up)], 1),
        w_dn=x["w_down"][0].reshape(2, KF // 2, P, KD // 2, 2, P).transpose(0, 3, 4, 2, 1, 5)
            .reshape(KD, 2, P, KF // 2, P),
        conv=np.concatenate([x["conv_w"][0], x["conv_b"]]).reshape(4, KF, P).transpose(2, 1, 0),
        state=x["state_conv"].reshape(2, KF, P).transpose(2, 1, 0))
    returned = dict(k_a=(4, P, TOKENS), qk_b=(5, P, TOKENS), v_all=(TOKENS, 5 * P), yT=(KD, P, TOKENS),
                    gate_prompt=(P, KF, 2), gate_sample=(P, KF, 2))

    nc = bacc.Bacc("TRN2", target_bir_lowering=False, num_devices=1)
    arrays = {name: np.ascontiguousarray(value, dtype=np.float32) for name, value in arrays.items()}
    drams = {name: nc.dram_tensor(name, value.shape, F32, kind="ExternalInput").ap() for name, value in arrays.items()}
    drams |= {name: nc.dram_tensor(name, shape, F32, kind="ExternalOutput").ap() for name, shape in returned.items()}
    encoder_step(nc, drams)
    got = run_bass_kernel_spmd(nc, [arrays], core_ids=[0]).results[0]

    y = got["yT"].reshape(D_MODEL, TOKENS).T
    k_a, k_b = got["k_a"].reshape(width, TOKENS).T, got["qk_b"][4].T
    v_a, v_b = got["v_all"][:, :width], got["v_all"][:, width:]
    last_a, last_b = slice(SEQ - 8 * CHUNK, SEQ), slice(SEQ - 2 * CHUNK, SEQ)
    heads = lambda t, rows: t[rows].reshape(1, 1, -1, t.shape[1] // HEAD, HEAD)
    conv_rows = lambda t: t.transpose(2, 1, 0).reshape(1, 1, 2, D_FF)
    sample = slice(SEQ, TOKENS)
    return tuple(np.ascontiguousarray(t) for t in (
        y[None, :SEQ], y[None, SEQ:],
        heads(k_a, last_a), heads(v_a, last_a), heads(k_b, last_b), heads(v_b, last_b),
        conv_rows(got["gate_prompt"]),
        heads(k_a, sample), heads(v_a, sample), heads(k_b, sample), heads(v_b, sample),
        conv_rows(got["gate_sample"])))
```
